# Optimizing a Trainium2 kernel written in Bass

```python
import jax, jax.numpy as jnp
from jax import lax
import numpy as np

D_MODEL = 1024
BATCH = 1
SEQ = 512
DEPTH = 2

MLA_HEADS = 8
QK_NOPE_DIM = 64
QK_ROPE_DIM = 32
V_HEAD_DIM = 64
Q_LORA_RANK = 384
KV_LORA_RANK = 256
ROPE_THETA = 10000.0
Q_BLOCK = 128
MLA_WIDTH = MLA_HEADS * V_HEAD_DIM
POOL_WINDOWS = (2, 4, 8, 16)
POOL_GROUP_DIM = 64
POOL_WIDTH = len(POOL_WINDOWS) * POOL_GROUP_DIM
SG_HEADS = 4
SG_HEAD_DIM = 64
SG_WIDTH = SG_HEADS * SG_HEAD_DIM
SG_CHUNK = 128
D_MIX = MLA_WIDTH + POOL_WIDTH + SG_WIDTH
IN_COLS = Q_LORA_RANK + KV_LORA_RANK + QK_ROPE_DIM + POOL_WIDTH + 2 * SG_WIDTH
D_FF = -(-(8 * D_MODEL) // (3 * 256)) * 256
EPS = 1e-6


def rmsnorm(x, g):
    xf = x.astype(jnp.float32)
    y = xf * lax.rsqrt(jnp.mean(xf * xf, axis=-1, keepdims=True) + EPS)
    return (y * g.astype(jnp.float32)).astype(x.dtype)

def rope_tables(positions):
    inv_freq = ROPE_THETA ** (-jnp.arange(0, QK_ROPE_DIM, 2, dtype=jnp.float32) / QK_ROPE_DIM)
    ang = positions.astype(jnp.float32)[..., None] * inv_freq
    return jnp.cos(ang), jnp.sin(ang)

def apply_rope(t, cos, sin):
    tf = t.astype(jnp.float32)
    half = QK_ROPE_DIM // 2
    t1, t2 = tf[..., :half], tf[..., half:]
    out = jnp.concatenate([t1 * cos - t2 * sin, t1 * sin + t2 * cos], axis=-1)
    return out.astype(t.dtype)

def mla_mixer(h_q, h_kv, k_rope_in, positions, q_norm_g, kv_norm_g, w_uq, w_ukv):
    B, S, _ = h_q.shape
    cq = rmsnorm(h_q, q_norm_g)
    q = jnp.einsum('bsr,rn->bsn', cq, w_uq).reshape(B, S, MLA_HEADS, QK_NOPE_DIM + QK_ROPE_DIM)
    q_nope, q_rope = q[..., :QK_NOPE_DIM], q[..., QK_NOPE_DIM:]
    ckv = rmsnorm(h_kv, kv_norm_g)
    kv = jnp.einsum('bsr,rn->bsn', ckv, w_ukv).reshape(B, S, MLA_HEADS, QK_NOPE_DIM + V_HEAD_DIM)
    k_nope, v = kv[..., :QK_NOPE_DIM], kv[..., QK_NOPE_DIM:]
    cos, sin = rope_tables(positions)
    q_rope = apply_rope(q_rope, cos[:, :, None, :], sin[:, :, None, :])
    k_rope = apply_rope(k_rope_in, cos, sin)
    scale = (QK_NOPE_DIM + QK_ROPE_DIM) ** -0.5
    nb = S // Q_BLOCK

    def blockify(t):
        return jnp.moveaxis(t.reshape(B, nb, Q_BLOCK, *t.shape[2:]), 1, 0)

    def attend(blk):
        qn, qr = blk
        s = (jnp.einsum('bqhd,bkhd->bhqk', qn, k_nope)
             + jnp.einsum('bqhr,bkr->bhqk', qr, k_rope))
        p = jax.nn.softmax(s.astype(jnp.float32) * scale, axis=-1).astype(v.dtype)
        return jnp.einsum('bhqk,bkhd->bqhd', p, v)

    o = lax.map(attend, (blockify(q_nope), blockify(q_rope)))
    return jnp.moveaxis(o, 0, 1).reshape(B, S, MLA_WIDTH)

def pool_mixer(h, w_pool, pool_scale):
    B, S, _ = h.shape
    hf = h.astype(jnp.float32)
    cs = jnp.concatenate([jnp.zeros((B, 1, POOL_WIDTH), jnp.float32), lax.cumsum(hf, axis=1)], axis=1)
    t = jnp.arange(S)
    outs = []
    for g, w in enumerate(POOL_WINDOWS):
        left = w // 2
        right = w - 1 - left
        lo = jnp.clip(t - left, 0, S)
        hi = jnp.clip(t + right + 1, 0, S)
        sl = slice(g * POOL_GROUP_DIM, (g + 1) * POOL_GROUP_DIM)
        csg = cs[:, :, sl]
        mean = (csg[:, hi] - csg[:, lo]) / (hi - lo).astype(jnp.float32)[None, :, None]
        d = (mean - hf[:, :, sl]).astype(h.dtype)
        outs.append(jnp.einsum('bsc,cd->bsd', d, w_pool[g]))
    return jnp.concatenate(outs, axis=-1) * pool_scale

def sg_mixer(h_uv, sg_norm_g, w_s, b_s):
    B, S, _ = h_uv.shape
    z = jax.nn.gelu(h_uv)
    u, v = z[..., :SG_WIDTH], z[..., SG_WIDTH:]
    v = rmsnorm(v.reshape(B, S, SG_HEADS, SG_HEAD_DIM), sg_norm_g.reshape(SG_HEADS, SG_HEAD_DIM))
    vc = v.reshape(B, S // SG_CHUNK, SG_CHUNK, SG_HEADS, SG_HEAD_DIM)
    mixed = jnp.einsum('gpq,bcqgd->bcpgd', w_s, vc) + b_s.T[None, None, :, :, None]
    return u * mixed.reshape(B, S, SG_WIDTH)

def first_inputs(seed: int = 0) -> dict:
    key = jax.random.key(seed)
    ks = jax.random.split(key, 20)
    f32 = jnp.float32

    def nrm(k, shape, fan_in):
        return jax.random.normal(k, shape, f32) * (fan_in ** -0.5)

    def gain(k, shape):
        return 1.0 + 0.05 * jax.random.normal(k, shape, f32)

    x = jax.random.normal(ks[0], (BATCH, SEQ, D_MODEL), f32)
    positions = jnp.broadcast_to(jnp.arange(SEQ, dtype=jnp.int32), (BATCH, SEQ))
    return {
        "x": x,
        "positions": positions,
        "mix_norm": gain(ks[1], (DEPTH, D_MODEL)),
        "w_in": nrm(ks[2], (DEPTH, D_MODEL, IN_COLS), D_MODEL),
        "q_norm": gain(ks[3], (DEPTH, Q_LORA_RANK)),
        "kv_norm": gain(ks[4], (DEPTH, KV_LORA_RANK)),
        "w_uq": nrm(ks[5], (DEPTH, Q_LORA_RANK, MLA_HEADS * (QK_NOPE_DIM + QK_ROPE_DIM)), Q_LORA_RANK),
        "w_ukv": nrm(ks[6], (DEPTH, KV_LORA_RANK, MLA_HEADS * (QK_NOPE_DIM + V_HEAD_DIM)), KV_LORA_RANK),
        "w_pool": nrm(ks[7], (DEPTH, len(POOL_WINDOWS), POOL_GROUP_DIM, POOL_GROUP_DIM), POOL_GROUP_DIM),
        "pool_scale": gain(ks[8], (DEPTH, POOL_WIDTH)),
        "sg_norm": gain(ks[9], (DEPTH, SG_WIDTH)),
        "w_s": nrm(ks[10], (DEPTH, SG_HEADS, SG_CHUNK, SG_CHUNK), SG_CHUNK),
        "b_s": 1.0 + 0.05 * jax.random.normal(ks[11], (DEPTH, SG_HEADS, SG_CHUNK), f32),
        "w_o": nrm(ks[12], (DEPTH, D_MIX, D_MODEL), D_MIX),
        "ffn_norm": gain(ks[13], (DEPTH, D_MODEL)),
        "w_gate": nrm(ks[14], (DEPTH, D_MODEL, D_FF), D_MODEL),
        "w_up": nrm(ks[15], (DEPTH, D_MODEL, D_FF), D_MODEL),
        "w_down": nrm(ks[16], (DEPTH, D_FF, D_MODEL), D_FF),
        "final_norm": gain(ks[17], (D_MODEL,)),
    }

def first_block(x, positions, mix_norm, w_in, q_norm, kv_norm, w_uq, w_ukv, w_pool, pool_scale,
              sg_norm, w_s, b_s, w_o, ffn_norm, w_gate, w_up, w_down, final_norm):
    o1 = Q_LORA_RANK
    o2 = o1 + KV_LORA_RANK
    o3 = o2 + QK_ROPE_DIM
    o4 = o3 + POOL_WIDTH
    for l in range(DEPTH):
        h = rmsnorm(x, mix_norm[l])
        p = jnp.einsum('bsd,dn->bsn', h, w_in[l])
        a = mla_mixer(p[..., :o1], p[..., o1:o2], p[..., o2:o3], positions,
                      q_norm[l], kv_norm[l], w_uq[l], w_ukv[l])
        b = pool_mixer(p[..., o3:o4], w_pool[l], pool_scale[l])
        c = sg_mixer(p[..., o4:], sg_norm[l], w_s[l], b_s[l])
        mix = jnp.concatenate([a, b, c], axis=-1)
        x = x + jnp.einsum('bsn,nd->bsd', mix, w_o[l])
        h = rmsnorm(x, ffn_norm[l])
        g = jnp.einsum('bsd,df->bsf', h, w_gate[l])
        u = jnp.einsum('bsd,df->bsf', h, w_up[l])
        x = x + jnp.einsum('bsf,fd->bsd', jax.nn.silu(g) * u, w_down[l])
    return rmsnorm(x, final_norm)


DEPTH_2 = 1

RET_HEADS = 4
RET_V_DIM = D_MODEL // 2 // RET_HEADS
RET_QK_DIM = RET_V_DIM // 2
RET_CHUNK = 128
ATT_HEAD_DIM = 64
ATT_HEADS = D_MODEL // 2 // ATT_HEAD_DIM
DILATED_CONFIGS = ((128, 1), (512, 4), (2048, 16))
N_EXPERTS = 16
EC_CAPACITY_FACTOR = 2
D_FF_EXPERT = 2048

RET_QK_W = RET_HEADS * RET_QK_DIM
RET_V_W = RET_HEADS * RET_V_DIM
ATT_W = ATT_HEADS * ATT_HEAD_DIM
MIX_WIDTH = RET_V_W + ATT_W
IN_PROJ_WIDTH = 2 * RET_QK_W + 2 * RET_V_W + 3 * ATT_W
RMS_EPS = 1e-6
GN_EPS = 1e-5
MASK_VALUE = -1e30


def rmsnorm_2(x, g):
    xf = x.astype(jnp.float32)
    y = xf * lax.rsqrt(jnp.mean(xf * xf, axis=-1, keepdims=True) + RMS_EPS)
    return (y * g.astype(jnp.float32)).astype(x.dtype)

def alibi_slopes(n):
    return 2.0 ** (-8.0 * (jnp.arange(n, dtype=jnp.float32) + 1.0) / n)

def retention_scan(q, k, v, log_gamma, inclusive):
    B, H, S, dk = q.shape
    dv = v.shape[-1]
    C = RET_CHUNK
    n = S // C
    qc = q.reshape(B, H, n, C, dk)
    kc = k.reshape(B, H, n, C, dk)
    vc = v.reshape(B, H, n, C, dv)
    pos = jnp.arange(C, dtype=jnp.float32)
    rel = pos[:, None] - pos[None, :]
    mask = (rel >= 0) if inclusive else (rel > 0)
    lg = log_gamma[:, None, None]
    intra_decay = jnp.where(mask[None], jnp.exp(lg * jnp.where(mask, rel, 0.0)[None]), 0.0)
    scores = jnp.einsum('bhnid,bhnjd->bhnij', qc, kc) * intra_decay[None, :, None]
    o = jnp.einsum('bhnij,bhnjv->bhniv', scores, vc)
    k_tail = kc * jnp.exp(log_gamma[:, None] * (C - 1.0 - pos))[None, :, None, :, None]
    kv = jnp.einsum('bhnjd,bhnjv->nbhdv', k_tail, vc)
    chunk_decay = jnp.exp(log_gamma * C)[None, :, None, None]

    def step(state, kv_n):
        return chunk_decay * state + kv_n, state

    _, prev = lax.scan(step, jnp.zeros((B, H, dk, dv), jnp.float32), kv)
    q_head = qc * jnp.exp(log_gamma[:, None] * (pos + 1.0))[None, :, None, :, None]
    o = o + jnp.einsum('bhnid,nbhdv->bhniv', q_head, prev)
    return o.reshape(B, H, S, dv)

def bidirectional_retention(q, k, v, logit_fwd, logit_bwd):
    qf, kf, vf = q.astype(jnp.float32), k.astype(jnp.float32), v.astype(jnp.float32)
    lg_f = jax.nn.log_sigmoid(logit_fwd.astype(jnp.float32))
    lg_b = jax.nn.log_sigmoid(logit_bwd.astype(jnp.float32))
    y_f = retention_scan(qf, kf, vf, lg_f, True)
    y_b = jnp.flip(retention_scan(jnp.flip(qf, 2), jnp.flip(kf, 2), jnp.flip(vf, 2), lg_b, False), 2)
    y = y_f + y_b
    mu = jnp.mean(y, axis=-1, keepdims=True)
    var = jnp.mean(jnp.square(y - mu), axis=-1, keepdims=True)
    return (y - mu) * lax.rsqrt(var + GN_EPS)

def banded_attention(q, k, v, half, slopes):
    N, H, L, dh = q.shape
    W = half
    nb = -(-L // W)
    pad = nb * W - L
    qb = jnp.pad(q, ((0, 0), (0, 0), (0, pad), (0, 0))).reshape(N, H, nb, W, dh)

    def windows(t):
        tb = jnp.pad(t, ((0, 0), (0, 0), (W, pad + W), (0, 0))).reshape(N, H, nb + 2, W, dh)
        return jnp.concatenate([tb[:, :, :-2], tb[:, :, 1:-1], tb[:, :, 2:]], axis=3)

    kw, vw = windows(k), windows(v)
    qpos = jnp.arange(nb * W).reshape(nb, W)
    kpos = jnp.arange(nb)[:, None] * W - W + jnp.arange(3 * W)[None, :]
    dist = jnp.abs(kpos[:, None, :] - qpos[:, :, None])
    valid = (dist <= W) & (kpos[:, None, :] >= 0) & (kpos[:, None, :] < L)
    s = jnp.einsum('nhbqd,nhbkd->nhbqk', qb, kw).astype(jnp.float32) * (dh ** -0.5)
    s = s - slopes[None, :, None, None, None] * dist.astype(jnp.float32)[None, None]
    s = jnp.where(valid[None, None], s, MASK_VALUE)
    lse = jax.nn.logsumexp(s, axis=-1)
    p = jnp.exp(s - lse[..., None])
    o = jnp.einsum('nhbqk,nhbkd->nhbqd', p, vw.astype(jnp.float32))
    return o.reshape(N, H, nb * W, dh)[:, :, :L], lse.reshape(N, H, nb * W)[:, :, :L]

def dilated_attention(q, k, v, window, dilation, slopes):
    B, H, S, dh = q.shape
    L = S // dilation

    def to_sub(t):
        return t.reshape(B, H, L, dilation, dh).transpose(0, 3, 1, 2, 4).reshape(B * dilation, H, L, dh)

    o, lse = banded_attention(to_sub(q), to_sub(k), to_sub(v), window // (2 * dilation), slopes * dilation)
    o = o.reshape(B, dilation, H, L, dh).transpose(0, 2, 3, 1, 4).reshape(B, H, S, dh)
    lse = lse.reshape(B, dilation, H, L).transpose(0, 2, 3, 1).reshape(B, H, S)
    return o, lse

def expert_choice_moe(h, w_router, w_gate, w_up, w_down):
    B, S, D = h.shape
    E = w_router.shape[-1]
    cap = EC_CAPACITY_FACTOR * S // E
    affinity = jax.nn.softmax((h @ w_router).astype(jnp.float32), axis=-1)
    gates, idx = lax.top_k(jnp.swapaxes(affinity, 1, 2), cap)
    flat_idx = idx.reshape(B, E * cap)
    b_idx = jnp.arange(B)[:, None]
    xe = h[b_idx, flat_idx].reshape(B, E, cap, D)
    a = jnp.einsum('becd,edf->becf', xe, w_gate)
    u = jnp.einsum('becd,edf->becf', xe, w_up)
    ye = jnp.einsum('becf,efd->becd', jax.nn.silu(a) * u, w_down)
    ye = ye * gates[..., None].astype(ye.dtype)
    out = jnp.zeros_like(h).at[b_idx, flat_idx].add(ye.reshape(B, E * cap, D).astype(h.dtype))
    return out

def second_inputs(seed: int = 0) -> dict:
    key = jax.random.key(seed)
    ks = jax.random.split(key, 20)
    f32 = jnp.float32
    D, F, E = D_MODEL, D_FF_EXPERT, N_EXPERTS
    nrm = lambda k, shape, s: jax.random.normal(k, shape, f32) * s
    base_logit = jnp.log(2.0 ** (5.0 + jnp.arange(RET_HEADS, dtype=f32)) - 1.0)
    return {
        "x": nrm(ks[0], (BATCH, SEQ, D), 1.0),
        "c": nrm(ks[1], (BATCH, D), 1.0),
        "w_ada": nrm(ks[2], (DEPTH_2, D, 6 * D), 0.5 * D ** -0.5),
        "b_ada": nrm(ks[3], (DEPTH_2, 6 * D), 0.01),
        "g_pre_mix": 1.0 + nrm(ks[4], (DEPTH_2, D), 0.01),
        "g_post_mix": 1.0 + nrm(ks[5], (DEPTH_2, D), 0.01),
        "g_pre_ffn": 1.0 + nrm(ks[6], (DEPTH_2, D), 0.01),
        "g_post_ffn": 1.0 + nrm(ks[7], (DEPTH_2, D), 0.01),
        "w_in": nrm(ks[8], (DEPTH_2, D, IN_PROJ_WIDTH), D ** -0.5),
        "ret_decay_fwd": base_logit[None] + nrm(ks[9], (DEPTH_2, RET_HEADS), 0.1),
        "ret_decay_bwd": base_logit[None] + nrm(ks[10], (DEPTH_2, RET_HEADS), 0.1),
        "w_out": nrm(ks[11], (DEPTH_2, MIX_WIDTH, D), MIX_WIDTH ** -0.5),
        "w_router": nrm(ks[12], (DEPTH_2, D, E), D ** -0.5),
        "w_gate_e": nrm(ks[13], (DEPTH_2, E, D, F), D ** -0.5),
        "w_up_e": nrm(ks[14], (DEPTH_2, E, D, F), D ** -0.5),
        "w_down_e": nrm(ks[15], (DEPTH_2, E, F, D), F ** -0.5),
    }

def second_block(x, c, w_ada, b_ada, g_pre_mix, g_post_mix, g_pre_ffn, g_post_ffn, w_in,
              ret_decay_fwd, ret_decay_bwd, w_out, w_router, w_gate_e, w_up_e, w_down_e):
    B, S, D = x.shape
    slopes = alibi_slopes(ATT_HEADS)
    split_at = np.cumsum([RET_QK_W, RET_QK_W, RET_V_W, RET_V_W, ATT_W, ATT_W]).tolist()

    def heads(t, n_heads):
        return t.reshape(B, S, n_heads, -1).transpose(0, 2, 1, 3)

    for l in range(DEPTH_2):
        mod = jax.nn.silu(c) @ w_ada[l] + b_ada[l]
        shift_m, scale_m, gate_m, shift_f, scale_f, gate_f = [m[:, None, :] for m in jnp.split(mod, 6, axis=-1)]

        h = rmsnorm_2(x, g_pre_mix[l]) * (1.0 + scale_m) + shift_m
        proj = h @ w_in[l]
        rq, rk, rv, rg, aq, ak, av = jnp.split(proj, split_at, axis=-1)

        y_ret = bidirectional_retention(heads(rq, RET_HEADS), heads(rk, RET_HEADS) * (RET_QK_DIM ** -0.5),
                                        heads(rv, RET_HEADS), ret_decay_fwd[l], ret_decay_bwd[l])
        y_ret = y_ret.transpose(0, 2, 1, 3).reshape(B, S, RET_V_W).astype(x.dtype)
        y_ret = jax.nn.silu(rg) * y_ret

        qh, kh, vh = heads(aq, ATT_HEADS), heads(ak, ATT_HEADS), heads(av, ATT_HEADS)
        results = [dilated_attention(qh, kh, vh, w, d, slopes) for (w, d) in DILATED_CONFIGS]
        outs = jnp.stack([r[0] for r in results])
        lses = jnp.stack([r[1] for r in results])
        mix_w = jax.nn.softmax(lses, axis=0)
        y_att = jnp.sum(mix_w[..., None] * outs, axis=0)
        y_att = y_att.transpose(0, 2, 1, 3).reshape(B, S, ATT_W).astype(x.dtype)

        mixed = jnp.concatenate([y_ret, y_att], axis=-1) @ w_out[l]
        x = x + gate_m * rmsnorm_2(mixed, g_post_mix[l])

        h = rmsnorm_2(x, g_pre_ffn[l]) * (1.0 + scale_f) + shift_f
        moe = expert_choice_moe(h, w_router[l], w_gate_e[l], w_up_e[l], w_down_e[l])
        x = x + gate_f * rmsnorm_2(moe, g_post_ffn[l])
    return x


def setup_inputs(seed=0):
    out = dict(first_inputs(seed))
    for name, value in second_inputs(seed + 1).items():
        if name != "x":
            out[name + "_2"] = value
    return out


def reference(
    x, positions, mix_norm, w_in, q_norm, kv_norm, w_uq, w_ukv, w_pool, pool_scale, sg_norm,
    w_s, b_s, w_o, ffn_norm, w_gate, w_up, w_down, final_norm, c_2, w_ada_2, b_ada_2,
    g_pre_mix_2, g_post_mix_2, g_pre_ffn_2, g_post_ffn_2, w_in_2, ret_decay_fwd_2,
    ret_decay_bwd_2, w_out_2, w_router_2, w_gate_e_2, w_up_e_2, w_down_e_2,
):
    x = first_block(
        x, positions, mix_norm, w_in, q_norm, kv_norm, w_uq, w_ukv, w_pool, pool_scale, sg_norm,
        w_s, b_s, w_o, ffn_norm, w_gate, w_up, w_down, final_norm,
    )
    return second_block(
        x, c_2, w_ada_2, b_ada_2, g_pre_mix_2, g_post_mix_2, g_pre_ffn_2, g_post_ffn_2, w_in_2,
        ret_decay_fwd_2, ret_decay_bwd_2, w_out_2, w_router_2, w_gate_e_2, w_up_e_2, w_down_e_2,
    )


_drawn_inputs = setup_inputs


def setup_inputs(seed=0):
    import zlib

    import numpy as np

    out = dict(_drawn_inputs(seed))
    spreads = {}
    factors = {'q_norm': 2.809,
     'kv_norm': 2.76,
     'g_pre_mix_2': 4.912,
     'g_post_mix_2': 5.14,
     'g_post_ffn_2': 8.0}
    for name, (base, spread) in spreads.items():
        noise = np.random.default_rng([zlib.crc32(name.encode()), seed]).standard_normal(out[name].shape)
        drawn = base * np.exp(spread * noise) if base else spread * noise
        out[name] = __import__('jax').numpy.asarray(drawn.astype(out[name].dtype))
    for name, factor in factors.items():
        out[name] = (out[name] * factor).astype(out[name].dtype)
    return out
```

```python
from contextlib import ExitStack

import concourse.bass as bass
from concourse import mybir

F32 = mybir.dt.float32
F32R = mybir.dt.float32r
I32 = mybir.dt.int32
ALU = mybir.AluOpType
ACT = mybir.ActivationFunctionType
AX = mybir.AxisListType

P = 128
S = 512
TC = S // P
D = 1024
DK = D // P
BANK = 512
EPS = 1e-6
GN_EPS = 1e-5

LAYERS = 2
HEADS, NOPE, ROPE, VDIM = 8, 64, 32, 64
QK = NOPE + ROPE
Q_LORA, KV_LORA = 384, 256
QC, KVC = Q_LORA // P, KV_LORA // P
ATT_SCALE = float(QK) ** -0.5
POOL_WINDOWS = (2, 4, 8, 16)
PAD = max(POOL_WINDOWS)
SG_HEADS, SG_DIM = 4, 64
SG_WIDTH = SG_HEADS * SG_DIM
D_FF = 2816
FF_CHUNKS = D_FF // P
GROUPS = 2
FG = FF_CHUNKS // GROUPS

TILE = 1024
N_V, N_POOL, N_Q, N_KV, N_KR, N_U = 0, 2, 4, 7, 9, 10
N_UQ, N_UK, N_UV, N_WO = 12, 16, 17, 18
N_FFN = 26
DOWN_TILES = -(-FG // 2)
GROUP_TILES = 2 * FG + 2 * DOWN_TILES
LAYER_TILES = N_FFN + GROUPS * GROUP_TILES
MIX2_T0 = LAYERS * LAYER_TILES
MIX2_TILES = 24
WO2_TILES = 8
N_TILES = MIX2_T0 + MIX2_TILES + WO2_TILES
UQ_W = 2 * QC * QK

ADA_TILES = 6 * D // (2 * P)
ADA_PER_GROUP = ADA_TILES // (LAYERS * GROUPS)

G_MIX, G_FFN, G_Q, G_KV, G_PS = 0, DK, 2 * DK, 2 * DK + QC, 2 * DK + QC + KVC
N_GAIN = G_PS + 2
PR_BS = N_GAIN + (N_GAIN % 2)
PR_SG = PR_BS + 2 * P
PR_WS = PR_SG + SG_WIDTH
PR_WP = PR_WS + SG_HEADS * P
N_PARAM = PR_WP + 2 * P

C_ID, C_ONE, C_CNT, C_ROT, C_FREQ = 0, P, 2 * P, 2 * P + 2 * S, 2 * P + 2 * S + ROPE
C_TRI = C_FREQ + 1
C_IOTA = C_TRI + P
C_I2 = C_IOTA + P
C_EPS = C_I2 + 64
C_GEPS = C_EPS + 1
N_CONST = C_GEPS + 1

RET_HEADS, RET_QK, RET_V = 4, 64, 128
DIL_HEADS, DIL_DIM = 8, 64
DIL_CONFIGS = ((128, 1), (512, 4), (2048, 16))
MASKED = -1e30
REL = 2 * S - P
REL0 = S - P
EXPERTS, CAPACITY, D_EXP = 16, 2 * S // 16, 2048
Q2 = {"rqk": 0, "aqk": 4, "rv": 12, "rg": 16, "av": 20, "wo": 24}
P2_PRE, P2_POST, P2_FPRE, P2_FPOST = 0, DK, 2 * DK, 3 * DK
P2_B = 4 * DK
P2_LOGIT = P2_B + 6 * DK
N_P2 = P2_LOGIT + 2 * RET_HEADS
SHIFT_M, SCALE_M, GATE_M, SHIFT_F, SCALE_F, GATE_F = (j * DK for j in range(6))

MT = 2 * D
E_TILES = 24
RAW_RING, SPLIT_RING = 6, 3
HALF_F = D_EXP // 2

TWO_PI = 6.283185307179586
PI2_A = 6.28125
PI2_B = 0.0019350051879882812
PI2_C = TWO_PI - PI2_A - PI2_B
MAGIC = 12582912.0
PI_IN = 3.1415925


def build(nc, A):
    ctx = ExitStack()
    with ctx:
        def sb(name, shape, dt=F32, where=None):
            return (where or ctx).enter_context(nc.sbuf_tensor(name, shape, dt))

        names = (
            "const_in x_in cbc_in cos_done raw_in0 raw_in1 hi_done lo_done tile_used params_in params_free pos_in trig_arg trig_done "
            "ada_in ada_used silu_c x_upd nrt xn_done tr_done hn_hi hn_lo v_out vsq_done vss_done proj_out ssq_done rt_done "
            "cn_done c_hi c_lo vn_ready pool_ready pmm_done sg_done sgr mix_hi mix_lo qe_done q_raw rot_done q_rope "
            "k_done k_out v2_out s_done nm_done p_done tr2_done pts_done av_done a_out at_done silu_done fr_done fhi flo "
            "out_done p2_in fn_in rel_in diag_done rows_done rows_out sg_in sg_exp xf_done tmb hib lob rt2 pj2 rv_out rg_out av_out "
            "e_arg e_tab tab_free abs_done tab_ready rs_done dec_done y_done gn_var gn_rt yn ret_out s2_done nm2 p2_done tr3 "
            "pts2 av2 a2_out ct_done mh ml post_ss post_rt post_r t_ready x2_upd h_done hT_done hT_out wr_in lg_done lg_sh "
            "lg_exp aff_done affT thr_d thr_bc ge_done pre_done route_done "
            "moe_hi moe_lo moe_used unit_out sc_done sc_add sgT sg_ready t_jobs silu_m hf_m hhi hlo g2_ready gg_ready gat_done "
            "gmod xhi xlo acc_zero moe_free fin_ss fin_out"
        ).split()
        names += [f"moe_in{i}" for i in range(RAW_RING)]
        sem = {n: ctx.enter_context(nc.semaphore(n)) for n in names}
        bank = [ctx.enter_context(nc.psum_tensor(f"bank{i}", [P, BANK], F32)) for i in range(8)]

        const = sb("const", [P, N_CONST])
        ident, ones = const[:, C_ID:C_ID + P], const[:, C_ONE:C_ONE + P]
        x = sb("x", [P, TC, D])
        hTh, hTl = sb("hTh", [P, DK, S], F32R), sb("hTl", [P, DK, S], F32R)
        raw_t, whi_t, wlo_t = sb("raw_t", [P, MT]), sb("whi_t", [P, MT], F32R), sb("wlo_t", [P, MT], F32R)
        raw, whi, wlo = ([t[:, i * TILE:(i + 1) * TILE] for i in range(2)] for t in (raw_t, whi_t, wlo_t))
        junk = sb("junk", [P, D])
        stats = sb("stats", [P, 64])
        mods = sb("mods", [P, 6 * DK])

        b1 = ExitStack()
        param = sb("param", [P, N_PARAM], where=b1)
        trig = sb("trig", [P, 2, S], where=b1)
        ada = sb("ada", [P, 2, D], where=b1)
        cbc = sb("cbc", [P, D], where=b1)
        ada_sum = sb("ada_sum", [P, 2 * ADA_PER_GROUP], where=b1)
        vstat = sb("vstat", [P, 3, TC * SG_HEADS], where=b1)
        astat = sb("astat", [P, 4, HEADS * TC], where=b1)
        xn = sb("xn", [P, TC * D], where=b1)
        with ExitStack() as mix_scope:
            craw = sb("craw", [P, QC + KVC, S], where=mix_scope)
            ch = sb("ch", [P, QC + KVC, S], F32R, where=mix_scope)
            cl = sb("cl", [P, QC + KVC, S], F32R, where=mix_scope)
            rbc = sb("rbc", [P, 2, S], where=mix_scope)
            qk = sb("qk", [P, 2 * HEADS * S], where=mix_scope)
            vt = sb("vt", [P, TC, HEADS * VDIM], where=mix_scope)
            uT = sb("uT", [P, 2, S], where=mix_scope)
            krw = sb("krw", [P, S], where=mix_scope)
        with ExitStack() as ffn_scope:
            fTh = sb("fTh", [P, FG, S], F32R, where=ffn_scope)
            fTl = sb("fTl", [P, FG, S], F32R, where=ffn_scope)
            sgr = sb("sgr_t", [P, 2, S], where=ffn_scope)
            fr = sb("fr", [P, 2, S], where=ffn_scope)
        b1.close()
        rows = sb("rows", [P, 2, D])
        with ExitStack() as b2:
            rqk = sb("rqk", [P, 4, S], where=b2)
            aqk = sb("aqk", [P, 8, S], where=b2)
            avt = sb("avt", [P, TC, S], where=b2)
            rvt = sb("rvt", [P, TC, S], where=b2)
            rgt = sb("rgt", [P, TC, S], where=b2)
            xh2 = sb("xh2", [P, TC * D], where=b2)
            cat = sb("cat", [P, TC, D], where=b2)
            tab = sb("tab", [P, 2, REL], where=b2)
            rel = sb("rel", [P, 2 * REL], where=b2)
            sm = sb("sm", [P, 2, S], where=b2)
            prob2_t = sb("prob2", [P, 4, S], where=b2)
            fnrow = sb("fnrow", [P, D], where=b2)
            p2 = sb("p2", [P, N_P2], where=b2)
            decay_lg = sb("decay_lg", [P, 8, 2 * RET_HEADS], where=b2)
            gn = sb("gn", [P, TC * 6 + TC * 2 + 2 * TC], where=b2)
            ast2 = sb("ast2", [P, 4, DIL_HEADS * TC], where=b2)
            st2 = sb("st2", [P, 16], where=b2)
        with ExitStack() as b3:
            moe_raw = [sb(f"mraw{i}", [P, MT], where=b3) for i in range(RAW_RING - 1)] + [raw_t]
            hn = sb("hn", [P, TC, D], where=b3)
            acc = sb("acc", [P, TC, D], where=b3)
            moe_hi = [whi_t] + [sb(f"mhi{i}", [P, MT], F32R, where=b3) for i in range(SPLIT_RING - 1)]
            asb = sb("asb", [P, 2, HALF_F], where=b3)
            sgl = sb("sgl", [P, S], where=b3)
            hf = sb("hf", [P, S], where=b3)
            g2 = sb("g2", [P, TC, P], where=b3)
            gg2 = sb("gg2", [P, TC, P], where=b3)
            sgt = sb("sgt", [P, S], where=b3)
            ysb = sb("ysb", [P, D], where=b3)
            wr = sb("wr", [P, DK, EXPERTS], where=b3)
            aff = sb("aff", [P, TC, EXPERTS], where=b3)
            rt_s = sb("rt_s", [P, 8, TC, EXPERTS], where=b3)
            affe = sb("affe", [P, (EXPERTS + 1) * TC], where=b3)
            slots = sb("slots", [P, (EXPERTS + 1) * TC], where=b3)
            cur = sb("cur", [P, 2, TC], where=b3)
        hT_flat = hTh[:, :, :].rearrange("p k t -> p (k t)")
        lo_flat = hTl[:, :, :].rearrange("p k t -> p (k t)")
        xTe = hT_flat[:, 0:DK * P].rearrange("p (k t) -> p k t", t=P)
        hTe = hT_flat[:, DK * P:3 * DK * P].rearrange("p (k t) -> p k t", t=P)
        moe_lo = [wlo_t[:, :], lo_flat[:, 0:MT], lo_flat[:, MT:2 * MT]]
        hTf = acc[:, :, :].rearrange("p i d -> p (i d)").rearrange("p (k t) -> p k t", t=S)
        top = ysb[0:EXPERTS, 0:S]
        top8 = ysb[0:EXPERTS, S:S + 64]
        dthr = ysb[0:EXPERTS, S + 64:S + 64 + EXPERTS]
        diag = xh2[:, 0:2 * DK * P].rearrange("p (k n) -> p k n", n=P)
        decayed = [xh2[:, r * TC * S:(r + 1) * TC * S].rearrange("p (j t) -> p j t", t=S) for r in range(2)]
        xh4 = xh2[:, :].rearrange("p (i d) -> p i d", i=TC)
        prob2 = [prob2_t[:, r, :] for r in range(2)]
        probT2 = [prob2_t[:, 2 + r, :] for r in range(2)]
        delta, lnm = rel[:, 0:REL], rel[:, REL:2 * REL]
        bst = gn[:, 0:6 * TC].rearrange("p (i s) -> p i s", s=6)
        mv = gn[:, 6 * TC:8 * TC].rearrange("p (i s) -> p i s", s=2)
        gr = gn[:, 8 * TC:10 * TC]

        def rel_cols(i):
            return slice(REL0 - i * P, REL0 - i * P + S)

        xn4 = xn[:, :].rearrange("p (i d) -> p i d", i=TC)
        csq = xn[:, 0:(QC + KVC) * S].rearrange("p (c t) -> p c t", t=S)
        prob = [xn[:, r * S:(r + 1) * S] for r in range(2)]
        probT = [xn[:, (2 + r) * S:(3 + r) * S] for r in range(2)]
        att = xn[:, 4 * S:8 * S].rearrange("p (i n) -> p i n", i=TC)
        qT = qk[:, 0:HEADS * S].rearrange("p (h t) -> p h t", t=S)
        kT = qk[:, HEADS * S:].rearrange("p (h t) -> p h t", t=S)
        W2 = S + 2 * PAD
        hp = qk[:, 0:2 * W2].rearrange("p (c t) -> p c t", c=2)
        s2 = qk[:, 2 * W2:4 * W2].rearrange("p (c t) -> p c t", c=2)
        s4 = qk[:, 4 * W2:6 * W2].rearrange("p (c t) -> p c t", c=2)
        s8 = qk[:, 6 * W2:7 * W2]
        o = 7 * W2
        pooled = qk[:, o:o + 2 * S].rearrange("p (c t) -> p c t", c=2)
        vz = qk[:, o + 2 * S:o + 4 * S].rearrange("p (i n) -> p i n", i=TC)
        vsq = qk[:, o + 4 * S:o + 6 * S].rearrange("p (i n) -> p i n", i=TC)
        assert o + 6 * S <= 2 * HEADS * S
        vn = junk[:, :].rearrange("p (i n) -> p i n", i=TC)
        wsT = param[:, PR_WS:PR_WP].rearrange("p (g n) -> p g n", g=SG_HEADS)
        wp_bd = param[:, PR_WP:N_PARAM].rearrange("p (c n) -> p c n", c=2)

        def gain(k):
            return param[:, k:k + 1]

        def tiles_before(l, g, n):
            return l * LAYER_TILES + g * GROUP_TILES + n, l * (LAYER_TILES // 2) + g * (GROUP_TILES // 2) + n // 2

        def tile_width(n):
            if N_UQ <= n < N_UK:
                return UQ_W
            if n >= N_FFN and (n - N_FFN) % GROUP_TILES >= 2 * FG:
                q = ((n - N_FFN) % GROUP_TILES - 2 * FG) % DOWN_TILES
                return min(2, FG - 2 * q) * BANK
            return TILE

        block = ctx.enter_context(nc.Block())

        @block.sync
        def _(sp):
            sp.dma_start(const[:, :], A["const"]).then_inc(sem["const_in"], 16)
            sp.dma_start(x[:, :, :], A["x"].rearrange("b (i p) d -> p (b i) d", p=P)).then_inc(sem["x_in"], 16)

            def load(l, g, n):
                before, pair = tiles_before(l, g, n)
                w = tile_width(n)
                sp.wait_ge(sem["lo_done"], before + 1)
                sp.dma_start(raw[n % 2][:, 0:w], A["tiles"][bass.ds(before, 1), :, 0:w].rearrange("a p n -> p (a n)"))\
                    .then_inc(sem[f"raw_in{n % 2}"], 16)

            with sp.Fori(0, LAYERS) as l:
                for n in range(N_FFN):
                    load(l, 0, n)
                with sp.Fori(0, GROUPS) as g:
                    for n in range(N_FFN, N_FFN + GROUP_TILES):
                        load(l, g, n)
            for t in range(MIX2_T0, N_TILES):
                sp.wait_ge(sem["lo_done"], t + 1)
                sp.dma_start(raw[t % 2], A["tiles"][t]).then_inc(sem[f"raw_in{t % 2}"], 16)
            sp.wait_ge(sem["moe_free"], 1)
            with sp.Fori(0, EXPERTS) as e:
                for n in range(E_TILES):
                    sp.wait_ge(sem["moe_lo"], e * E_TILES + n + 1)
                    u, q = n // 4, n % 4
                    if u < 4:
                        src = A["w_up" if u % 2 else "w_gate"][bass.ds(e, 1), q * 256:(q + 1) * 256,
                                                               (u // 2) * HALF_F:(u // 2 + 1) * HALF_F]
                    else:
                        q = n - 16
                        src = A["w_down"][bass.ds(e, 1), q * 256:(q + 1) * 256, :]
                    sp.dma_start(moe_raw[n % RAW_RING][:, :].rearrange("p (c f) -> p c f", c=2),
                                 src.rearrange("a (c p) f -> p (a c) f", p=P)).then_inc(sem[f"moe_in{n % RAW_RING}"], 16)
            for i in range(TC):
                sp.wait_ge(sem["fin_out"], i + 1)
                sp.dma_start(A["out"][0, i * P:(i + 1) * P, :], x[:, i, :]).then_inc(sem["out_done"], 16)
            sp.wait_ge(sem["out_done"], 16 * TC)

        @block.scalar
        def _(act):
            def split(l, g, n):
                before, pair = tiles_before(l, g, n)
                s, w = n % 2, tile_width(n)
                act.wait_ge(sem[f"raw_in{s}"], (pair + 1) * 16)
                act.wait_ge(sem["tile_used"], before + 1)
                nc.scalar.activation(whi[s][:, 0:w], raw[s][:, 0:w], ACT.Copy).then_inc(sem["hi_done"], 1)

            def used(l, g, n):
                act.wait_ge(sem["tile_used"], tiles_before(l, g, n)[0] + 3)

            def norm_stats(nn):
                for i in range(TC):
                    if i:
                        act.drain()
                    nc.scalar.activation(junk[:, :], x[:, i, :], ACT.Square, accum_out=stats[:, i:i + 1])
                act.drain()
                nc.scalar.activation(stats[:, 4:8], stats[:, 0:4], ACT.Sqrt, scale=1.0 / D,
                                     bias=const[:, C_EPS:C_EPS + 1]).then_inc(sem["nrt"], 1)

            def norm_hi(nn, g0):
                for k in range(DK):
                    act.wait_ge(sem["tr_done"], nn * DK + k + 1)
                    nc.scalar.activation(hTh[:, k, :], bank[k % 4][:, :], ACT.Copy, scale=gain(g0 + k))\
                        .then_inc(sem["hn_hi"], 1)

            act.wait_ge(sem["const_in"], 16)
            act.wait_ge(sem["cbc_in"], 16)
            nc.scalar.activation(cbc[:, :], cbc[:, :], ACT.Silu).then_inc(sem["silu_c"], 1)
            act.wait_ge(sem["trig_arg"], 1)
            for r in range(2):
                last = nc.scalar.activation(trig[64:96, r, :], trig[64:96, r, :], ACT.Sin)
            last.then_inc(sem["trig_done"], 1)
            split(0, 0, 0)
            with act.Fori(0, LAYERS) as l:
                act.drain()
                act.wait_ge(sem["x_upd"], l * 24 + 1)
                norm_stats(l * 2)
                act.wait_ge(sem["params_in"], l * 16 + 16)
                norm_hi(l * 2, G_MIX)
                split(l, 0, 1)
                used(l, 0, 0)
                split(l, 0, 2)
                used(l, 0, 1)
                for i in range(TC):
                    nc.scalar.activation(vz[:, i, :], bank[i][:, 0:SG_WIDTH], ACT.Gelu_apprx_tanh).then_inc(sem["v_out"], 1)
                for n in range(N_POOL, N_UQ):
                    c = n - N_POOL
                    b = bank[4 + c % 4]
                    split(l, 0, n + 1)
                    if n == N_U:
                        act.wait_ge(sem["ssq_done"], l * 2 + 2)
                        nc.scalar.activation(rbc[:, 0, :], bank[0][:, :], ACT.Sqrt, scale=1.0 / Q_LORA,
                                             bias=const[:, C_EPS:C_EPS + 1]).then_inc(sem["rt_done"], 1)
                        nc.scalar.activation(rbc[:, 1, :], bank[1][:, :], ACT.Sqrt, scale=1.0 / KV_LORA,
                                             bias=const[:, C_EPS:C_EPS + 1]).then_inc(sem["rt_done"], 1)
                        act.wait_ge(sem["vss_done"], l + 1)
                        nc.scalar.activation(vstat[:, 1, :], vstat[:, 0, :], ACT.Sqrt, scale=1.0 / SG_DIM,
                                             bias=const[:, C_EPS:C_EPS + 1]).then_inc(sem["rt_done"], 1)
                    used(l, 0, n)
                    if n < N_Q:
                        nc.scalar.activation(hp[:, c, PAD:PAD + S], b[:, :], ACT.Copy).then_inc(sem["proj_out"], 1)
                    elif n < N_KR:
                        nc.scalar.activation(craw[:, n - N_Q, :], b[:, :], ACT.Copy)
                        nc.scalar.activation(csq[:, n - N_Q, :], b[:, :], ACT.Square).then_inc(sem["proj_out"], 1)
                    elif n < N_U:
                        nc.scalar.activation(krw[0:QK, :], b[0:QK, :], ACT.Copy).then_inc(sem["proj_out"], 1)
                    else:
                        nc.scalar.activation(uT[:, n - N_U, :], b[:, :], ACT.Gelu_apprx_tanh).then_inc(sem["proj_out"], 1)
                act.wait_ge(sem["cn_done"], l + 1)
                for c in range(QC + KVC):
                    nc.scalar.activation(ch[:, c, :], craw[:, c, :], ACT.Copy, scale=gain(G_Q + c)).then_inc(sem["c_hi"], 1)
                for c in range(2):
                    act.wait_ge(sem["pmm_done"], l * 2 + c + 1)
                    nc.scalar.activation(hTh[:, 4 + c, :], bank[2 + c][:, :], ACT.Copy, scale=gain(G_PS + c))\
                        .then_inc(sem["mix_hi"], 1)
                for c in range(2):
                    act.wait_ge(sem["sgr"], l * 2 + c + 1)
                    nc.scalar.activation(hTh[:, 6 + c, :], craw[:, c, :], ACT.Copy).then_inc(sem["mix_hi"], 1)
                for m in range(HEADS // 2):
                    split(l, 0, N_UQ + m + 1)
                    act.wait_ge(sem["qe_done"], l * 4 + m + 1)
                    nc.scalar.activation(qT[0:QK, 2 * m, :], bank[4][0:QK, :], ACT.Copy).then_inc(sem["q_raw"], 1)
                    used(l, 0, N_UQ + m)
                    nc.scalar.activation(qT[0:QK, 2 * m + 1, :], bank[5][0:QK, :], ACT.Copy).then_inc(sem["q_raw"], 1)
                split(l, 0, N_UV)
                for j in range(HEADS // 2):
                    if j < 3:
                        act.wait_ge(sem["k_done"], l * 3 + j + 1)
                    else:
                        used(l, 0, N_UK)
                    nc.scalar.activation(kT[0:NOPE, 2 * j, :], bank[j][0:64, :], ACT.Copy)
                    nc.scalar.activation(kT[0:NOPE, 2 * j + 1, :], bank[j][64:128, :], ACT.Copy).then_inc(sem["k_out"], 1)
                split(l, 0, N_WO)
                for it in range(HEADS * TC + 1):
                    if it < HEADS * TC:
                        act.wait_ge(sem["nm_done"], l * 32 + it + 1)
                        if it >= 2:
                            act.wait_ge(sem["tr2_done"], l * 32 + it - 1)
                        nc.scalar.activation(prob[it % 2], bank[it % 2][:, :], ACT.Exp, bias=astat[:, 1, it:it + 1],
                                             scale=ATT_SCALE, accum_out=astat[:, 2, it:it + 1]).then_inc(sem["p_done"], 1)
                    if it >= 1:
                        e = it - 1
                        act.wait_ge(sem["tr2_done"], l * 32 + e + 1)
                        if e >= 2:
                            act.wait_ge(sem["av_done"], l * 32 + e - 1)
                        nc.scalar.activation(probT[e % 2], bank[2 + e % 2][:, :], ACT.Copy).then_inc(sem["pts_done"], 1)
                for k in range(4):
                    act.wait_ge(sem["at_done"], l * 4 + k + 1)
                    nc.scalar.activation(hTh[:, k, :], bank[6 + k % 2][:, :], ACT.Copy).then_inc(sem["mix_hi"], 1)
                for n in range(N_WO, N_FFN):
                    split(l, 0, n + 1)
                act.drain()
                act.wait_ge(sem["x_upd"], l * 24 + 9)
                norm_stats(l * 2 + 1)
                norm_hi(l * 2 + 1, G_FFN)
                with act.Fori(0, GROUPS) as g:
                    for j in range(FG):
                        n = N_FFN + 2 * j
                        split(l, g, n + 1)
                        used(l, g, n)
                        nc.scalar.activation(sgr[:, j % 2, :], bank[2 * (j % 2)][:, :], ACT.Silu).then_inc(sem["silu_done"], 1)
                        split(l, g, n + 2)
                        act.wait_ge(sem["fr_done"], (l * GROUPS + g) * FG + j + 1)
                        nc.scalar.activation(fTh[:, j, :], fr[:, j % 2, :], ACT.Copy).then_inc(sem["fhi"], 1)
                    for q in range(2 * DOWN_TILES):
                        n = N_FFN + 2 * FG + q
                        if q < 2 * DOWN_TILES - 1:
                            split(l, g, n + 1)
                    before, pair = tiles_before(l, g, N_FFN + GROUP_TILES)
                    act.wait_ge(sem["raw_in0"], (pair + 1) * 16)
                    act.wait_ge(sem["tile_used"], before + 1)
                    nc.scalar.activation(whi[0][:, :], raw[0][:, :], ACT.Copy).then_inc(sem["hi_done"], 1)

            def copy2(out, in_, name, **kw):
                nc.scalar.activation(out, in_, kw.pop("func", ACT.Copy), **kw).then_inc(sem[name], 1)

            def split2(n):
                t = MIX2_T0 + n
                act.wait_ge(sem[f"raw_in{t % 2}"], (t // 2 + 1) * 16)
                act.wait_ge(sem["tile_used"], t + 1)
                copy2(whi[t % 2], raw[t % 2], "hi_done")

            def used2(n):
                act.wait_ge(sem["tile_used"], MIX2_T0 + n + 3)

            act.wait_ge(sem["sg_in"], 1)
            copy2(decay_lg[:, 1, :], decay_lg[:, 0, :], "sg_exp", func=ACT.Exp, scale=-1.0)
            act.drain()
            act.wait_ge(sem["x_upd"], LAYERS * 24 + 1)
            norm_stats(4)
            for b in range(4):
                act.wait_ge(sem["rows_done"], b // 2 + 1)
                copy2(rows[:, b // 2, (b % 2) * BANK:(b % 2 + 1) * BANK], bank[4 + b][:, :], "rows_out")
            act.drain()
            act.wait_ge(sem["xf_done"], 1)
            norm_stats(5)
            for k in range(DK):
                act.wait_ge(sem["tmb"], k + 1)
                copy2(hTh[:, k, :], sm[:, k % 2, :], "hib")

            def table(h):
                act.wait_ge(sem["e_arg"], h + 1)
                copy2(tab[:, h % 2, :], tab[:, h % 2, :], "e_tab", func=ACT.Exp)

            for c in range(12):
                split2(c + 1)
                used2(c)
                if c < 4:
                    copy2(rqk[:, c, :], bank[4 + c % 4][:, :], "pj2", scale=1.0 if c < 2 else RET_QK ** -0.5)
                else:
                    copy2(aqk[:, c - 4, :], bank[4 + c % 4][:, :], "pj2", scale=DIL_DIM ** -0.5 if c < 8 else 1.0)
                if c == 4:
                    table(0)
                    table(1)
            for n in range(Q2["rv"], Q2["wo"]):
                split2(n + 1)
                if n == Q2["av"] - 1:
                    used2(n)
                    for i in range(TC):
                        copy2(rgt[:, i, :], bank[4 + i][:, :], "rg_out", func=ACT.Silu)
            for h in range(1, RET_HEADS + 1):
                if h + 1 < RET_HEADS:
                    table(h + 1)
                act.wait_ge(sem["gn_var"], h)
                copy2(gr[:, 0:TC], mv[:, :, 1], "gn_rt", func=ACT.Sqrt, bias=const[:, C_GEPS:C_GEPS + 1])
            for it in range(DIL_HEADS * TC + 1):
                if it < DIL_HEADS * TC:
                    act.wait_ge(sem["nm2"], it + 1)
                    if it >= 2:
                        act.wait_ge(sem["tr3"], it - 1)
                    copy2(prob2[it % 2], sm[:, it % 2, :], "p2_done", func=ACT.Exp, bias=ast2[:, 1, it:it + 1],
                          accum_out=ast2[:, 2, it:it + 1])
                if it >= 1:
                    act.wait_ge(sem["tr3"], it)
                    if it >= 3:
                        act.wait_ge(sem["av2"], it - 2)
                    copy2(probT2[(it - 1) % 2], bank[2 + (it - 1) % 2][:, :], "pts2")
            for k in range(DK):
                act.wait_ge(sem["ct_done"], k + 1)
                copy2(hTh[:, k, :], bank[6 + k % 2][:, :], "mh")
            for half in range(2):
                for q in range(4):
                    n = Q2["wo"] + 4 * half + q
                    if n + 1 < MIX2_TILES + WO2_TILES:
                        split2(n + 1)
                used2(Q2["wo"] + 4 * half + 3)
                for i in range(TC):
                    act.drain()
                    last = nc.scalar.activation(junk[:, 0:BANK], bank[4 * half + i][:, :], ACT.Square,
                                                accum_out=st2[:, 4 * half + i:4 * half + i + 1])
            last.then_inc(sem["post_ss"], 1)
            act.wait_ge(sem["post_r"], 1)
            copy2(st2[:, 4:8], st2[:, 0:4], "post_rt", func=ACT.Sqrt, scale=1.0 / D, bias=const[:, C_EPS:C_EPS + 1])
            act.drain()
            act.wait_ge(sem["x2_upd"], 2 * TC)
            norm_stats(6)
            for k in range(DK):
                act.wait_ge(sem["hT_done"], k + 1)
                copy2(hTf[:, k, :], bank[k % 4][:, :], "hT_out", func=ACT.Identity, scale=mods[:, SCALE_F + k:SCALE_F + k + 1],
                      bias=mods[:, SHIFT_F + k:SHIFT_F + k + 1])
            act.wait_ge(sem["lg_sh"], 1)
            copy2(rt_s[:, 0, :, :], rt_s[:, 0, :, :], "lg_exp", func=ACT.Exp)

            def x_hi(value):
                act.wait_ge(sem["gmod"], value)
                copy2(xTe[:, :, 0:64], hf[:, :].rearrange("p (k t) -> p k t", t=64), "xhi")

            x_hi(1)
            act.sem_inc(sem["unit_out"], 1)
            act.sem_inc(sem["moe_hi"], 1)
            with act.Fori(0, EXPERTS) as e:
                def evac(dst, b0, tile, units):
                    act.wait_ge(sem["moe_used"], e * E_TILES + tile + 1 + SPLIT_RING)
                    for b in range(2):
                        last = nc.scalar.activation(dst[:, b * BANK:(b + 1) * BANK], bank[b0 + b][:, :], ACT.Copy)
                    last.then_inc(sem["unit_out"], 1)

                for n in range(E_TILES):
                    s = n % RAW_RING
                    act.wait_ge(sem[f"moe_in{s}"], e * (E_TILES // RAW_RING * 16) + (n // RAW_RING + 1) * 16)
                    act.wait_ge(sem["moe_used"], e * E_TILES + n + 1)
                    copy2(moe_hi[n % SPLIT_RING][:, :], moe_raw[s][:, :], "moe_hi")
                    if n == 1:
                        evac(ysb, 4, -1, 0)
                    elif n == 5:
                        evac(asb[:, 0, :], 0, 3, 1)
                    elif n == 7:
                        act.wait_ge(sem["sgT"], e + 1)
                        copy2(sgt[:, :], bank[7][:, :], "sg_ready")
                    elif n == 8 or n == 16:
                        act.wait_ge(sem["t_jobs"], e * 4 + (1 if n == 8 else 3))
                        copy2(sgl[:, :], bank[6][:, :], "silu_m", func=ACT.Silu)
                    elif n == 9:
                        evac(asb[:, 1, :], 2, 7, 2)
                    elif n == 13:
                        act.wait_ge(sem["hf_m"], e * 2 + 1)
                        copy2(hTe[:, 0:8, 0:64], hf[:, :].rearrange("p (k t) -> p k t", t=64), "hhi")
                        evac(asb[:, 0, :], 0, 11, 3)
                    elif n == 17:
                        evac(asb[:, 1, :], 2, 15, 4)
                    elif n == 19:
                        x_hi(e + 2)
                    elif n == 20:
                        act.wait_ge(sem["hf_m"], e * 2 + 2)
                        copy2(hTe[:, 8:16, 0:64], hf[:, :].rearrange("p (k t) -> p k t", t=64), "hhi")
            act.wait_ge(sem["moe_used"], EXPERTS * E_TILES + SPLIT_RING)
            for b in range(2):
                last = nc.scalar.activation(ysb[:, b * BANK:(b + 1) * BANK], bank[4 + b][:, :], ACT.Copy)
            last.then_inc(sem["unit_out"], 1)
            act.wait_ge(sem["sc_add"], 2 * EXPERTS + 2)
            for i in range(TC):
                act.drain()
                nc.scalar.activation(asb[:, 0, :], acc[:, i, :], ACT.Square, accum_out=stats[:, i:i + 1])
            act.drain()
            copy2(stats[:, 4:8], stats[:, 0:4], "fin_ss", func=ACT.Sqrt, scale=1.0 / D, bias=const[:, C_EPS:C_EPS + 1])

        @block.vector
        def _(dve):
            def split(l, g, n):
                before, _ = tiles_before(l, g, n)
                s, w = n % 2, tile_width(n)
                dve.wait_ge(sem["hi_done"], before + 1)
                nc.vector.tensor_tensor(wlo[s][:, 0:w], raw[s][:, 0:w], whi[s][:, 0:w].bitcast(F32), ALU.subtract)\
                    .then_inc(sem["lo_done"], 1)

            def used(l, g, n):
                dve.wait_ge(sem["tile_used"], tiles_before(l, g, n)[0] + 3)

            def norm_scale(nn):
                dve.wait_ge(sem["nrt"], nn + 1)
                nc.vector.reciprocal(stats[:, 8:12], stats[:, 4:8])
                dve.drain()
                for i in range(TC):
                    last = nc.vector.tensor_scalar(xn4[:, i, :], x[:, i, :], stats[:, 8 + i:9 + i], None, ALU.mult)
                last.then_inc(sem["xn_done"], 1)

            def norm_lo(nn, g0):
                for k in range(DK):
                    dve.wait_ge(sem["hn_hi"], nn * DK + k + 1)
                    nc.vector.scalar_tensor_tensor(out=hTl[:, k, :], in0=bank[k % 4][:, :], scalar=gain(g0 + k),
                                                   in1=hTh[:, k, :].bitcast(F32), op0=ALU.mult, op1=ALU.subtract)\
                        .then_inc(sem["hn_lo"], 1)

            dve.sem_inc(sem["lo_done"], 2)
            dve.wait_ge(sem["x_in"], 16)
            dve.sem_inc(sem["x_upd"], 1)
            dve.sem_inc(sem["params_free"], 1)
            dve.sem_inc(sem["ada_used"], 1)
            dve.wait_ge(sem["pos_in"], 16)
            dve.wait_ge(sem["const_in"], 16)
            R = slice(64, 96)
            ang, turns, t2 = xn[R, 0:S], xn[R, S:2 * S], xn[R, 2 * S:3 * S]
            nc.vector.tensor_copy(ang, trig[R, 0, :].bitcast(I32))
            dve.drain()
            nc.vector.tensor_scalar(ang, ang, const[R, C_FREQ:C_FREQ + 1], None, ALU.mult)
            for r, quarter in ((0, 0.25), (1, 0.0)):
                dve.drain()
                nc.vector.tensor_scalar(turns, ang, 1.0 / TWO_PI, quarter, ALU.mult, ALU.add)
                dve.drain()
                nc.vector.tensor_scalar(turns, turns, MAGIC, None, ALU.add)
                dve.drain()
                nc.vector.tensor_scalar(turns, turns, MAGIC, None, ALU.subtract)
                dve.drain()
                nc.vector.scalar_tensor_tensor(out=t2, in0=turns, scalar=-PI2_A, in1=ang, op0=ALU.mult, op1=ALU.add)
                for part in (PI2_B, PI2_C):
                    dve.drain()
                    nc.vector.scalar_tensor_tensor(out=t2, in0=turns, scalar=-part, in1=t2, op0=ALU.mult, op1=ALU.add)
                dve.drain()
                nc.vector.tensor_scalar(t2, t2, quarter * TWO_PI, PI_IN, ALU.add, ALU.min)
                dve.drain()
                last = nc.vector.tensor_scalar(trig[R, r, :], t2, -PI_IN, None, ALU.max)
            last.then_inc(sem["trig_arg"], 1)
            split(0, 0, 0)
            with dve.Fori(0, LAYERS) as l:
                norm_scale(l * 2)
                norm_lo(l * 2, G_MIX)
                split(l, 0, 1)
                split(l, 0, 2)
                for n in range(N_POOL, N_UQ):
                    split(l, 0, n + 1)
                    if n == N_Q:
                        dve.wait_ge(sem["vsq_done"], l + 1)
                        nc.vector.tensor_reduce(vstat[:, 0, :], vsq.rearrange("p i (h e) -> p (i h) e", e=SG_DIM),
                                                AX.X, ALU.add).then_inc(sem["vss_done"], 1)
                    if n == N_U:
                        dve.wait_ge(sem["rt_done"], l * 3 + 3)
                        nc.vector.reciprocal(rbc[:, :, :], rbc[:, :, :])
                        nc.vector.reciprocal(vstat[:, 2, :], vstat[:, 1, :])
                        dve.drain()
                        nc.vector.tensor_tensor(craw[:, 0:QC, :], craw[:, 0:QC, :],
                                                rbc[:, 0:1, :].broadcast_to([P, QC, S]), ALU.mult)
                        nc.vector.tensor_tensor(craw[:, QC:, :], craw[:, QC:, :],
                                                rbc[:, 1:2, :].broadcast_to([P, KVC, S]), ALU.mult)\
                            .then_inc(sem["cn_done"], 1)
                        nc.vector.tensor_tensor(
                            vn.rearrange("p i (h e) -> p (i h) e", e=SG_DIM), vz.rearrange("p i (h e) -> p (i h) e", e=SG_DIM),
                            vstat[:, 2, :].rearrange("p (a b) -> p a b", b=1).broadcast_to([P, TC * SG_HEADS, SG_DIM]), ALU.mult)
                        dve.drain()
                        nc.vector.tensor_tensor(
                            vn, vn, param[:, PR_SG:PR_WS].rearrange("p (a n) -> p a n", a=1).broadcast_to([P, TC, SG_WIDTH]),
                            ALU.mult).then_inc(sem["vn_ready"], 1)
                for c in range(QC + KVC):
                    dve.wait_ge(sem["c_hi"], l * 5 + c + 1)
                    nc.vector.scalar_tensor_tensor(out=cl[:, c, :], in0=craw[:, c, :], scalar=gain(G_Q + c),
                                                   in1=ch[:, c, :].bitcast(F32), op0=ALU.mult, op1=ALU.subtract)\
                        .then_inc(sem["c_lo"], 1)
                for c in range(2):
                    dve.wait_ge(sem["mix_hi"], l * 8 + c + 1)
                    nc.vector.scalar_tensor_tensor(out=hTl[:, 4 + c, :], in0=bank[2 + c][:, :], scalar=gain(G_PS + c),
                                                   in1=hTh[:, 4 + c, :].bitcast(F32), op0=ALU.mult, op1=ALU.subtract)\
                        .then_inc(sem["mix_lo"], 1)
                dve.drain()
                dve.wait_ge(sem["proj_out"], l * 10 + 10)
                for c in range(2):
                    dve.wait_ge(sem["sg_done"], l * 2 + c + 1)
                    bias = param[:, PR_BS + c * P:PR_BS + (c + 1) * P].rearrange("p (a n) -> p a n", a=1)
                    v4 = lambda ap: ap.rearrange("p (i n) -> p i n", i=TC)
                    nc.vector.tensor_tensor(v4(craw[:, c, :]), v4(bank[c][:, :]), bias.broadcast_to([P, TC, P]), ALU.add)
                    dve.drain()
                    nc.vector.tensor_tensor(craw[:, c, :], craw[:, c, :], uT[:, c, :], ALU.mult).then_inc(sem["sgr"], 1)
                for c in range(2):
                    dve.wait_ge(sem["mix_hi"], l * 8 + c + 3)
                    nc.vector.tensor_tensor(hTl[:, 6 + c, :], craw[:, c, :], hTh[:, 6 + c, :].bitcast(F32), ALU.subtract)\
                        .then_inc(sem["mix_lo"], 1)

                def rope(h):
                    vec = qT[64:96, h, :] if h < HEADS else krw[64:96, :]
                    turned = craw[64:96, 2 + h % 2, :]
                    dve.wait_ge(sem["rot_done"], l * 9 + h + 1)
                    nc.vector.tensor_tensor(turned, bank[6 + h % 2][64:96, :], trig[64:96, 1, :], ALU.mult)
                    nc.vector.tensor_tensor(vec, vec, trig[64:96, 0, :], ALU.mult)
                    dve.drain()
                    last = nc.vector.tensor_tensor(vec, vec, turned, ALU.add)
                    if h == HEADS:
                        dve.drain()
                        last = nc.vector.tensor_copy(
                            kT[64:96, :, :], vec.rearrange("p (a t) -> p a t", a=1).broadcast_to([ROPE, HEADS, S]))
                    last.then_inc(sem["q_rope"], 1)
                    dve.drain()

                for m in range(HEADS // 2):
                    split(l, 0, N_UQ + m + 1)
                    if m:
                        rope(2 * m - 2)
                        rope(2 * m - 1)
                split(l, 0, N_UV)
                for h in range(HEADS - 2, HEADS + 1):
                    rope(h)
                split(l, 0, N_WO)
                used(l, 0, N_UV)
                for i in range(TC):
                    nc.vector.tensor_copy(vt[:, i, :], bank[4 + i][:, :]).then_inc(sem["v2_out"], 1)
                for it in range(HEADS * TC + 2):
                    if it < HEADS * TC:
                        dve.wait_ge(sem["s_done"], l * 32 + it + 1)
                        nc.vector.tensor_reduce(astat[:, 0, it:it + 1], bank[it % 2][:, :], AX.X, ALU.max)
                        dve.drain()
                        nc.vector.tensor_scalar(astat[:, 1, it:it + 1], astat[:, 0, it:it + 1], -ATT_SCALE, None, ALU.mult)\
                            .then_inc(sem["nm_done"], 1)
                    if it >= 2:
                        e = it - 2
                        h, i = e // TC, e % TC
                        dve.wait_ge(sem["av_done"], l * 32 + e + 1)
                        nc.vector.reciprocal(astat[:, 3, e:e + 1], astat[:, 2, e:e + 1])
                        dve.drain()
                        nc.vector.tensor_scalar(att[:, i, h * VDIM:(h + 1) * VDIM], bank[4 + e % 2][:, 0:VDIM],
                                                astat[:, 3, e:e + 1], None, ALU.mult).then_inc(sem["a_out"], 1)
                for k in range(4):
                    dve.wait_ge(sem["mix_hi"], l * 8 + 5 + k)
                    nc.vector.tensor_tensor(hTl[:, k, :], bank[6 + k % 2][:, :], hTh[:, k, :].bitcast(F32), ALU.subtract)\
                        .then_inc(sem["mix_lo"], 1)

                def add_to_x(half, b0):
                    for i in range(TC):
                        cols = x[:, i, half * BANK:(half + 1) * BANK]
                        nc.vector.tensor_tensor(cols, bank[b0 + i][:, :], cols, ALU.add).then_inc(sem["x_upd"], 1)

                for half in range(2):
                    for n in range(N_WO + 4 * half, N_WO + 4 * half + 4):
                        split(l, 0, n + 1)
                    used(l, 0, N_WO + 4 * half + 3)
                    add_to_x(half, 4 * half)
                dve.drain()
                norm_scale(l * 2 + 1)
                norm_lo(l * 2 + 1, G_FFN)
                dve.drain()
                dve.sem_inc(sem["params_free"], 1)
                with dve.Fori(0, GROUPS) as g:
                    lg = l * GROUPS + g
                    for j in range(FG):
                        n = N_FFN + 2 * j
                        split(l, g, n + 1)
                        if j < ADA_PER_GROUP:
                            dve.drain()
                            if j == 0:
                                dve.wait_ge(sem["silu_c"], 1)
                            dve.wait_ge(sem["ada_in"], (lg * ADA_PER_GROUP + j + 1) * 16)
                            for r in range(2):
                                if r:
                                    dve.drain()
                                last = nc.vector.tensor_tensor_reduce(
                                    out=junk[:, :], in0=ada[:, r, :], in1=cbc[:, :], scale=1.0, scalar=0.0, op0=ALU.mult,
                                    op1=ALU.add, accum_out=ada_sum[:, 2 * j + r:2 * j + r + 1])
                            last.then_inc(sem["ada_used"], 1)
                        split(l, g, n + 2)
                        used(l, g, n + 1)
                        dve.wait_ge(sem["silu_done"], lg * FG + j + 1)
                        nc.vector.tensor_tensor(fr[:, j % 2, :], sgr[:, j % 2, :], bank[2 * (j % 2) + 1][:, :], ALU.mult)\
                            .then_inc(sem["fr_done"], 1)
                        dve.wait_ge(sem["fhi"], lg * FG + j + 1)
                        nc.vector.tensor_tensor(fTl[:, j, :], fr[:, j % 2, :], fTh[:, j, :].bitcast(F32), ALU.subtract)\
                            .then_inc(sem["flo"], 1)
                    dve.drain()
                    nc.vector.tensor_copy(mods[:, bass.ds(lg * (2 * ADA_PER_GROUP), 2 * ADA_PER_GROUP)], ada_sum[:, :])
                    for q in range(2 * DOWN_TILES):
                        n = N_FFN + 2 * FG + q
                        if q < 2 * DOWN_TILES - 1:
                            split(l, g, n + 1)
                        if q % DOWN_TILES == DOWN_TILES - 1:
                            half = q // DOWN_TILES
                            used(l, g, n)
                            add_to_x(half, 4 - 4 * half)
                    dve.wait_ge(sem["hi_done"], tiles_before(l, g, N_FFN + GROUP_TILES)[0] + 1)
                    nc.vector.tensor_tensor(wlo[0][:, :], raw[0][:, :], whi[0][:, :].bitcast(F32), ALU.subtract)\
                        .then_inc(sem["lo_done"], 1)

            def diff2(out, a, hi, name, wait, value):
                dve.wait_ge(sem[wait], value)
                nc.vector.tensor_tensor(out, a, hi.bitcast(F32), ALU.subtract).then_inc(sem[name], 1)

            def split2(n):
                t = MIX2_T0 + n
                diff2(wlo[t % 2], raw[t % 2], whi[t % 2], "lo_done", "hi_done", t + 1)

            def used2(n):
                dve.wait_ge(sem["tile_used"], MIX2_T0 + n + 3)

            V = nc.vector
            dve.drain()
            dve.wait_ge(sem["p2_in"], 16)
            logit = p2[:, P2_LOGIT:P2_LOGIT + 2 * RET_HEADS]
            V.scalar_tensor_tensor(out=decay_lg[:, 0, :], in0=logit, scalar=-1.0, in1=logit, op0=ALU.mult, op1=ALU.max).then_inc(sem["sg_in"], 1)
            V.tensor_tensor(mods[:, :], mods[:, :], p2[:, P2_B:P2_B + 6 * DK], ALU.add)
            dve.drain()
            for sc, g0 in ((SCALE_M, P2_PRE), (SCALE_F, P2_FPRE)):
                V.scalar_tensor_tensor(out=mods[:, sc:sc + DK], in0=mods[:, sc:sc + DK], scalar=1.0, in1=p2[:, g0:g0 + DK],
                                       op0=ALU.add, op1=ALU.mult)
            for gt, g0 in ((GATE_M, P2_POST), (GATE_F, P2_FPOST)):
                V.tensor_tensor(mods[:, gt:gt + DK], mods[:, gt:gt + DK], p2[:, g0:g0 + DK], ALU.mult)
            dve.drain()
            for r, gt in enumerate((GATE_M, GATE_F)):
                for k in range(DK):
                    last = V.tensor_scalar(diag[:, r * DK + k, :], ident, mods[:, gt + k:gt + k + 1], None, ALU.mult)
            last.then_inc(sem["diag_done"], 1)
            dve.wait_ge(sem["nrt"], 5)
            V.reciprocal(stats[:, 8:12], stats[:, 4:8])
            dve.drain()
            dve.wait_ge(sem["fn_in"], 16)
            for i in range(TC):
                last = V.scalar_tensor_tensor(out=x[:, i, :], in0=x[:, i, :], scalar=stats[:, 8 + i:9 + i], in1=fnrow[:, :],
                                              op0=ALU.mult, op1=ALU.mult)
            last.then_inc(sem["xf_done"], 1)
            dve.wait_ge(sem["sg_exp"], 1)
            y, z, z2, ac = (decay_lg[:, r, :] for r in (1, 2, 3, 4))
            V.tensor_scalar(z, y, 2.0, None, ALU.add)
            dve.drain()
            V.reciprocal(z, z)
            dve.drain()
            V.tensor_tensor(z, z, y, ALU.mult)
            dve.drain()
            V.tensor_tensor(z2, z, z, ALU.mult)
            dve.drain()
            V.tensor_scalar(ac, z2, 1.0 / 17.0, None, ALU.mult)
            for k in (15, 13, 11, 9, 7, 5, 3):
                dve.drain()
                V.scalar_tensor_tensor(out=ac, in0=ac, scalar=1.0 / k, in1=z2, op0=ALU.add, op1=ALU.mult)
            dve.drain()
            V.scalar_tensor_tensor(out=ac, in0=ac, scalar=1.0, in1=z, op0=ALU.add, op1=ALU.mult)
            V.tensor_scalar(decay_lg[:, 5, :], logit, 0.0, None, ALU.min)
            dve.drain()
            V.scalar_tensor_tensor(out=decay_lg[:, 6, :], in0=ac, scalar=-2.0, in1=decay_lg[:, 5, :], op0=ALU.mult, op1=ALU.add)
            dve.drain()
            V.tensor_scalar(decay_lg[:, 7, :], decay_lg[:, 6, :], -1.0, None, ALU.mult)
            dve.wait_ge(sem["nrt"], 6)
            V.reciprocal(stats[:, 8:12], stats[:, 4:8])
            dve.drain()
            dve.wait_ge(sem["rows_done"], 2)
            for i in range(TC):
                last = V.tensor_scalar(xh4[:, i, :], x[:, i, :], stats[:, 8 + i:9 + i], None, ALU.mult)
            last.then_inc(sem["xn_done"], 1)
            for k in range(DK):
                dve.wait_ge(sem["tr_done"], 4 * DK + k + 1)
                dve.drain()
                V.tensor_scalar(sm[:, k % 2, :], bank[k % 4][:, :], mods[:, SCALE_M + k:SCALE_M + k + 1],
                                mods[:, SHIFT_M + k:SHIFT_M + k + 1], ALU.mult, ALU.add).then_inc(sem["tmb"], 1)
                if k:
                    diff2(hTl[:, k - 1, :], sm[:, (k - 1) % 2, :], hTh[:, k - 1, :], "lob", "hib", k)
            diff2(hTl[:, DK - 1, :], sm[:, (DK - 1) % 2, :], hTh[:, DK - 1, :], "lob", "hib", DK)

            def table(h):
                dve.drain()
                V.tensor_scalar(tab[:, h % 2, :], delta, 0.0, decay_lg[:, 6, h:h + 1], ALU.max, ALU.mult)
                dve.drain()
                for a, b in ((0, S), (S, REL)):
                    V.tensor_scalar(junk[:, 0:b - a], delta[:, a:b], 0.0, decay_lg[:, 7, RET_HEADS + h:RET_HEADS + h + 1],
                                    ALU.min, ALU.mult)
                    dve.drain()
                    last = V.tensor_tensor(tab[:, h % 2, a:b], tab[:, h % 2, a:b], junk[:, 0:b - a], ALU.add)
                    dve.drain()
                dve.sem_inc(sem["e_arg"], 1)

            dve.wait_ge(sem["rel_in"], 16)
            for c in range(12):
                split2(c + 1)
                if c in (1, 2):
                    table(c - 1)
            for n in range(Q2["rv"], Q2["wo"]):
                split2(n + 1)
                if n == Q2["rg"] - 1 or n == Q2["wo"] - 1:
                    used2(n)
                    dst, name = (rvt, "rv_out") if n == Q2["rg"] - 1 else (avt, "av_out")
                    for i in range(TC):
                        V.tensor_copy(dst[:, i, :], bank[i][:, :]).then_inc(sem[name], 1)
            for h in range(RET_HEADS + 1):
                if h < RET_HEADS:
                    dve.wait_ge(sem["e_tab"], h + 1)
                    if h >= 2:
                        dve.wait_ge(sem["y_done"], h - 1)
                    for j in range(TC):
                        dve.wait_ge(sem["rs_done"], h * TC + j + 1)
                        V.tensor_tensor(decayed[h % 2][:, j, :], bank[4 + j % 2][:, :], tab[:, h % 2, rel_cols(j)], ALU.mult)\
                            .then_inc(sem["dec_done"], 1)
                    dve.drain()
                    dve.sem_inc(sem["tab_free"], 1)
                    if h + 2 < RET_HEADS:
                        table(h + 2)
                    if h + 2 == RET_HEADS:
                        V.scalar_tensor_tensor(out=delta, in0=delta, scalar=-1.0, in1=delta, op0=ALU.mult, op1=ALU.max).then_inc(sem["abs_done"], 1)
                if h >= 1:
                    b = bank[6 + (h - 1) % 2]
                    dve.wait_ge(sem["y_done"], h)
                    dve.drain()
                    for i in range(TC):
                        V.bn_stats(bst[:, i, :], b[:, i * P:(i + 1) * P])
                    dve.drain()
                    for i in range(TC):
                        last = V.bn_aggr(mv[:, i, :], bst[:, i, :])
                    last.then_inc(sem["gn_var"], 1)
                    dve.wait_ge(sem["gn_rt"], h)
                    V.reciprocal(gr[:, TC:2 * TC], gr[:, 0:TC])
                    dve.drain()
                    for i in range(TC):
                        last = V.tensor_scalar(cat[:, i, (h - 1) * RET_V:h * RET_V], b[:, i * P:(i + 1) * P], mv[:, i, 0:1],
                                               gr[:, TC + i:TC + i + 1], ALU.subtract, ALU.mult)
                    last.then_inc(sem["yn"], 1)
            for it in range(DIL_HEADS * TC + 2):
                if it < DIL_HEADS * TC:
                    h, i = it // TC, it % TC
                    if i == 0:
                        dve.wait_ge(sem["tab_ready"], h + 1)
                    dve.wait_ge(sem["s2_done"], it + 1)
                    if it >= 2:
                        dve.wait_ge(sem["p2_done"], it - 1)
                    V.tensor_tensor_reduce(out=sm[:, it % 2, :], in0=bank[it % 2][:, :], in1=tab[:, h % 2, rel_cols(i)],
                                           scale=1.0, scalar=-3e38, op0=ALU.add, op1=ALU.max, accum_out=ast2[:, 0, it:it + 1])
                    dve.drain()
                    V.tensor_scalar(ast2[:, 1, it:it + 1], ast2[:, 0, it:it + 1], -1.0, None, ALU.mult).then_inc(sem["nm2"], 1)
                    if i == TC - 1:
                        dve.sem_inc(sem["tab_free"], 1)
                if it >= 2:
                    c = it - 2
                    h, i = c // TC, c % TC
                    dve.wait_ge(sem["av2"], c + 1)
                    V.reciprocal(ast2[:, 3, c:c + 1], ast2[:, 2, c:c + 1])
                    dve.drain()
                    o0 = RET_HEADS * RET_V + h * DIL_DIM
                    V.tensor_scalar(cat[:, i, o0:o0 + DIL_DIM], bank[4 + c % 2][:, 0:DIL_DIM], ast2[:, 3, c:c + 1], None, ALU.mult)\
                        .then_inc(sem["a2_out"], 1)
            for k in range(DK):
                diff2(hTl[:, k, :], bank[6 + k % 2][:, :], hTh[:, k, :], "ml", "mh", k + 1)
            for n in range(Q2["wo"] + 1, MIX2_TILES + WO2_TILES):
                split2(n)
            dve.wait_ge(sem["post_ss"], 1)
            V.tensor_tensor(st2[:, 0:4], st2[:, 0:4], st2[:, 4:8], ALU.add).then_inc(sem["post_r"], 1)
            dve.wait_ge(sem["post_rt"], 1)
            V.reciprocal(st2[:, 8:12], st2[:, 4:8])
            dve.drain()
            for p in range(2 * TC):
                i, half = p % TC, p // TC
                if p >= 2:
                    dve.wait_ge(sem["x2_upd"], p - 1)
                V.scalar_tensor_tensor(out=sm[:, p % 2, :], in0=bank[p][:, :], scalar=st2[:, 8 + i:9 + i],
                                       in1=rows[:, 0, half * BANK:(half + 1) * BANK], op0=ALU.mult, op1=ALU.mult)\
                    .then_inc(sem["t_ready"], 1)
            dve.wait_ge(sem["nrt"], 7)
            V.reciprocal(stats[:, 8:12], stats[:, 4:8])
            dve.drain()
            for i in range(TC):
                last = V.tensor_scalar(hn[:, i, :], x[:, i, :], stats[:, 8 + i:9 + i], None, ALU.mult)
            last.then_inc(sem["h_done"], 1)

            def over(ap, n):
                return ap.rearrange("p (i a) -> p i a", a=1).broadcast_to([P, TC, n])

            lgt = bank[4][:, 0:TC * EXPERTS].rearrange("p (i e) -> p i e", e=EXPERTS)
            ex = rt_s[:, 0, :, :]
            dve.wait_ge(sem["lg_done"], 1)
            V.tensor_reduce(stats[:, 12:16], lgt, AX.X, ALU.max)
            dve.drain()
            V.tensor_tensor(ex, lgt, over(stats[:, 12:16], EXPERTS), ALU.subtract).then_inc(sem["lg_sh"], 1)
            dve.wait_ge(sem["lg_exp"], 1)
            V.tensor_reduce(stats[:, 16:20], ex, AX.X, ALU.add)
            dve.drain()
            V.reciprocal(stats[:, 20:24], stats[:, 16:20])
            dve.drain()
            V.tensor_tensor(aff[:, :, :], ex, over(stats[:, 20:24], EXPERTS), ALU.mult).then_inc(sem["aff_done"], 1)
            dve.wait_ge(sem["affT"], 1)
            V.tensor_copy(top, bank[5][0:EXPERTS, :])
            for r in range(CAPACITY // 8):
                dve.drain()
                V.max(top8[:, 8 * r:8 * r + 8], top)
                dve.drain()
                if r < CAPACITY // 8 - 1:
                    V.match_replace(top, top8[:, 8 * r:8 * r + 8], top, -1.0)
            V.tensor_scalar(dthr, const[0:EXPERTS, C_ID:C_ID + EXPERTS], top8[:, CAPACITY - 1:CAPACITY], None, ALU.mult)\
                .then_inc(sem["thr_d"], 1)
            ge = rt_s[:, 1:3, :, :]
            dve.wait_ge(sem["thr_bc"], 1)
            thr = bank[6][:, 0:EXPERTS].rearrange("p (a e) -> p a e", a=1).broadcast_to([P, TC, EXPERTS])
            V.tensor_tensor(ge[:, 0], aff[:, :, :], thr, ALU.is_gt)
            V.tensor_tensor(ge[:, 1], aff[:, :, :], thr, ALU.is_equal).then_inc(sem["ge_done"], 1)
            dve.wait_ge(sem["pre_done"], 1)
            before = bank[7][:, 0:2 * TC * EXPERTS].rearrange("p (w i e) -> p w i e", w=2, i=TC)
            total = bank[7][:, 2 * TC * EXPERTS:2 * TC * EXPERTS + EXPERTS]
            need = stats[:, 24:24 + EXPERTS]
            V.tensor_scalar(need, total, -1.0, float(CAPACITY), ALU.mult, ALU.add)
            dve.drain()
            need4 = need.rearrange("p (a e) -> p a e", a=1).broadcast_to([P, TC, EXPERTS])
            V.tensor_tensor(rt_s[:, 3], before[:, 1], need4, ALU.is_lt)
            V.tensor_tensor(rt_s[:, 4], before[:, 1], need4, ALU.min)
            dve.drain()
            V.tensor_tensor(rt_s[:, 3], rt_s[:, 3], ge[:, 1], ALU.mult)
            V.tensor_tensor(rt_s[:, 4], before[:, 0], rt_s[:, 4], ALU.add)
            dve.drain()
            V.tensor_tensor(rt_s[:, 3], rt_s[:, 3], ge[:, 0], ALU.add)
            dve.drain()
            V.scalar_tensor_tensor(out=rt_s[:, 5], in0=rt_s[:, 4], scalar=1.0, in1=rt_s[:, 3], op0=ALU.add, op1=ALU.mult)
            dve.drain()
            by_e = lambda t: t[:, 0:EXPERTS * TC].rearrange("p (e i) -> p i e", i=TC)
            V.tensor_scalar(by_e(slots), rt_s[:, 5], 1.0, None, ALU.subtract)
            V.tensor_copy(by_e(affe), aff[:, :, :])
            V.memset(slots[:, EXPERTS * TC:], -1.0)
            V.memset(affe[:, EXPERTS * TC:], 0.0)
            V.memset(sgt[:, :], 0.0)
            dve.drain()

            def look_up(at):
                V.tensor_copy(cur[:, 0, :], slots[:, bass.ds(at * TC, TC)])
                V.tensor_copy(cur[:, 1, :], affe[:, bass.ds(at * TC, TC)])
                dve.drain()
                V.tensor_tensor(g2[:, :, :], const[:, C_IOTA:C_IOTA + P].rearrange("p (a n) -> p a n", a=1).broadcast_to([P, TC, P]),
                                over(cur[:, 0, :], P), ALU.is_equal).then_inc(sem["g2_ready"], 1)

            h3 = lambda ap: ap.rearrange("p (k t) -> p k t", t=64)

            def modulate(value):
                cols = lambda c: mods[:, c:c + DK].rearrange("p (k a) -> p k a", a=1).broadcast_to([P, DK, 64])
                dve.drain()
                dve.wait_ge(sem["gat_done"], value)
                V.tensor_tensor(h3(hf[:, :]), h3(bank[7][:, :]), cols(SCALE_F), ALU.mult)
                dve.drain()
                V.tensor_tensor(h3(hf[:, :]), h3(hf[:, :]), cols(SHIFT_F), ALU.add).then_inc(sem["gmod"], 1)

            def x_lo(value):
                dve.wait_ge(sem["xhi"], value)
                V.tensor_tensor(xTe[:, :, 64:128], h3(hf[:, :]), xTe[:, :, 0:64].bitcast(F32), ALU.subtract)\
                    .then_inc(sem["xlo"], 1)

            look_up(0)
            modulate(1)
            x_lo(1)
            dve.sem_inc(sem["moe_lo"], RAW_RING)
            with dve.Fori(0, EXPERTS) as e:
                def gather_add(which):
                    dve.wait_ge(sem["sc_done"], e * 2 + which + 1)
                    for i, b in enumerate((7, 6, 4, 5)):
                        part = acc[:, i, which * BANK:(which + 1) * BANK]
                        last = V.tensor_tensor(part, bank[b][:, :], part, ALU.add)
                    last.then_inc(sem["sc_add"], 1)

                for n in range(E_TILES):
                    s = n % RAW_RING
                    dve.wait_ge(sem["moe_hi"], e * E_TILES + n + 2)
                    V.tensor_tensor(moe_lo[n % SPLIT_RING], moe_raw[s][:, :], moe_hi[n % SPLIT_RING][:, :].bitcast(F32),
                                    ALU.subtract).then_inc(sem["moe_lo"], 1)
                    if n == 4:
                        gather_add(0)
                    elif n == 6:
                        gather_add(1)
                    elif n == 9:
                        dve.wait_ge(sem["sg_ready"], e + 1)
                        dve.wait_ge(sem["gg_ready"], e + 1)
                        look_up(e + 1)
                    elif n in (12, 20):
                        r = 0 if n == 12 else 1
                        dve.drain()
                        dve.wait_ge(sem["silu_m"], e * 2 + r + 1)
                        dve.wait_ge(sem["t_jobs"], e * 4 + 2 * r + 2)
                        V.tensor_tensor(hf[:, :], sgl[:, :], bank[7 - r][:, :], ALU.mult).then_inc(sem["hf_m"], 1)
                    if n in (13, 20):
                        r = 0 if n == 13 else 1
                        dve.wait_ge(sem["hhi"], e * 2 + r + 1)
                        V.tensor_tensor(hTe[:, 8 * r:8 * r + 8, 64:128], h3(hf[:, :]), hTe[:, 8 * r:8 * r + 8, 0:64].bitcast(F32),
                                        ALU.subtract).then_inc(sem["hlo"], 1)
                    if n == 18:
                        modulate(e + 2)
                    if n == 19:
                        x_lo(e + 2)
            for which in range(2):
                dve.wait_ge(sem["sc_done"], EXPERTS * 2 + which + 1)
                for i, b in enumerate((7, 6, 4, 5)):
                    part = acc[:, i, which * BANK:(which + 1) * BANK]
                    last = V.tensor_tensor(part, bank[b][:, :], part, ALU.add)
                last.then_inc(sem["sc_add"], 1)
            dve.wait_ge(sem["fin_ss"], 1)
            V.reciprocal(stats[:, 8:12], stats[:, 4:8])
            dve.drain()
            for i in range(TC):
                V.scalar_tensor_tensor(out=acc[:, i, :], in0=acc[:, i, :], scalar=stats[:, 8 + i:9 + i], in1=rows[:, 1, :],
                                       op0=ALU.mult, op1=ALU.mult)
                dve.drain()
                V.tensor_tensor(x[:, i, :], x[:, i, :], acc[:, i, :], ALU.add).then_inc(sem["fin_out"], 1)

        @block.gpsimd
        def _(pool):
            pool.dma_start(cbc[:, :], A["c"].broadcast_to([P, D])).then_inc(sem["cbc_in"], 16)
            pool.dma_start(trig[64:96, 0, :].bitcast(I32), A["positions"].broadcast_to([ROPE, S])).then_inc(sem["pos_in"], 16)
            with pool.Fori(0, LAYERS) as l:
                pool.wait_ge(sem["params_free"], l + 1)
                pool.dma_start(param[:, :], A["params"][bass.ds(l, 1)].rearrange("a p n -> p (a n)"))\
                    .then_inc(sem["params_in"], 16)
                pool.wait_ge(sem["v_out"], l * TC + TC)
                nc.gpsimd.tensor_tensor(vsq, vz, vz, ALU.mult).then_inc(sem["vsq_done"], 1)
                nc.gpsimd.memset(hp[:, :, 0:PAD], 0.0)
                nc.gpsimd.memset(hp[:, :, PAD + S:], 0.0)
                pool.drain()
                pool.wait_ge(sem["proj_out"], l * 10 + 2)
                nc.gpsimd.tensor_tensor(s2[:, :, 1:], hp[:, :, 0:W2 - 1], hp[:, :, 1:], ALU.add)
                pool.drain()
                nc.gpsimd.tensor_tensor(s4[:, :, 2:W2 - 1], s2[:, :, 1:W2 - 2], s2[:, :, 3:], ALU.add)
                pool.drain()
                nc.gpsimd.tensor_tensor(s8[:, 4:W2 - 3], s4[:, 1, 2:W2 - 5], s4[:, 1, 6:W2 - 1], ALU.add)
                pool.drain()
                lo, hi = slice(0, 64), slice(64, 128)
                cnt = const[:, C_CNT:C_CNT + 2 * S].rearrange("p (c t) -> p c t", c=2)
                mid = slice(PAD, PAD + S)
                pool.wait_ge(sem["const_in"], 16)
                nc.gpsimd.tensor_tensor(pooled[hi, 1, :], s8[hi, PAD - 4:PAD - 4 + S], s8[hi, PAD + 4:PAD + 4 + S], ALU.add)
                nc.gpsimd.tensor_tensor(pooled[lo, 0, :], s2[lo, 0, mid], cnt[lo, 0, :], ALU.mult)
                nc.gpsimd.tensor_tensor(pooled[hi, 0, :], s4[hi, 0, mid], cnt[hi, 0, :], ALU.mult)
                nc.gpsimd.tensor_tensor(pooled[lo, 1, :], s8[lo, mid], cnt[lo, 1, :], ALU.mult)
                pool.drain()
                nc.gpsimd.tensor_tensor(pooled[hi, 1, :], pooled[hi, 1, :], cnt[hi, 1, :], ALU.mult)
                pool.drain()
                nc.gpsimd.tensor_tensor(pooled, pooled, hp[:, :, mid], ALU.subtract).then_inc(sem["pool_ready"], 1)
                with pool.Fori(0, GROUPS) as g:
                    for j in range(ADA_PER_GROUP):
                        t = (l * GROUPS + g) * ADA_PER_GROUP + j
                        pool.wait_ge(sem["ada_used"], t + 1)
                        pool.dma_start(ada[:, :, :], A["ada"][bass.ds(t, 1)].rearrange("a p (r d) -> p (a r) d", r=2))\
                            .then_inc(sem["ada_in"], 16)

            pool.wait_ge(sem["x_upd"], LAYERS * 24 + 1)
            pool.dma_start(p2[:, :], A["params2"]).then_inc(sem["p2_in"], 16)
            pool.dma_start(fnrow[:, :], A["final_norm"].rearrange("(a d) -> a d", a=1).broadcast_to([P, D])).then_inc(sem["fn_in"], 16)
            pool.dma_start(rel[:, :], A["rel"]).then_inc(sem["rel_in"], 16)
            pool.wait_ge(sem["rg_out"], TC)
            for h in range(RET_HEADS):
                c = slice(h * RET_V, (h + 1) * RET_V)
                pool.wait_ge(sem["yn"], h + 1)
                nc.gpsimd.tensor_tensor(cat[:, :, c], cat[:, :, c], rgt[:, :, c], ALU.mult).then_inc(sem["ret_out"], 1)
                if h == 2:
                    pool.wait_ge(sem["abs_done"], 1)
            for h in range(DIL_HEADS):
                pool.wait_ge(sem["tab_free"], RET_HEADS + h - 1)
                slope = 2.0 ** (-8.0 * (h + 1) / DIL_HEADS)
                pool.drain()
                nc.gpsimd.tensor_scalar(tab[:, h % 2, :], delta, -slope, 0.0, ALU.mult, ALU.add)
                pool.drain()
                nc.gpsimd.tensor_tensor(tab[:, h % 2, :], tab[:, h % 2, :], lnm, ALU.add).then_inc(sem["tab_ready"], 1)
            pool.wait_ge(sem["a2_out"], DIL_HEADS * TC)
            pool.wait_ge(sem["ct_done"], DK)
            pool.sem_inc(sem["moe_free"], 1)
            for p in range(2 * TC):
                part = x[:, p % TC, (p // TC) * BANK:(p // TC + 1) * BANK]
                pool.wait_ge(sem["t_ready"], p + 1)
                nc.gpsimd.tensor_tensor(part, part, sm[:, p % 2, :], ALU.add).then_inc(sem["x2_upd"], 1)
            pool.wait_ge(sem["nrt"], 7)
            pool.dma_start(wr[:, :, :], A["w_router"].rearrange("(k p) e -> p k e", p=P)).then_inc(sem["wr_in"], 16)
            pool.wait_ge(sem["lg_done"], 1)
            nc.gpsimd.memset(acc[:, :, :], 0.0).then_inc(sem["acc_zero"], 1)

            def gates(value):
                pool.wait_ge(sem["g2_ready"], value)
                nc.gpsimd.tensor_tensor(gg2[:, :, :], g2[:, :, :],
                                        cur[:, 1, :].rearrange("p (i a) -> p i a", a=1).broadcast_to([P, TC, P]), ALU.mult)\
                    .then_inc(sem["gg_ready"], 1)

            gates(1)
            with pool.Fori(0, EXPERTS) as e:
                pool.wait_ge(sem["sgT"], e + 1)
                gates(e + 2)

        @block.tensor
        def _(pe):
            def mm3(out, stat, mov, start, stop):
                nc.tensor.matmul(out, stat[0], mov[0], start=start, stop=False)
                nc.tensor.matmul(out, stat[0], mov[1], start=False, stop=False)
                return nc.tensor.matmul(out, stat[1], mov[0], start=False, stop=stop)

            def arrived(l, g, n):
                pe.wait_ge(sem["lo_done"], tiles_before(l, g, n)[0] + 3)

            def w(n, a, b):
                return whi[n % 2][:, a:b], wlo[n % 2][:, a:b]

            def h(k, a=0, b=S):
                return hTh[:, k, a:b], hTl[:, k, a:b]

            def norm_T(nn, ready):
                pe.wait_ge(sem["xn_done"], ready)
                for k in range(DK):
                    if k >= 4:
                        pe.wait_ge(sem["hn_lo"], nn * DK + k - 3)
                    for i in range(TC):
                        last = nc.tensor.transpose(bank[k % 4][:, i * P:(i + 1) * P], xn4[:, i, k * P:(k + 1) * P], ident)
                    last.then_inc(sem["tr_done"], 1)

            pe.wait_ge(sem["const_in"], 16)
            pe.sem_inc(sem["tile_used"], 2)
            with pe.Fori(0, LAYERS) as l:
                norm_T(l * 2, l * 2 + 1)
                pe.wait_ge(sem["hn_lo"], l * 16 + 8)
                for n in (0, 1):
                    arrived(l, 0, n)
                    for kk in range(4):
                        k = 4 * n + kk
                        for i in range(TC):
                            last = mm3(bank[i][:, 0:SG_WIDTH], h(k, i * P, (i + 1) * P),
                                       w(n, kk * SG_WIDTH, (kk + 1) * SG_WIDTH), k == 0, k == DK - 1)
                    last.then_inc(sem["tile_used"], 1)
                for n in range(N_POOL, N_UQ):
                    c = n - N_POOL
                    arrived(l, 0, n)
                    if c >= 4:
                        pe.wait_ge(sem["proj_out"], l * 10 + c - 3)
                    for k in range(DK):
                        last = mm3(bank[4 + c % 4][:, :], w(n, k * P, (k + 1) * P), h(k), k == 0, k == DK - 1)
                    last.then_inc(sem["tile_used"], 1)
                    if n == N_KR:
                        pe.wait_ge(sem["v_out"], l * TC + TC)
                        pe.wait_ge(sem["proj_out"], l * 10 + 7)
                        for b, c0, c1 in ((0, 0, QC), (1, QC, QC + KVC)):
                            for cc in range(c0, c1):
                                last = nc.tensor.matmul(bank[b][:, :], ones, csq[:, cc, :], start=cc == c0, stop=cc == c1 - 1)
                            last.then_inc(sem["ssq_done"], 1)
                pe.wait_ge(sem["pool_ready"], l + 1)
                for c in range(2):
                    nc.tensor.matmul(bank[2 + c][:, :], wp_bd[:, c, :], pooled[:, c, :], start=True, stop=True)\
                        .then_inc(sem["pmm_done"], 1)
                pe.wait_ge(sem["vn_ready"], l + 1)
                pe.wait_ge(sem["rt_done"], l * 3 + 3)
                for c in range(2):
                    for i in range(TC):
                        for gg in range(2):
                            hd = 2 * c + gg
                            last = nc.tensor.matmul(bank[c][gg * 64:(gg + 1) * 64, i * P:(i + 1) * P],
                                                    vn[:, i, hd * SG_DIM:(hd + 1) * SG_DIM], wsT[:, hd, :],
                                                    start=True, stop=True)
                    last.then_inc(sem["sg_done"], 1)

                def rot(hd):
                    vec = qT[0:QK, hd, :] if hd < HEADS else krw[0:QK, :]
                    pe.wait_ge(sem["q_raw"], l * 8 + min(hd, HEADS - 1) + 1)
                    if hd >= 2:
                        pe.wait_ge(sem["q_rope"], l * 9 + hd - 1)
                    nc.tensor.matmul(bank[6 + hd % 2][64:96, :], const[0:QK, C_ROT:C_ROT + ROPE], vec, start=True, stop=True)\
                        .then_inc(sem["rot_done"], 1)

                pe.wait_ge(sem["proj_out"], l * 10 + 10)
                pe.wait_ge(sem["c_lo"], l * 5 + QC)
                for hd in range(HEADS):
                    n = N_UQ + hd // 2
                    if hd % 2 == 0:
                        arrived(l, 0, n)
                    if hd >= 2:
                        pe.wait_ge(sem["q_raw"], l * 8 + hd - 1)
                    for k in range(QC):
                        a = ((hd % 2) * QC + k) * QK
                        last = mm3(bank[4 + hd % 2][0:QK, :], w(n, a, a + QK), (ch[:, k, :], cl[:, k, :]), k == 0, k == QC - 1)
                    last.then_inc(sem["tile_used" if hd % 2 else "qe_done"], 1)
                    if hd:
                        rot(hd - 1)
                rot(HEADS - 1)
                rot(HEADS)
                pe.wait_ge(sem["mix_lo"], l * 8 + 4)
                pe.wait_ge(sem["c_lo"], l * 5 + QC + KVC)
                arrived(l, 0, N_UK)
                for j in range(HEADS // 2):
                    for k in range(KVC):
                        a = k * BANK + j * P
                        last = mm3(bank[j][:, :], w(N_UK, a, a + P), (ch[:, QC + k, :], cl[:, QC + k, :]), k == 0, k == KVC - 1)
                    last.then_inc(sem["k_done" if j < 3 else "tile_used"], 1)
                arrived(l, 0, N_UV)
                pe.wait_ge(sem["q_raw"], l * 8 + 8)
                pe.wait_ge(sem["q_rope"], l * 9 + 9)
                for i in range(TC):
                    for k in range(KVC):
                        last = mm3(bank[4 + i][:, :], (ch[:, QC + k, i * P:(i + 1) * P], cl[:, QC + k, i * P:(i + 1) * P]),
                                   w(N_UV, k * BANK, (k + 1) * BANK), k == 0, k == KVC - 1)
                last.then_inc(sem["tile_used"], 1)
                pe.wait_ge(sem["k_out"], l * 4 + 4)
                pe.wait_ge(sem["v2_out"], l * 4 + 4)
                N_IT = HEADS * TC
                for it in range(-1, N_IT + 1):
                    if it + 1 < N_IT:
                        e = it + 1
                        hd, i = e // TC, e % TC
                        if e >= 2:
                            pe.wait_ge(sem["p_done"], l * 32 + e - 1)
                        nc.tensor.matmul(bank[e % 2][:, :], qT[0:QK, hd, i * P:(i + 1) * P], kT[0:QK, hd, :],
                                         start=True, stop=True).then_inc(sem["s_done"], 1)
                    if 0 <= it < N_IT:
                        pe.wait_ge(sem["p_done"], l * 32 + it + 1)
                        if it >= 2:
                            pe.wait_ge(sem["pts_done"], l * 32 + it - 1)
                        for kc in range(TC):
                            last = nc.tensor.transpose(bank[2 + it % 2][:, kc * P:(kc + 1) * P],
                                                       prob[it % 2][:, kc * P:(kc + 1) * P], ident)
                        last.then_inc(sem["tr2_done"], 1)
                    if it >= 1:
                        e = it - 1
                        hd = e // TC
                        pe.wait_ge(sem["pts_done"], l * 32 + e + 1)
                        if e >= 2:
                            pe.wait_ge(sem["a_out"], l * 32 + e - 1)
                        for kc in range(TC):
                            last = nc.tensor.matmul(bank[4 + e % 2][:, 0:VDIM], probT[e % 2][:, kc * P:(kc + 1) * P],
                                                    vt[:, kc, hd * VDIM:(hd + 1) * VDIM], start=kc == 0, stop=kc == TC - 1)
                        last.then_inc(sem["av_done"], 1)
                pe.wait_ge(sem["a_out"], l * 32 + 32)
                for k in range(4):
                    if k >= 2:
                        pe.wait_ge(sem["mix_lo"], l * 8 + 3 + k)
                    for i in range(TC):
                        last = nc.tensor.transpose(bank[6 + k % 2][:, i * P:(i + 1) * P], att[:, i, k * P:(k + 1) * P], ident)
                    last.then_inc(sem["at_done"], 1)
                pe.wait_ge(sem["mix_lo"], l * 8 + 8)
                for half in range(2):
                    for q in range(4):
                        n = N_WO + 4 * half + q
                        arrived(l, 0, n)
                        for kk in range(2):
                            k = 2 * q + kk
                            for i in range(TC):
                                last = mm3(bank[4 * half + i][:, :], h(k, i * P, (i + 1) * P),
                                           w(n, kk * BANK, (kk + 1) * BANK), k == 0, k == DK - 1)
                        last.then_inc(sem["tile_used"], 1)
                norm_T(l * 2 + 1, l * 2 + 2)
                with pe.Fori(0, GROUPS) as g:
                    pe.wait_ge(sem["hn_lo"], l * 16 + 16)
                    lg = l * GROUPS + g
                    pe.wait_ge(sem["x_upd"], l * 24 + g * 8 + 9)
                    for j in range(FG):
                        for up in range(2):
                            n = N_FFN + 2 * j + up
                            arrived(l, g, n)
                            if j >= 2:
                                pe.wait_ge(sem["fr_done"], lg * FG + j - 1)
                            for k in range(DK):
                                last = mm3(bank[2 * (j % 2) + up][:, :], w(n, k * P, (k + 1) * P), h(k), k == 0, k == DK - 1)
                            last.then_inc(sem["tile_used"], 1)
                    pe.wait_ge(sem["flo"], lg * FG + FG)
                    for half in range(2):
                        for q in range(DOWN_TILES):
                            n = N_FFN + 2 * FG + half * DOWN_TILES + q
                            arrived(l, g, n)
                            for ff in range(min(2, FG - 2 * q)):
                                f = 2 * q + ff
                                for i in range(TC):
                                    last = mm3(bank[4 - 4 * half + i][:, :], (fTh[:, f, i * P:(i + 1) * P], fTl[:, f, i * P:(i + 1) * P]),
                                               w(n, ff * BANK, (ff + 1) * BANK), f == 0, f == FG - 1)
                            last.then_inc(sem["tile_used"], 1)

            def arrived2(n):
                pe.wait_ge(sem["lo_done"], MIX2_T0 + n + 3)

            def w2(n, a, b):
                t = (MIX2_T0 + n) % 2
                return whi[t][:, a:b], wlo[t][:, a:b]

            pe.wait_ge(sem["diag_done"], 1)
            for r in range(2):
                for k in range(DK):
                    last = nc.tensor.matmul(bank[4 + 2 * r + k // 4][:, (k % 4) * P:(k % 4 + 1) * P], ones, diag[:, r * DK + k, :],
                                            start=True, stop=True)
                last.then_inc(sem["rows_done"], 1)
            pe.wait_ge(sem["xn_done"], 5)
            for k in range(DK):
                if k >= 4:
                    pe.wait_ge(sem["tmb"], k - 3)
                for i in range(TC):
                    last = nc.tensor.transpose(bank[k % 4][:, i * P:(i + 1) * P], xh4[:, i, k * P:(k + 1) * P], ident)
                last.then_inc(sem["tr_done"], 1)
            pe.wait_ge(sem["lob"], DK)
            pe.wait_ge(sem["rows_out"], 4)
            for c in range(12):
                arrived2(c)
                if c >= 4:
                    pe.wait_ge(sem["pj2"], c - 3)
                for k in range(DK):
                    last = mm3(bank[4 + c % 4][:, :], w2(c, k * P, (k + 1) * P), h(k), k == 0, k == DK - 1)
                last.then_inc(sem["tile_used"], 1)

            def by_token(n0, b0, hT):
                for q in range(4):
                    arrived2(n0 + q)
                    for kk in range(2):
                        k = 2 * q + kk
                        for i in range(TC):
                            last = mm3(bank[b0 + i][:, :], hT(k, i * P, (i + 1) * P), w2(n0 + q, kk * BANK, (kk + 1) * BANK),
                                       k == 0, k == DK - 1)
                    last.then_inc(sem["tile_used"], 1)

            by_token(Q2["rv"], 0, h)
            pe.wait_ge(sem["pj2"], 12)
            by_token(Q2["rg"], 4, h)
            pe.wait_ge(sem["rv_out"], TC)
            by_token(Q2["av"], 0, h)
            pe.wait_ge(sem["rg_out"], TC)
            for hd in range(RET_HEADS + 1):
                if hd < RET_HEADS:
                    r = slice(64 * (hd % 2), 64 * (hd % 2) + 64)
                    for j in range(TC):
                        if hd or j >= 2:
                            pe.wait_ge(sem["dec_done"], hd * TC + j - 1)
                        nc.tensor.matmul(bank[4 + j % 2][:, :], rqk[r, 2 + hd // 2, j * P:(j + 1) * P], rqk[r, hd // 2, :],
                                         start=True, stop=True).then_inc(sem["rs_done"], 1)
                if hd:
                    g = hd - 1
                    pe.wait_ge(sem["dec_done"], hd * TC)
                    if g >= 2:
                        pe.wait_ge(sem["yn"], g - 1)
                    for i in range(TC):
                        for j in range(TC):
                            last = nc.tensor.matmul(bank[6 + g % 2][:, i * P:(i + 1) * P], decayed[g % 2][:, j, i * P:(i + 1) * P],
                                                    rvt[:, j, g * RET_V:(g + 1) * RET_V], start=j == 0, stop=j == TC - 1)
                    last.then_inc(sem["y_done"], 1)
            pe.wait_ge(sem["av_out"], TC)
            pe.wait_ge(sem["dec_done"], RET_HEADS * TC)
            N_IT = DIL_HEADS * TC
            for it in range(-1, N_IT + 1):
                if it + 1 < N_IT:
                    c = it + 1
                    hd, i = c // TC, c % TC
                    r = slice(64 * (hd % 2), 64 * (hd % 2) + 64)
                    if c >= 2:
                        pe.wait_ge(sem["nm2"], c - 1)
                    nc.tensor.matmul(bank[c % 2][:, :], aqk[r, hd // 2, i * P:(i + 1) * P], aqk[r, 4 + hd // 2, :],
                                     start=True, stop=True).then_inc(sem["s2_done"], 1)
                if 0 <= it < N_IT:
                    pe.wait_ge(sem["p2_done"], it + 1)
                    if it >= 2:
                        pe.wait_ge(sem["pts2"], it - 1)
                    for kc in range(TC):
                        last = nc.tensor.transpose(bank[2 + it % 2][:, kc * P:(kc + 1) * P],
                                                   prob2[it % 2][:, kc * P:(kc + 1) * P], ident)
                    last.then_inc(sem["tr3"], 1)
                if it >= 1:
                    c = it - 1
                    hd = c // TC
                    pe.wait_ge(sem["pts2"], c + 1)
                    if c >= 2:
                        pe.wait_ge(sem["a2_out"], c - 1)
                    for kc in range(TC):
                        last = nc.tensor.matmul(bank[4 + c % 2][:, 0:DIL_DIM], probT2[c % 2][:, kc * P:(kc + 1) * P],
                                                avt[:, kc, hd * DIL_DIM:(hd + 1) * DIL_DIM], start=kc == 0, stop=kc == TC - 1)
                    last.then_inc(sem["av2"], 1)
            pe.wait_ge(sem["a2_out"], N_IT)
            pe.wait_ge(sem["ret_out"], RET_HEADS)
            for k in range(DK):
                if k >= 2:
                    pe.wait_ge(sem["ml"], k - 1)
                for i in range(TC):
                    last = nc.tensor.transpose(bank[6 + k % 2][:, i * P:(i + 1) * P], cat[:, i, k * P:(k + 1) * P], ident)
                last.then_inc(sem["ct_done"], 1)
            pe.wait_ge(sem["ml"], DK)
            by_token(Q2["wo"], 0, h)
            by_token(Q2["wo"] + 4, 4, h)
            pe.wait_ge(sem["h_done"], 1)
            for k in range(DK):
                if k >= 4:
                    pe.wait_ge(sem["hT_out"], k - 3)
                for i in range(TC):
                    last = nc.tensor.transpose(bank[k % 4][:, i * P:(i + 1) * P], hn[:, i, k * P:(k + 1) * P], ident)
                last.then_inc(sem["hT_done"], 1)
            pe.wait_ge(sem["hT_out"], DK)
            pe.wait_ge(sem["wr_in"], 16)
            for i in range(TC):
                for k in range(DK):
                    last = nc.tensor.matmul(bank[4][:, i * EXPERTS:(i + 1) * EXPERTS], hTf[:, k, i * P:(i + 1) * P], wr[:, k, :],
                                            start=k == 0, stop=k == DK - 1)
            last.then_inc(sem["lg_done"], 1)
            pe.wait_ge(sem["aff_done"], 1)
            for i in range(TC):
                last = nc.tensor.transpose(bank[5][0:EXPERTS, i * P:(i + 1) * P], aff[:, i, :], ident)
            last.then_inc(sem["affT"], 1)
            pe.wait_ge(sem["thr_d"], 1)
            nc.tensor.matmul(bank[6][:, 0:EXPERTS], const[0:EXPERTS, C_ONE:C_ONE + P], dthr, start=True, stop=True)\
                .then_inc(sem["thr_bc"], 1)
            pe.wait_ge(sem["ge_done"], 1)
            for wh in range(2):
                for i in range(TC):
                    for j in range(i + 1):
                        nc.tensor.matmul(bank[7][:, (wh * TC + i) * EXPERTS:(wh * TC + i + 1) * EXPERTS],
                                         ones if j < i else const[:, C_TRI:C_TRI + P], rt_s[:, 1 + wh, j, :], start=j == 0, stop=j == i)
            for j in range(TC):
                last = nc.tensor.matmul(bank[7][:, 2 * TC * EXPERTS:2 * TC * EXPERTS + EXPERTS], ones, rt_s[:, 1, j, :],
                                        start=j == 0, stop=j == TC - 1)
            last.then_inc(sem["pre_done"], 1)

            def gather(value):
                pe.wait_ge(sem["g2_ready"], value)
                for k in range(DK):
                    for i in range(TC):
                        last = nc.tensor.matmul(bank[7][:, k * 64:(k + 1) * 64], hn[:, i, k * P:(k + 1) * P], g2[:, i, 0:64],
                                                start=i == 0, stop=i == TC - 1)
                last.then_inc(sem["gat_done"], 1)

            def scatter(which):
                for i, b in enumerate((7, 6, 4, 5)):
                    last = nc.tensor.matmul(bank[b][:, :], sgt[:, i * P:(i + 1) * P], ysb[:, which * BANK:(which + 1) * BANK],
                                            start=True, stop=True)
                last.then_inc(sem["sc_done"], 1)

            gather(1)
            pe.wait_ge(sem["acc_zero"], 1)
            pe.sem_inc(sem["moe_used"], SPLIT_RING)
            with pe.Fori(0, EXPERTS) as e:
                pe.wait_ge(sem["xlo"], e + 1)
                for n in range(E_TILES):
                    s = n % SPLIT_RING
                    pe.wait_ge(sem["moe_lo"], e * E_TILES + n + 1 + RAW_RING)
                    if n == 8:
                        pe.wait_ge(sem["unit_out"], e * 5 + 3)
                    elif n == 12:
                        pe.wait_ge(sem["unit_out"], e * 5 + 4)
                    elif n == 16:
                        pe.wait_ge(sem["hlo"], e * 2 + 1)
                    elif n == 20:
                        pe.wait_ge(sem["hlo"], e * 2 + 2)
                    elif n == 0:
                        pe.wait_ge(sem["unit_out"], e * 5 + 1)
                    b0 = (0, 2, 0, 2, 4, 4)[n // 4]
                    for c in range(2):
                        k = 2 * (n % 4) + c if n < 16 else 2 * (n - 16) + c
                        first, final = k == 0, k == (DK if n < 16 else 2 * DK) - 1
                        stat = xTe[:, k, :] if n < 16 else hTe[:, k, :]
                        for part in (moe_hi[s][:, :], moe_lo[s]):
                            for b in range(2):
                                a = c * D + b * BANK
                                is_hi = part is not moe_lo[s]
                                last = nc.tensor.matmul(bank[b0 + b][:, :], stat, part[:, a:a + BANK],
                                                        start=first and is_hi, stop=final and not is_hi)
                    last.then_inc(sem["moe_used"], 1)
                    if n == 2:
                        pe.wait_ge(sem["unit_out"], e * 5 + 2)
                        scatter(0)
                    elif n == 4:
                        pe.wait_ge(sem["sc_add"], e * 2 + 1)
                        scatter(1)
                    elif n == 5:
                        pe.wait_ge(sem["gg_ready"], e + 1)
                        pe.wait_ge(sem["sc_add"], e * 2 + 2)
                        for i in range(TC):
                            last = nc.tensor.transpose(bank[7][:, i * P:(i + 1) * P], gg2[:, i, :], ident)
                        last.then_inc(sem["sgT"], 1)
                    elif n in (6, 10, 14, 18):
                        u = (6, 10, 14, 18).index(n)
                        pe.wait_ge(sem["unit_out"], e * 5 + 3 + u)
                        if u == 0:
                            pe.wait_ge(sem["sc_add"], e * 2 + 2)
                        elif u == 1:
                            pe.wait_ge(sem["sg_ready"], e + 1)
                        elif u == 2:
                            pe.wait_ge(sem["silu_m"], e * 2 + 1)
                        else:
                            pe.wait_ge(sem["silu_m"], e * 2 + 2)
                        for j in range(8):
                            last = nc.tensor.matmul(bank[7 if u == 1 else 6][:, j * 64:(j + 1) * 64],
                                                    asb[:, u % 2, j * P:(j + 1) * P], const[:, C_I2:C_I2 + 64], start=True, stop=True)
                        last.then_inc(sem["t_jobs"], 1)
                    elif n == 16:
                        pe.wait_ge(sem["hf_m"], e * 2 + 1)
                        gather(e + 2)
            for which in range(2):
                pe.wait_ge(sem["unit_out"], EXPERTS * 5 + 2)
                if which:
                    pe.wait_ge(sem["sc_add"], EXPERTS * 2 + 1)
                scatter(which)


def _chunks(w, cols):
    import numpy as np
    k = w.shape[0] // P
    return np.ascontiguousarray(w.reshape(k, P, cols).transpose(1, 0, 2).reshape(P, k * cols))


def _tiles(a):
    import numpy as np
    out = np.zeros((N_TILES, P, TILE), np.float32)
    o1, o2 = Q_LORA, Q_LORA + KV_LORA
    o3 = o2 + ROPE
    o4 = o3 + 256
    o5 = o4 + SG_WIDTH
    for l in range(LAYERS):
        w_in, w_o, w_uq, w_ukv = a["w_in"][l], a["w_o"][l], a["w_uq"][l], a["w_ukv"][l]
        t0 = l * LAYER_TILES

        def put(n, block):
            out[t0 + n, :, 0:block.shape[1]] = block

        for q in range(2):
            put(N_V + q, _chunks(w_in[q * 512:(q + 1) * 512, o5:], SG_WIDTH))
            put(N_POOL + q, _chunks(w_in[:, o3 + q * P:o3 + (q + 1) * P], P))
            put(N_U + q, _chunks(w_in[:, o4 + q * P:o4 + (q + 1) * P], P))
            put(N_KV + q, _chunks(w_in[:, o1 + q * P:o1 + (q + 1) * P], P))
        for q in range(QC):
            put(N_Q + q, _chunks(w_in[:, q * P:(q + 1) * P], P))
        put(N_KR, _chunks(w_in[:, o2 - 64:o2 + 64], P))
        for m in range(HEADS // 2):
            put(N_UQ + m, np.concatenate([_chunks(w_uq[:, hd * QK:(hd + 1) * QK], QK) for hd in (2 * m, 2 * m + 1)], axis=1))
        kv = w_ukv.reshape(KV_LORA, HEADS, NOPE + VDIM)
        put(N_UK, _chunks(kv[:, :, :NOPE].reshape(KV_LORA, -1), BANK))
        put(N_UV, _chunks(kv[:, :, NOPE:].reshape(KV_LORA, -1), BANK))
        for half in range(2):
            cols = slice(half * BANK, (half + 1) * BANK)
            for q in range(4):
                put(N_WO + 4 * half + q, _chunks(w_o[q * 256:(q + 1) * 256, cols], BANK))
        for g in range(GROUPS):
            g0 = N_FFN + g * GROUP_TILES
            for j in range(FG):
                f = g * FG + j
                put(g0 + 2 * j, _chunks(a["w_gate"][l][:, f * P:(f + 1) * P], P))
                put(g0 + 2 * j + 1, _chunks(a["w_up"][l][:, f * P:(f + 1) * P], P))
            for half in range(2):
                for q in range(DOWN_TILES):
                    r0 = (g * FG + 2 * q) * P
                    r1 = min(r0 + 2 * P, (g + 1) * FG * P)
                    put(g0 + 2 * FG + half * DOWN_TILES + q,
                        _chunks(a["w_down"][l][r0:r1, half * BANK:(half + 1) * BANK], BANK))
    w = a["w_in_2"][0]
    for n in range(12):
        c0 = n * P if n < 4 else 1536 + (n - 4) * P
        out[MIX2_T0 + n] = _chunks(w[:, c0:c0 + P], P)
    for name, c0 in (("rv", 512), ("rg", 1024), ("av", 2560)):
        for q in range(4):
            out[MIX2_T0 + Q2[name] + q] = _chunks(w[q * 256:(q + 1) * 256, c0:c0 + BANK], BANK)
    for half in range(2):
        for q in range(4):
            out[MIX2_T0 + Q2["wo"] + 4 * half + q] = _chunks(a["w_out_2"][0][q * 256:(q + 1) * 256, half * BANK:(half + 1) * BANK], BANK)
    return out


def _params(a):
    import numpy as np
    out = np.zeros((LAYERS, P, N_PARAM), np.float32)
    for l in range(LAYERS):
        p = out[l]
        for off, v in ((G_MIX, a["mix_norm"][l]), (G_FFN, a["ffn_norm"][l]), (G_Q, a["q_norm"][l]), (G_KV, a["kv_norm"][l]),
                       (G_PS, a["pool_scale"][l])):
            p[:, off:off + v.size // P] = v.reshape(-1, P).T
        for c in range(2):
            p[:, PR_BS + c * P:PR_BS + (c + 1) * P] = np.repeat(a["b_s"][l][2 * c:2 * c + 2], 64, axis=0)
            for q in range(2):
                p[q * 64:(q + 1) * 64, PR_WP + c * P + q * 64:PR_WP + c * P + (q + 1) * 64] = a["w_pool"][l][2 * c + q]
        p[:, PR_SG:PR_WS] = a["sg_norm"][l][None, :]
        p[:, PR_WS:PR_WP] = a["w_s"][l].transpose(2, 0, 1).reshape(P, -1)
    return out


def _const():
    import numpy as np
    c = np.zeros((P, N_CONST), np.float32)
    c[:, C_ID:C_ID + P] = np.eye(P)
    c[:, C_ONE:C_ONE + P] = 1.0
    t = np.arange(S)
    for g, wdw in enumerate(POOL_WINDOWS):
        left = wdw // 2
        n = np.clip(t + wdw - left, 0, S) - np.clip(t - left, 0, S)
        r = slice((g % 2) * 64, (g % 2) * 64 + 64)
        c[r, C_CNT + (g // 2) * S:C_CNT + (g // 2 + 1) * S] = (1.0 / n.astype(np.float32))[None, :]
    half = ROPE // 2
    for j in range(half):
        c[64 + half + j, C_ROT + j] = -1.0
        c[64 + j, C_ROT + half + j] = 1.0
    freq = (np.float32(10000.0) ** (-np.arange(0, ROPE, 2, dtype=np.float32) / np.float32(ROPE))).astype(np.float32)
    c[64:96, C_FREQ] = np.concatenate([freq, freq])
    c[:, C_TRI:C_TRI + P] = np.triu(np.ones((P, P)), 1)
    c[:, C_IOTA:C_IOTA + P] = (np.arange(P) % 64)[None, :]
    c[:, C_I2:C_I2 + 64] = (np.arange(P)[:, None] % 64) == np.arange(64)[None, :]
    c[:, C_EPS] = EPS
    c[:, C_GEPS] = GN_EPS
    return c


def _ada(w_ada):
    import numpy as np
    return np.ascontiguousarray(w_ada.T.reshape(ADA_TILES, 2, P, D).transpose(0, 2, 1, 3).reshape(ADA_TILES, P, 2 * D))


def _params2(a):
    import numpy as np
    out = np.zeros((P, N_P2), np.float32)
    for off, name in ((P2_PRE, "g_pre_mix_2"), (P2_POST, "g_post_mix_2"), (P2_FPRE, "g_pre_ffn_2"), (P2_FPOST, "g_post_ffn_2"),
                      (P2_B, "b_ada_2")):
        v = a[name][0]
        out[:, off:off + v.size // P] = v.reshape(-1, P).T
    out[:, P2_LOGIT:P2_LOGIT + RET_HEADS] = a["ret_decay_fwd_2"][0][None, :]
    out[:, P2_LOGIT + RET_HEADS:] = a["ret_decay_bwd_2"][0][None, :]
    return out


def _rel():
    import numpy as np
    d = np.arange(REL)[None, :] - REL0 - np.arange(P)[:, None]
    many = sum(((d % dil == 0) & (abs(d) <= win // 2)).astype(np.float64) for win, dil in DIL_CONFIGS)
    lnm = np.where(many > 0, np.log(np.maximum(many, 1.0)), MASKED)
    return np.concatenate([d, lnm], axis=1).astype(np.float32)


def arrays_of(inputs):
    import numpy as np
    a = {k: np.asarray(v) for k, v in inputs.items()}
    return {
        "x": a["x"], "positions": a["positions"], "c": a["c_2"], "const": _const(), "tiles": _tiles(a), "params": _params(a),
        "ada": _ada(a["w_ada_2"][0]), "params2": _params2(a), "rel": _rel(), "final_norm": a["final_norm"],
        "w_router": a["w_router_2"][0], "w_gate": a["w_gate_e_2"][0], "w_up": a["w_up_e_2"][0], "w_down": a["w_down_e_2"][0],
    }


def kernel(**inputs):
    import concourse.bacc as _bacc
    from concourse.bass_utils import run_bass_kernel_spmd as _run

    nc = _bacc.Bacc("TRN2", target_bir_lowering=False, num_devices=1)
    arrays = arrays_of(inputs)
    A = {k: nc.dram_tensor(f"in_{k}", v.shape, mybir.dt.from_np(v.dtype), kind="ExternalInput").ap() for k, v in arrays.items()}
    A["out"] = nc.dram_tensor("out_x", (1, S, D), F32, kind="ExternalOutput").ap()
    build(nc, A)
    r = _run(nc, [{f"in_{k}": v for k, v in arrays.items()}], core_ids=[0])
    return r.results[0]["out_x"]
```

```python
from contextlib import ExitStack

import concourse.bass as bass
from concourse import mybir

F32 = mybir.dt.float32
F32R = mybir.dt.float32r
I32 = mybir.dt.int32
ALU = mybir.AluOpType
ACT = mybir.ActivationFunctionType
AX = mybir.AxisListType

P = 128
S = 512
TC = S // P
D = 1024
DK = D // P
BANK = 512
EPS = 1e-6
GN_EPS = 1e-5

LAYERS = 2
HEADS, NOPE, ROPE, VDIM = 8, 64, 32, 64
QK = NOPE + ROPE
Q_LORA, KV_LORA = 384, 256
QC, KVC = Q_LORA // P, KV_LORA // P
ATT_SCALE = float(QK) ** -0.5
POOL_WINDOWS = (2, 4, 8, 16)
PAD = max(POOL_WINDOWS)
SG_HEADS, SG_DIM = 4, 64
SG_WIDTH = SG_HEADS * SG_DIM
D_FF = 2816
FF_CHUNKS = D_FF // P
GROUPS = 2
FG = FF_CHUNKS // GROUPS

TILE = 1024
N_V, N_POOL, N_Q, N_KV, N_KR, N_U = 0, 2, 4, 7, 9, 10
N_UQ, N_UK, N_UV, N_WO = 12, 16, 17, 18
N_FFN = 26
DOWN_TILES = -(-FG // 2)
GROUP_TILES = 2 * FG + 2 * DOWN_TILES
LAYER_TILES = N_FFN + GROUPS * GROUP_TILES
MIX2_T0 = LAYERS * LAYER_TILES
MIX2_TILES = 24
WO2_TILES = 8
N_TILES = MIX2_T0 + MIX2_TILES + WO2_TILES
UQ_W = 2 * QC * QK

ADA_TILES = 6 * D // (2 * P)
ADA_PER_GROUP = ADA_TILES // (LAYERS * GROUPS)

G_MIX, G_FFN, G_Q, G_KV, G_PS = 0, DK, 2 * DK, 2 * DK + QC, 2 * DK + QC + KVC
N_GAIN = G_PS + 2
PR_BS = N_GAIN + (N_GAIN % 2)
PR_SG = PR_BS + 2 * P
PR_WS = PR_SG + SG_WIDTH
PR_WP = PR_WS + SG_HEADS * P
N_PARAM = PR_WP + 2 * P

C_ID, C_ONE, C_ROT, C_FREQ = 0, P, 2 * P, 2 * P + ROPE
C_TRI = C_FREQ + 1
C_IOTA = C_TRI + P
C_I2 = C_IOTA + P
C_EPS = C_I2 + 64
C_GEPS = C_EPS + 1
N_CONST = C_GEPS + 1

RET_HEADS, RET_QK, RET_V = 4, 64, 128
DIL_HEADS, DIL_DIM = 8, 64
DIL_CONFIGS = ((128, 1), (512, 4), (2048, 16))
MASKED = -1e30
REL = 2 * S - P
REL0 = S - P
EXPERTS, CAPACITY, D_EXP = 16, 2 * S // 16, 2048
Q2 = {"rqk": 0, "rv": 4, "aqk": 8, "rg": 16, "av": 20, "wo": 24}
CAT_ORDER = (4, 5, 6, 7, 0, 1, 2, 3)
Y_BANK = (0, 1, 0, 6)
P2_PRE, P2_POST, P2_FPRE, P2_FPOST = 0, DK, 2 * DK, 3 * DK
P2_B = 4 * DK
P2_LOGIT = P2_B + 6 * DK
N_P2 = P2_LOGIT + 2 * RET_HEADS
SHIFT_M, SCALE_M, GATE_M, SHIFT_F, SCALE_F, GATE_F = (j * DK for j in range(6))

MT = 2 * D
E_TILES = 24
RAW_RING, SPLIT_RING = 6, 3
HALF_F = D_EXP // 2

TWO_PI = 6.283185307179586
PI2_A = 6.28125
PI2_B = 0.0019350051879882812
PI2_C = TWO_PI - PI2_A - PI2_B
MAGIC = 12582912.0
PI_IN = 3.1415925


def build(nc, A):
    ctx = ExitStack()
    with ctx:
        def sb(name, shape, dt=F32, where=None):
            return (where or ctx).enter_context(nc.sbuf_tensor(name, shape, dt))

        names = (
            "const_in x_in counts_in cbc_in cos_done raw_in0 raw_in1 hi_done lo_done tile_used params_in params_free pos_in trig_arg trig_done "
            "ada_in ada_used silu_c x_upd nrt xn_done tr_done hn_hi hn_lo v_out vsq_done vss_done proj_out ssq_done rt_done "
            "cn_done c_hi c_lo vn_ready pool_ready pmm_done sg_done sgr mix_hi mix_lo qe_done q_raw rot_done q_rope "
            "k_done k_out v2_out s_done nm_done p_done tr2_done pts_done av_done a_out at_done silu_done fr_done fhi flo "
            "out_done p2_in fn_in rel_in diag_done rows_done rows_out sg_in sg_exp xf_done tmb hib lob rt2 pj2 rv_out rg_out av_out "
            "e_arg e_tab tab_free abs_done tab_ready rs_done dec_done y_done gn_var gn_rt yn ret_out s2_done nm2 p2_done tr3 "
            "pts2 av2 a2_out ct_done mh ml post_ss post_rt post_r t_ready x2_upd h_done hT_done hT_out wr_in lg_done lg_sh back_done h_out h_split "
            "lg_exp aff_done affT thr_d thr_bc ge_done pre_done route_done "
            "moe_hi moe_lo moe_used y_out gate_out up_out gate_t up_t sc_done sc_add sgT sg_ready silu_m hf_m hhi hlo g2_ready gg_ready gat_done "
            "gat_out x_turned x_done acc_zero moe_free fin_ss fin_out"
        ).split()
        names += [f"moe_in{i}" for i in range(RAW_RING)]
        sem = {n: ctx.enter_context(nc.semaphore(n)) for n in names}
        bank = [ctx.enter_context(nc.psum_tensor(f"bank{i}", [P, BANK], F32)) for i in range(8)]

        const = sb("const", [P, N_CONST])
        ident, ones = const[:, C_ID:C_ID + P], const[:, C_ONE:C_ONE + P]
        x = sb("x", [P, TC, D])
        hTh, hTl = sb("hTh", [P, DK, S], F32R), sb("hTl", [P, DK, S], F32R)
        raw_t, whi_t, wlo_t = sb("raw_t", [P, MT]), sb("whi_t", [P, MT], F32R), sb("wlo_t", [P, MT], F32R)
        raw, whi, wlo = ([t[:, i * TILE:(i + 1) * TILE] for i in range(2)] for t in (raw_t, whi_t, wlo_t))
        junk = sb("junk", [P, D])
        stats = sb("stats", [P, 64])
        mods = sb("mods", [P, 6 * DK])

        b1 = ExitStack()
        param = sb("param", [P, N_PARAM], where=b1)
        trig = sb("trig", [P, 2, S], where=b1)
        ada = sb("ada", [P, 2, D], where=b1)
        cbc = sb("cbc", [P, D], where=b1)
        ada_sum = sb("ada_sum", [P, 2 * ADA_PER_GROUP], where=b1)
        cnt = sb("cnt", [P, 2, S], where=b1)
        vstat = sb("vstat", [P, 3, TC * SG_HEADS], where=b1)
        astat = sb("astat", [P, 4, HEADS * TC], where=b1)
        xn = sb("xn", [P, TC * D], where=b1)
        with ExitStack() as mix_scope:
            craw = sb("craw", [P, QC + KVC, S], where=mix_scope)
            ch = sb("ch", [P, QC + KVC, S], F32R, where=mix_scope)
            cl = sb("cl", [P, QC + KVC, S], F32R, where=mix_scope)
            rbc = sb("rbc", [P, 2, S], where=mix_scope)
            qk = sb("qk", [P, 2 * HEADS * S], where=mix_scope)
            vt = sb("vt", [P, TC, HEADS * VDIM], where=mix_scope)
            uT = sb("uT", [P, 2, S], where=mix_scope)
            krw = sb("krw", [P, S], where=mix_scope)
        with ExitStack() as ffn_scope:
            fTh = sb("fTh", [P, FG, S], F32R, where=ffn_scope)
            fTl = sb("fTl", [P, FG, S], F32R, where=ffn_scope)
            sgr = sb("sgr_t", [P, 2, S], where=ffn_scope)
            fr = sb("fr", [P, 2, S], where=ffn_scope)
        b1.close()
        rows = sb("rows", [P, 2, D])
        with ExitStack() as b2:
            rqk = sb("rqk", [P, 4, S], where=b2)
            aqk = sb("aqk", [P, 8, S], where=b2)
            avt = sb("avt", [P, TC, S], where=b2)
            rvt = sb("rvt", [P, TC, S], where=b2)
            rgt = sb("rgt", [P, TC, S], where=b2)
            xh2 = sb("xh2", [P, TC * D], where=b2)
            cat = sb("cat", [P, TC, D], where=b2)
            tab = sb("tab", [P, 2, REL], where=b2)
            rel = sb("rel", [P, 2 * REL], where=b2)
            sm = sb("sm", [P, 2, S], where=b2)
            prob2_t = sb("prob2", [P, 4, S], where=b2)
            fnrow = sb("fnrow", [P, D], where=b2)
            p2 = sb("p2", [P, N_P2], where=b2)
            decay_lg = sb("decay_lg", [P, 8, 2 * RET_HEADS], where=b2)
            gn = sb("gn", [P, TC * 6 + TC * 2 + 2 * TC], where=b2)
            ast2 = sb("ast2", [P, 4, DIL_HEADS * TC], where=b2)
            st2 = sb("st2", [P, 16], where=b2)
        with ExitStack() as b3:
            moe_raw = [sb(f"mraw{i}", [P, MT], where=b3) for i in range(RAW_RING - 1)] + [raw_t]
            h_hi = [sb(f"h_hi{i}", [P, D], F32R, where=b3) for i in range(TC)]
            h_lo = [sb(f"h_lo{i}", [P, D], F32R, where=b3) for i in range(TC - 1)]
            acc = sb("acc", [P, TC, D], where=b3)
            moe_hi = [whi_t] + [sb(f"mhi{i}", [P, MT], F32R, where=b3) for i in range(SPLIT_RING - 1)]
            asb = sb("asb", [P, 2, HALF_F], where=b3)
            sgl = sb("sgl", [P, S], where=b3)
            hf = sb("hf", [P, S], where=b3)
            hot = sb("hot", [P, TC, 3 * 64], F32R, where=b3)
            gg2 = sb("gg2", [P, TC, P], where=b3)
            sgt = sb("sgt", [P, S], where=b3)
            aff = sb("aff", [P, TC, EXPERTS], where=b3)
            affe = sb("affe", [P, (EXPERTS + 1) * TC], where=b3)
            slots = sb("slots", [P, (EXPERTS + 1) * TC], where=b3)
            cur = sb("cur", [P, 2, TC], where=b3)
        hT_flat = hTh[:, :, :].rearrange("p k t -> p (k t)")
        lo_flat = hTl[:, :, :].rearrange("p k t -> p (k t)")
        xTe = hT_flat[:, 0:DK * P].rearrange("p (k t) -> p k t", t=P)
        hTe = hT_flat[:, DK * P:3 * DK * P].rearrange("p (k t) -> p k t", t=P)
        moe_lo = [wlo_t[:, :], lo_flat[:, 0:MT], lo_flat[:, MT:2 * MT]]
        h_lo.append(hT_flat[:, 3 * DK * P:4 * DK * P])
        ysb, gathered = rows[:, 0, :], junk
        hn = [asb[:, 0, :], asb[:, 1, :], ysb, junk[:, :]]
        wr = hf[:, 0:DK * EXPERTS].rearrange("p (k e) -> p k e", e=EXPERTS)
        rt_s = sgl[:, :].rearrange("p (r i e) -> p r i e", i=TC, e=EXPERTS)
        hTf = acc[:, :, :].rearrange("p i d -> p (i d)").rearrange("p (k t) -> p k t", t=S)
        top = ysb[0:EXPERTS, 0:S]
        top8 = ysb[0:EXPERTS, S:S + 64]
        dthr = ysb[0:EXPERTS, S + 64:S + 64 + EXPERTS]
        diag = xh2[:, 0:2 * DK * P].rearrange("p (k n) -> p k n", n=P)
        decayed = [xh2[:, r * TC * S:(r + 1) * TC * S].rearrange("p (j t) -> p j t", t=S) for r in range(2)]
        xh4 = xh2[:, :].rearrange("p (i d) -> p i d", i=TC)
        prob2 = [prob2_t[:, r, :] for r in range(2)]
        probT2 = [prob2_t[:, 2 + r, :] for r in range(2)]
        delta, lnm = rel[:, 0:REL], rel[:, REL:2 * REL]
        bst = gn[:, 0:6 * TC].rearrange("p (i s) -> p i s", s=6)
        mv = gn[:, 6 * TC:8 * TC].rearrange("p (i s) -> p i s", s=2)
        gr = gn[:, 8 * TC:10 * TC]

        ROUND = (("w_gate", 1, 0), ("w_up", 1, 0), ("w_down", 0, 0), ("w_gate", 0, 1), ("w_up", 0, 1), ("w_down", 1, 0))
        NEXT0, NEXT1 = 12, 20
        HEAD_TILES = NEXT1 - NEXT0
        SCATTER_BANKS = (4, 5, 6, 7)
        OPENING, LAST = -1, EXPERTS - 1

        def is_round(e, which):
            return type(e) is int and e == which

        def round_tile(e, n):
            if is_round(e, OPENING):
                return NEXT0 <= n < NEXT1, n - NEXT0, n - NEXT0
            if is_round(e, LAST):
                m = n if n < NEXT0 else n - HEAD_TILES
                return not NEXT0 <= n < NEXT1, HEAD_TILES + LAST * E_TILES + m, HEAD_TILES + m
            return True, HEAD_TILES + e * E_TILES + n, HEAD_TILES + n

        def rounds(eng, steps):
            steps(OPENING)
            with eng.Fori(0, LAST) as e:
                steps(e)
            steps(LAST)

        def by_feature(n):
            return n if n < Q2["rv"] else n - Q2["aqk"] + 4 if Q2["aqk"] <= n < Q2["rg"] else None

        def rel_cols(i):
            return slice(REL0 - i * P, REL0 - i * P + S)

        xn4 = xn[:, :].rearrange("p (i d) -> p i d", i=TC)
        csq = xn[:, 0:(QC + KVC) * S].rearrange("p (c t) -> p c t", t=S)
        prob = [xn[:, r * S:(r + 1) * S] for r in range(2)]
        probT = [xn[:, (2 + r) * S:(3 + r) * S] for r in range(2)]
        att = xn[:, 4 * S:8 * S].rearrange("p (i n) -> p i n", i=TC)
        qT = qk[:, 0:HEADS * S].rearrange("p (h t) -> p h t", t=S)
        kT = qk[:, HEADS * S:].rearrange("p (h t) -> p h t", t=S)
        W2 = S + 2 * PAD
        hp = qk[:, 0:2 * W2].rearrange("p (c t) -> p c t", c=2)
        s2 = qk[:, 2 * W2:4 * W2].rearrange("p (c t) -> p c t", c=2)
        s4 = qk[:, 4 * W2:6 * W2].rearrange("p (c t) -> p c t", c=2)
        s8 = qk[:, 6 * W2:7 * W2]
        o = 7 * W2
        pooled = qk[:, o:o + 2 * S].rearrange("p (c t) -> p c t", c=2)
        vz = qk[:, o + 2 * S:o + 4 * S].rearrange("p (i n) -> p i n", i=TC)
        vsq = qk[:, o + 4 * S:o + 6 * S].rearrange("p (i n) -> p i n", i=TC)
        assert o + 6 * S <= 2 * HEADS * S
        vn = junk[:, :].rearrange("p (i n) -> p i n", i=TC)
        wsT = param[:, PR_WS:PR_WP].rearrange("p (g n) -> p g n", g=SG_HEADS)
        wp_bd = param[:, PR_WP:N_PARAM].rearrange("p (c n) -> p c n", c=2)

        def gain(k):
            return param[:, k:k + 1]

        def tiles_before(l, g, n):
            return l * LAYER_TILES + g * GROUP_TILES + n, l * (LAYER_TILES // 2) + g * (GROUP_TILES // 2) + n // 2

        def tile_width(n):
            if N_UQ <= n < N_UK:
                return UQ_W
            if n >= N_FFN and (n - N_FFN) % GROUP_TILES >= 2 * FG:
                q = ((n - N_FFN) % GROUP_TILES - 2 * FG) % DOWN_TILES
                return min(2, FG - 2 * q) * BANK
            return TILE

        block = ctx.enter_context(nc.Block())

        @block.sync
        def _(sp):
            sp.dma_start(const[:, :], A["const"]).then_inc(sem["const_in"], 16)
            sp.dma_start(x[:, :, :], A["x"].rearrange("b (i p) d -> p (b i) d", p=P)).then_inc(sem["x_in"], 16)
            sp.dma_start(cnt[:, :, :], A["counts"]).then_inc(sem["counts_in"], 16)

            def load(l, g, n):
                before, pair = tiles_before(l, g, n)
                w = tile_width(n)
                sp.wait_ge(sem["lo_done"], before + 1)
                sp.dma_start(raw[n % 2][:, 0:w], A["tiles"][bass.ds(before, 1), :, 0:w].rearrange("a p n -> p (a n)"))\
                    .then_inc(sem[f"raw_in{n % 2}"], 16)

            with sp.Fori(0, LAYERS) as l:
                for n in range(N_FFN):
                    load(l, 0, n)
                with sp.Fori(0, GROUPS) as g:
                    for n in range(N_FFN, N_FFN + GROUP_TILES):
                        load(l, g, n)
            for t in range(MIX2_T0, N_TILES):
                sp.wait_ge(sem["lo_done"], t + 1)
                sp.dma_start(raw[t % 2], A["tiles"][t]).then_inc(sem[f"raw_in{t % 2}"], 16)
            sp.wait_ge(sem["moe_free"], 1)
            def expert_loads(e):
                for n in range(E_TILES):
                    there, before, c = round_tile(e, n)
                    if not there:
                        continue
                    sp.wait_ge(sem["moe_lo"], before + 1)
                    name, half, ahead = ROUND[n // 4]
                    q = n % 4 + (4 * half if name == "w_down" else 0)
                    rows_of = D_EXP if name == "w_down" else D
                    cols = slice(0, D) if name == "w_down" else slice(half * HALF_F, (half + 1) * HALF_F)
                    r0 = (e + ahead) * rows_of + q * 256
                    r = slice(r0, r0 + 256) if type(e) is int else bass.ds(r0, 256)
                    sp.dma_start(moe_raw[c % RAW_RING][:, :].rearrange("p (c f) -> p c f", c=2),
                                 A[name].rearrange("e k f -> (e k) f")[r, cols].rearrange("(c p) f -> p c f", p=P))\
                        .then_inc(sem[f"moe_in{c % RAW_RING}"], 16)

            rounds(sp, expert_loads)
            for i in range(TC):
                sp.wait_ge(sem["fin_out"], i + 1)
                sp.dma_start(A["out"][0, i * P:(i + 1) * P, :], x[:, i, :]).then_inc(sem["out_done"], 16)
            sp.wait_ge(sem["out_done"], 16 * TC)

        @block.scalar
        def _(act):
            def split(l, g, n):
                before, pair = tiles_before(l, g, n)
                s, w = n % 2, tile_width(n)
                act.wait_ge(sem[f"raw_in{s}"], (pair + 1) * 16)
                act.wait_ge(sem["tile_used"], before + 1)
                nc.scalar.activation(whi[s][:, 0:w], raw[s][:, 0:w], ACT.Copy).then_inc(sem["hi_done"], 1)

            def used(l, g, n):
                act.wait_ge(sem["tile_used"], tiles_before(l, g, n)[0] + 3)

            def norm_stats(nn):
                for i in range(TC):
                    if i:
                        act.drain()
                    nc.scalar.activation(junk[:, :], x[:, i, :], ACT.Square, accum_out=stats[:, i:i + 1])
                act.drain()
                nc.scalar.activation(stats[:, 4:8], stats[:, 0:4], ACT.Sqrt, scale=1.0 / D,
                                     bias=const[:, C_EPS:C_EPS + 1]).then_inc(sem["nrt"], 1)

            def norm_hi(nn, g0):
                for k in range(DK):
                    act.wait_ge(sem["tr_done"], nn * DK + k + 1)
                    nc.scalar.activation(hTh[:, k, :], bank[k % 4][:, :], ACT.Copy, scale=gain(g0 + k))\
                        .then_inc(sem["hn_hi"], 1)

            act.wait_ge(sem["const_in"], 16)
            act.wait_ge(sem["cbc_in"], 16)
            nc.scalar.activation(cbc[:, :], cbc[:, :], ACT.Silu).then_inc(sem["silu_c"], 1)
            act.wait_ge(sem["trig_arg"], 1)
            for r in range(2):
                last = nc.scalar.activation(trig[64:96, r, :], trig[64:96, r, :], ACT.Sin)
            last.then_inc(sem["trig_done"], 1)
            split(0, 0, 0)
            with act.Fori(0, LAYERS) as l:
                act.drain()
                act.wait_ge(sem["x_upd"], l * 24 + 1)
                norm_stats(l * 2)
                act.wait_ge(sem["params_in"], l * 16 + 16)
                norm_hi(l * 2, G_MIX)
                split(l, 0, 1)
                used(l, 0, 0)
                split(l, 0, 2)
                used(l, 0, 1)
                for i in range(TC):
                    nc.scalar.activation(vz[:, i, :], bank[i][:, 0:SG_WIDTH], ACT.Gelu_apprx_tanh).then_inc(sem["v_out"], 1)
                for n in range(N_POOL, N_UQ):
                    c = n - N_POOL
                    b = bank[4 + c % 4]
                    split(l, 0, n + 1)
                    if n == N_U:
                        act.wait_ge(sem["ssq_done"], l * 2 + 2)
                        nc.scalar.activation(rbc[:, 0, :], bank[0][:, :], ACT.Sqrt, scale=1.0 / Q_LORA,
                                             bias=const[:, C_EPS:C_EPS + 1]).then_inc(sem["rt_done"], 1)
                        nc.scalar.activation(rbc[:, 1, :], bank[1][:, :], ACT.Sqrt, scale=1.0 / KV_LORA,
                                             bias=const[:, C_EPS:C_EPS + 1]).then_inc(sem["rt_done"], 1)
                        act.wait_ge(sem["vss_done"], l + 1)
                        nc.scalar.activation(vstat[:, 1, :], vstat[:, 0, :], ACT.Sqrt, scale=1.0 / SG_DIM,
                                             bias=const[:, C_EPS:C_EPS + 1]).then_inc(sem["rt_done"], 1)
                    used(l, 0, n)
                    if n < N_Q:
                        nc.scalar.activation(hp[:, c, PAD:PAD + S], b[:, :], ACT.Copy).then_inc(sem["proj_out"], 1)
                    elif n < N_KR:
                        nc.scalar.activation(craw[:, n - N_Q, :], b[:, :], ACT.Copy)
                        nc.scalar.activation(csq[:, n - N_Q, :], b[:, :], ACT.Square).then_inc(sem["proj_out"], 1)
                    elif n < N_U:
                        nc.scalar.activation(krw[0:QK, :], b[0:QK, :], ACT.Copy).then_inc(sem["proj_out"], 1)
                    else:
                        nc.scalar.activation(uT[:, n - N_U, :], b[:, :], ACT.Gelu_apprx_tanh).then_inc(sem["proj_out"], 1)
                act.wait_ge(sem["cn_done"], l + 1)
                for c in range(QC + KVC):
                    nc.scalar.activation(ch[:, c, :], craw[:, c, :], ACT.Copy, scale=gain(G_Q + c)).then_inc(sem["c_hi"], 1)
                for c in range(2):
                    act.wait_ge(sem["pmm_done"], l * 2 + c + 1)
                    nc.scalar.activation(hTh[:, 4 + c, :], bank[2 + c][:, :], ACT.Copy, scale=gain(G_PS + c))\
                        .then_inc(sem["mix_hi"], 1)
                for c in range(2):
                    act.wait_ge(sem["sgr"], l * 2 + c + 1)
                    nc.scalar.activation(hTh[:, 6 + c, :], craw[:, c, :], ACT.Copy).then_inc(sem["mix_hi"], 1)
                for m in range(HEADS // 2):
                    split(l, 0, N_UQ + m + 1)
                    act.wait_ge(sem["qe_done"], l * 4 + m + 1)
                    nc.scalar.activation(qT[0:QK, 2 * m, :], bank[4][0:QK, :], ACT.Copy).then_inc(sem["q_raw"], 1)
                    used(l, 0, N_UQ + m)
                    nc.scalar.activation(qT[0:QK, 2 * m + 1, :], bank[5][0:QK, :], ACT.Copy).then_inc(sem["q_raw"], 1)
                split(l, 0, N_UV)
                for j in range(HEADS // 2):
                    if j < 3:
                        act.wait_ge(sem["k_done"], l * 3 + j + 1)
                    else:
                        used(l, 0, N_UK)
                    nc.scalar.activation(kT[0:NOPE, 2 * j, :], bank[j][0:64, :], ACT.Copy)
                    nc.scalar.activation(kT[0:NOPE, 2 * j + 1, :], bank[j][64:128, :], ACT.Copy).then_inc(sem["k_out"], 1)
                split(l, 0, N_WO)
                for it in range(HEADS * TC + 1):
                    if it < HEADS * TC:
                        act.wait_ge(sem["nm_done"], l * 32 + it + 1)
                        if it >= 2:
                            act.wait_ge(sem["tr2_done"], l * 32 + it - 1)
                        nc.scalar.activation(prob[it % 2], bank[it % 2][:, :], ACT.Exp, bias=astat[:, 1, it:it + 1],
                                             scale=ATT_SCALE, accum_out=astat[:, 2, it:it + 1]).then_inc(sem["p_done"], 1)
                    if it >= 1:
                        e = it - 1
                        act.wait_ge(sem["tr2_done"], l * 32 + e + 1)
                        if e >= 2:
                            act.wait_ge(sem["av_done"], l * 32 + e - 1)
                        nc.scalar.activation(probT[e % 2], bank[2 + e % 2][:, :], ACT.Copy).then_inc(sem["pts_done"], 1)
                for k in range(4):
                    act.wait_ge(sem["at_done"], l * 4 + k + 1)
                    nc.scalar.activation(hTh[:, k, :], bank[6 + k % 2][:, :], ACT.Copy).then_inc(sem["mix_hi"], 1)
                for n in range(N_WO, N_FFN):
                    split(l, 0, n + 1)
                act.drain()
                act.wait_ge(sem["x_upd"], l * 24 + 9)
                norm_stats(l * 2 + 1)
                norm_hi(l * 2 + 1, G_FFN)
                with act.Fori(0, GROUPS) as g:
                    for j in range(FG):
                        n = N_FFN + 2 * j
                        split(l, g, n + 1)
                        used(l, g, n)
                        nc.scalar.activation(sgr[:, j % 2, :], bank[2 * (j % 2)][:, :], ACT.Silu).then_inc(sem["silu_done"], 1)
                        split(l, g, n + 2)
                        act.wait_ge(sem["fr_done"], (l * GROUPS + g) * FG + j + 1)
                        nc.scalar.activation(fTh[:, j, :], fr[:, j % 2, :], ACT.Copy).then_inc(sem["fhi"], 1)
                    for q in range(2 * DOWN_TILES):
                        n = N_FFN + 2 * FG + q
                        if q < 2 * DOWN_TILES - 1:
                            split(l, g, n + 1)
                    before, pair = tiles_before(l, g, N_FFN + GROUP_TILES)
                    act.wait_ge(sem["raw_in0"], (pair + 1) * 16)
                    act.wait_ge(sem["tile_used"], before + 1)
                    nc.scalar.activation(whi[0][:, :], raw[0][:, :], ACT.Copy).then_inc(sem["hi_done"], 1)

            def copy2(out, in_, name, **kw):
                nc.scalar.activation(out, in_, kw.pop("func", ACT.Copy), **kw).then_inc(sem[name], 1)

            def split2(n):
                t = MIX2_T0 + n
                act.wait_ge(sem[f"raw_in{t % 2}"], (t // 2 + 1) * 16)
                act.wait_ge(sem["tile_used"], t + 1)
                copy2(whi[t % 2], raw[t % 2], "hi_done")

            def used2(n):
                act.wait_ge(sem["tile_used"], MIX2_T0 + n + 3)

            act.wait_ge(sem["sg_in"], 1)
            copy2(decay_lg[:, 1, :], decay_lg[:, 0, :], "sg_exp", func=ACT.Exp, scale=-1.0)
            act.drain()
            act.wait_ge(sem["x_upd"], LAYERS * 24 + 1)
            norm_stats(4)
            for b in range(4):
                act.wait_ge(sem["rows_done"], b // 2 + 1)
                copy2(rows[:, b // 2, (b % 2) * BANK:(b % 2 + 1) * BANK], bank[4 + b][:, :], "rows_out")
            act.drain()
            act.wait_ge(sem["xf_done"], 1)
            norm_stats(5)
            for k in range(DK):
                act.wait_ge(sem["tmb"], k + 1)
                copy2(hTh[:, k, :], sm[:, k % 2, :], "hib")

            def table(h):
                act.wait_ge(sem["e_arg"], h + 1)
                copy2(tab[:, h % 2, :], tab[:, h % 2, :], "e_tab", func=ACT.Exp)

            def group_norm_root(h):
                act.wait_ge(sem["gn_var"], h + 1)
                copy2(gr[:, 0:TC], mv[:, :, 1], "gn_rt", func=ACT.Sqrt, bias=const[:, C_GEPS:C_GEPS + 1])

            for n in range(Q2["wo"]):
                split2(n + 1)
                f = by_feature(n)
                if f is not None:
                    used2(n)
                    dst = rqk[:, f, :] if f < 4 else aqk[:, f - 4, :]
                    scale = 1.0 if f < 2 or f >= 8 else RET_QK ** -0.5 if f < 4 else DIL_DIM ** -0.5
                    copy2(dst, bank[4 + f % 2][:, :], "pj2", scale=scale)
                if n == 4:
                    table(0)
                    table(1)
                elif n == 12:
                    table(2)
                elif n == 13:
                    group_norm_root(0)
                elif n == 16:
                    table(3)
                elif n == 20:
                    used2(Q2["av"] - 1)
                    for i in range(TC):
                        copy2(rgt[:, i, :], bank[2 + i][:, :], "rg_out", func=ACT.Silu)
                    group_norm_root(1)
                elif n == 22:
                    group_norm_root(2)
            for it in range(DIL_HEADS * TC + 1):
                if it < DIL_HEADS * TC:
                    act.wait_ge(sem["nm2"], it + 1)
                    if it >= 2:
                        act.wait_ge(sem["tr3"], it - 1)
                    copy2(prob2[it % 2], sm[:, it % 2, :], "p2_done", func=ACT.Exp, bias=ast2[:, 1, it:it + 1],
                          accum_out=ast2[:, 2, it:it + 1])
                if it >= 1:
                    act.wait_ge(sem["tr3"], it)
                    if it >= 3:
                        act.wait_ge(sem["av2"], it - 2)
                    copy2(probT2[(it - 1) % 2], bank[2 + (it - 1) % 2][:, :], "pts2")
            group_norm_root(3)
            for c, k in enumerate(CAT_ORDER):
                act.wait_ge(sem["ct_done"], c + 1)
                copy2(hTh[:, k, :], bank[4 + c % 2][:, :], "mh")
            for half in range(2):
                for q in range(4):
                    n = Q2["wo"] + 4 * half + q
                    if n + 1 < MIX2_TILES + WO2_TILES:
                        split2(n + 1)
                used2(Q2["wo"] + 4 * half + 3)
                for i in range(TC):
                    act.drain()
                    last = nc.scalar.activation(junk[:, 0:BANK], bank[4 * half + i][:, :], ACT.Square,
                                                accum_out=st2[:, 4 * half + i:4 * half + i + 1])
            last.then_inc(sem["post_ss"], 1)
            act.wait_ge(sem["post_r"], 1)
            copy2(st2[:, 4:8], st2[:, 0:4], "post_rt", func=ACT.Sqrt, scale=1.0 / D, bias=const[:, C_EPS:C_EPS + 1])
            act.drain()
            act.wait_ge(sem["x2_upd"], 2 * TC)
            norm_stats(6)
            for k in range(DK):
                act.wait_ge(sem["hT_done"], k + 1)
                copy2(hTf[:, k, :], bank[k % 4][:, :], "hT_out", func=ACT.Identity, scale=mods[:, SCALE_F + k:SCALE_F + k + 1],
                      bias=mods[:, SHIFT_F + k:SHIFT_F + k + 1])
            act.wait_ge(sem["lg_sh"], 1)
            copy2(rt_s[:, 0, :, :], rt_s[:, 0, :, :], "lg_exp", func=ACT.Exp)

            for i in range(TC):
                act.wait_ge(sem["back_done"], i + 1)
                if i >= 2:
                    act.wait_ge(sem["h_split"], i - 1)
                for b in range(2):
                    c = slice(b * BANK, (b + 1) * BANK)
                    nc.scalar.activation(asb[:, i % 2, c], bank[2 * (i % 2) + b][:, :], ACT.Copy)
                    last = nc.scalar.activation(h_hi[i][:, c], bank[2 * (i % 2) + b][:, :], ACT.Copy)
                last.then_inc(sem["h_out"], 1)

            def stash_tokens(value):
                act.wait_ge(sem["gat_done"], value)
                for w in range(2):
                    last = nc.scalar.activation(gathered[:, w * BANK:(w + 1) * BANK], bank[2 + w][:, :], ACT.Copy)
                last.then_inc(sem["gat_out"], 1)
                act.drain()

            def new_tokens(value):
                act.wait_ge(sem["x_turned"], value)
                for b in range(2):
                    last = nc.scalar.activation(xTe[:, 4 * b:4 * b + 4, :], bank[b][:, :].rearrange("p (k t) -> p k t", t=P), ACT.Copy)
                last.then_inc(sem["x_done"], 1)

            def evac(dst, b0, name, used_tiles):
                act.wait_ge(sem["moe_used"], used_tiles + SPLIT_RING)
                for b in range(2):
                    last = nc.scalar.activation(dst[:, b * BANK:(b + 1) * BANK], bank[b0 + b][:, :], ACT.Copy)
                last.then_inc(sem[name], 1)

            def silu_gate(value):
                act.wait_ge(sem["gate_t"], value)
                copy2(sgl[:, :], bank[6][:, :], "silu_m", func=ACT.Silu)

            def h_high(r, value):
                act.wait_ge(sem["hf_m"], value)
                copy2(hTe[:, 8 * r:8 * r + 8, 0:64], hf[:, :].rearrange("p (k t) -> p k t", t=64), "hhi")

            def expert_hi(e):
                this, ahead = not is_round(e, OPENING), not is_round(e, LAST)
                for n in range(0 if this else NEXT0, E_TILES):
                    there, before, c = round_tile(e, n)
                    if there:
                        s = c % RAW_RING
                        in_before = c // RAW_RING + 1 + (0 if is_round(e, OPENING) else e * (E_TILES // RAW_RING))
                        act.wait_ge(sem[f"moe_in{s}"], in_before * 16)
                        act.wait_ge(sem["moe_used"], before + 1)
                        copy2(moe_hi[c % SPLIT_RING][:, :], moe_raw[s][:, :], "moe_hi")
                    if n == 2:
                        evac(ysb, 4, "y_out", HEAD_TILES + e * E_TILES)
                    elif n == 3:
                        if ahead:
                            stash_tokens(e + 2)
                    elif n == 4:
                        h_high(0, 2 * e + 1)
                    elif n == 6:
                        evac(asb[:, 0, :], 0, "gate_out", round_tile(e, 4)[1])
                    elif n == 10:
                        evac(asb[:, 1, :], 2, "up_out", round_tile(e, 8)[1])
                        if ahead:
                            new_tokens(e + 2)
                    elif n == 13 and this:
                        silu_gate(2 * e + 2)
                    elif n == 16 and this:
                        h_high(1, 2 * e + 2)
                    elif n == 18:
                        if this:
                            act.wait_ge(sem["sgT"], e + 1)
                            copy2(sgt[:, :], bank[7][:, :], "sg_ready")
                        if ahead:
                            evac(asb[:, 0, :], 0, "gate_out", round_tile(e, 16)[1])
                    elif n == 21 and ahead:
                        silu_gate(2 * e + 3)
                    elif n == 22 and ahead:
                        evac(asb[:, 1, :], 2, "up_out", round_tile(e, 19)[1] + 1)

            stash_tokens(1)
            new_tokens(1)
            rounds(act, expert_hi)
            evac(ysb, 4, "y_out", EXPERTS * E_TILES)
            act.wait_ge(sem["sc_add"], 2 * EXPERTS + 2)
            for i in range(TC):
                act.drain()
                nc.scalar.activation(asb[:, 0, :], acc[:, i, :], ACT.Square, accum_out=stats[:, i:i + 1])
            act.drain()
            copy2(stats[:, 4:8], stats[:, 0:4], "fin_ss", func=ACT.Sqrt, scale=1.0 / D, bias=const[:, C_EPS:C_EPS + 1])

        @block.vector
        def _(dve):
            def split(l, g, n):
                before, _ = tiles_before(l, g, n)
                s, w = n % 2, tile_width(n)
                dve.wait_ge(sem["hi_done"], before + 1)
                nc.vector.tensor_tensor(wlo[s][:, 0:w], raw[s][:, 0:w], whi[s][:, 0:w].bitcast(F32), ALU.subtract)\
                    .then_inc(sem["lo_done"], 1)

            def used(l, g, n):
                dve.wait_ge(sem["tile_used"], tiles_before(l, g, n)[0] + 3)

            def norm_scale(nn):
                dve.wait_ge(sem["nrt"], nn + 1)
                nc.vector.reciprocal(stats[:, 8:12], stats[:, 4:8])
                dve.drain()
                for i in range(TC):
                    last = nc.vector.tensor_scalar(xn4[:, i, :], x[:, i, :], stats[:, 8 + i:9 + i], None, ALU.mult)
                last.then_inc(sem["xn_done"], 1)

            def norm_lo(nn, g0):
                for k in range(DK):
                    dve.wait_ge(sem["hn_hi"], nn * DK + k + 1)
                    nc.vector.scalar_tensor_tensor(out=hTl[:, k, :], in0=bank[k % 4][:, :], scalar=gain(g0 + k),
                                                   in1=hTh[:, k, :].bitcast(F32), op0=ALU.mult, op1=ALU.subtract)\
                        .then_inc(sem["hn_lo"], 1)

            dve.sem_inc(sem["lo_done"], 2)
            dve.wait_ge(sem["x_in"], 16)
            dve.sem_inc(sem["x_upd"], 1)
            dve.sem_inc(sem["params_free"], 1)
            dve.sem_inc(sem["ada_used"], 1)
            dve.wait_ge(sem["pos_in"], 16)
            dve.wait_ge(sem["const_in"], 16)
            R = slice(64, 96)
            ang, turns, t2 = xn[R, 0:S], xn[R, S:2 * S], xn[R, 2 * S:3 * S]
            nc.vector.tensor_copy(ang, trig[R, 0, :].bitcast(I32))
            dve.drain()
            nc.vector.tensor_scalar(ang, ang, const[R, C_FREQ:C_FREQ + 1], None, ALU.mult)
            for r, quarter in ((0, 0.25), (1, 0.0)):
                dve.drain()
                nc.vector.tensor_scalar(turns, ang, 1.0 / TWO_PI, quarter, ALU.mult, ALU.add)
                dve.drain()
                nc.vector.tensor_scalar(turns, turns, MAGIC, None, ALU.add)
                dve.drain()
                nc.vector.tensor_scalar(turns, turns, MAGIC, None, ALU.subtract)
                dve.drain()
                nc.vector.scalar_tensor_tensor(out=t2, in0=turns, scalar=-PI2_A, in1=ang, op0=ALU.mult, op1=ALU.add)
                for part in (PI2_B, PI2_C):
                    dve.drain()
                    nc.vector.scalar_tensor_tensor(out=t2, in0=turns, scalar=-part, in1=t2, op0=ALU.mult, op1=ALU.add)
                dve.drain()
                nc.vector.tensor_scalar(t2, t2, quarter * TWO_PI, PI_IN, ALU.add, ALU.min)
                dve.drain()
                last = nc.vector.tensor_scalar(trig[R, r, :], t2, -PI_IN, None, ALU.max)
            last.then_inc(sem["trig_arg"], 1)
            split(0, 0, 0)
            with dve.Fori(0, LAYERS) as l:
                norm_scale(l * 2)
                norm_lo(l * 2, G_MIX)
                split(l, 0, 1)
                split(l, 0, 2)
                for n in range(N_POOL, N_UQ):
                    split(l, 0, n + 1)
                    if n == N_Q:
                        dve.wait_ge(sem["vsq_done"], l + 1)
                        nc.vector.tensor_reduce(vstat[:, 0, :], vsq.rearrange("p i (h e) -> p (i h) e", e=SG_DIM),
                                                AX.X, ALU.add).then_inc(sem["vss_done"], 1)
                    if n == N_U:
                        dve.wait_ge(sem["rt_done"], l * 3 + 3)
                        nc.vector.reciprocal(rbc[:, :, :], rbc[:, :, :])
                        nc.vector.reciprocal(vstat[:, 2, :], vstat[:, 1, :])
                        dve.drain()
                        nc.vector.tensor_tensor(craw[:, 0:QC, :], craw[:, 0:QC, :],
                                                rbc[:, 0:1, :].broadcast_to([P, QC, S]), ALU.mult)
                        nc.vector.tensor_tensor(craw[:, QC:, :], craw[:, QC:, :],
                                                rbc[:, 1:2, :].broadcast_to([P, KVC, S]), ALU.mult)\
                            .then_inc(sem["cn_done"], 1)
                        nc.vector.tensor_tensor(
                            vn.rearrange("p i (h e) -> p (i h) e", e=SG_DIM), vz.rearrange("p i (h e) -> p (i h) e", e=SG_DIM),
                            vstat[:, 2, :].rearrange("p (a b) -> p a b", b=1).broadcast_to([P, TC * SG_HEADS, SG_DIM]), ALU.mult)
                        dve.drain()
                        nc.vector.tensor_tensor(
                            vn, vn, param[:, PR_SG:PR_WS].rearrange("p (a n) -> p a n", a=1).broadcast_to([P, TC, SG_WIDTH]),
                            ALU.mult).then_inc(sem["vn_ready"], 1)
                for c in range(QC + KVC):
                    dve.wait_ge(sem["c_hi"], l * 5 + c + 1)
                    nc.vector.scalar_tensor_tensor(out=cl[:, c, :], in0=craw[:, c, :], scalar=gain(G_Q + c),
                                                   in1=ch[:, c, :].bitcast(F32), op0=ALU.mult, op1=ALU.subtract)\
                        .then_inc(sem["c_lo"], 1)
                for c in range(2):
                    dve.wait_ge(sem["mix_hi"], l * 8 + c + 1)
                    nc.vector.scalar_tensor_tensor(out=hTl[:, 4 + c, :], in0=bank[2 + c][:, :], scalar=gain(G_PS + c),
                                                   in1=hTh[:, 4 + c, :].bitcast(F32), op0=ALU.mult, op1=ALU.subtract)\
                        .then_inc(sem["mix_lo"], 1)
                dve.drain()
                dve.wait_ge(sem["proj_out"], l * 10 + 10)
                for c in range(2):
                    dve.wait_ge(sem["sg_done"], l * 2 + c + 1)
                    bias = param[:, PR_BS + c * P:PR_BS + (c + 1) * P].rearrange("p (a n) -> p a n", a=1)
                    v4 = lambda ap: ap.rearrange("p (i n) -> p i n", i=TC)
                    nc.vector.tensor_tensor(v4(craw[:, c, :]), v4(bank[c][:, :]), bias.broadcast_to([P, TC, P]), ALU.add)
                    dve.drain()
                    nc.vector.tensor_tensor(craw[:, c, :], craw[:, c, :], uT[:, c, :], ALU.mult).then_inc(sem["sgr"], 1)
                for c in range(2):
                    dve.wait_ge(sem["mix_hi"], l * 8 + c + 3)
                    nc.vector.tensor_tensor(hTl[:, 6 + c, :], craw[:, c, :], hTh[:, 6 + c, :].bitcast(F32), ALU.subtract)\
                        .then_inc(sem["mix_lo"], 1)

                def rope(h):
                    vec = qT[64:96, h, :] if h < HEADS else krw[64:96, :]
                    turned = craw[64:96, 2 + h % 2, :]
                    dve.wait_ge(sem["rot_done"], l * 9 + h + 1)
                    nc.vector.tensor_tensor(turned, bank[6 + h % 2][64:96, :], trig[64:96, 1, :], ALU.mult)
                    nc.vector.tensor_tensor(vec, vec, trig[64:96, 0, :], ALU.mult)
                    dve.drain()
                    last = nc.vector.tensor_tensor(vec, vec, turned, ALU.add)
                    if h == HEADS:
                        dve.drain()
                        last = nc.vector.tensor_copy(
                            kT[64:96, :, :], vec.rearrange("p (a t) -> p a t", a=1).broadcast_to([ROPE, HEADS, S]))
                    last.then_inc(sem["q_rope"], 1)
                    dve.drain()

                for m in range(HEADS // 2):
                    split(l, 0, N_UQ + m + 1)
                    if m:
                        rope(2 * m - 2)
                        rope(2 * m - 1)
                split(l, 0, N_UV)
                for h in range(HEADS - 2, HEADS + 1):
                    rope(h)
                split(l, 0, N_WO)
                used(l, 0, N_UV)
                for i in range(TC):
                    nc.vector.tensor_copy(vt[:, i, :], bank[4 + i][:, :]).then_inc(sem["v2_out"], 1)
                for it in range(HEADS * TC + 2):
                    if it < HEADS * TC:
                        dve.wait_ge(sem["s_done"], l * 32 + it + 1)
                        nc.vector.tensor_reduce(astat[:, 0, it:it + 1], bank[it % 2][:, :], AX.X, ALU.max)
                        dve.drain()
                        nc.vector.tensor_scalar(astat[:, 1, it:it + 1], astat[:, 0, it:it + 1], -ATT_SCALE, None, ALU.mult)\
                            .then_inc(sem["nm_done"], 1)
                    if it >= 2:
                        e = it - 2
                        h, i = e // TC, e % TC
                        dve.wait_ge(sem["av_done"], l * 32 + e + 1)
                        nc.vector.reciprocal(astat[:, 3, e:e + 1], astat[:, 2, e:e + 1])
                        dve.drain()
                        nc.vector.tensor_scalar(att[:, i, h * VDIM:(h + 1) * VDIM], bank[4 + e % 2][:, 0:VDIM],
                                                astat[:, 3, e:e + 1], None, ALU.mult).then_inc(sem["a_out"], 1)
                for k in range(4):
                    dve.wait_ge(sem["mix_hi"], l * 8 + 5 + k)
                    nc.vector.tensor_tensor(hTl[:, k, :], bank[6 + k % 2][:, :], hTh[:, k, :].bitcast(F32), ALU.subtract)\
                        .then_inc(sem["mix_lo"], 1)

                def add_to_x(half, b0):
                    for i in range(TC):
                        cols = x[:, i, half * BANK:(half + 1) * BANK]
                        nc.vector.tensor_tensor(cols, bank[b0 + i][:, :], cols, ALU.add).then_inc(sem["x_upd"], 1)

                for half in range(2):
                    for n in range(N_WO + 4 * half, N_WO + 4 * half + 4):
                        split(l, 0, n + 1)
                    used(l, 0, N_WO + 4 * half + 3)
                    add_to_x(half, 4 * half)
                dve.drain()
                norm_scale(l * 2 + 1)
                norm_lo(l * 2 + 1, G_FFN)
                dve.drain()
                dve.sem_inc(sem["params_free"], 1)
                with dve.Fori(0, GROUPS) as g:
                    lg = l * GROUPS + g
                    for j in range(FG):
                        n = N_FFN + 2 * j
                        split(l, g, n + 1)
                        if j < ADA_PER_GROUP:
                            dve.drain()
                            if j == 0:
                                dve.wait_ge(sem["silu_c"], 1)
                            dve.wait_ge(sem["ada_in"], (lg * ADA_PER_GROUP + j + 1) * 16)
                            for r in range(2):
                                if r:
                                    dve.drain()
                                last = nc.vector.tensor_tensor_reduce(
                                    out=junk[:, :], in0=ada[:, r, :], in1=cbc[:, :], scale=1.0, scalar=0.0, op0=ALU.mult,
                                    op1=ALU.add, accum_out=ada_sum[:, 2 * j + r:2 * j + r + 1])
                            last.then_inc(sem["ada_used"], 1)
                        split(l, g, n + 2)
                        used(l, g, n + 1)
                        dve.wait_ge(sem["silu_done"], lg * FG + j + 1)
                        nc.vector.tensor_tensor(fr[:, j % 2, :], sgr[:, j % 2, :], bank[2 * (j % 2) + 1][:, :], ALU.mult)\
                            .then_inc(sem["fr_done"], 1)
                        dve.wait_ge(sem["fhi"], lg * FG + j + 1)
                        nc.vector.tensor_tensor(fTl[:, j, :], fr[:, j % 2, :], fTh[:, j, :].bitcast(F32), ALU.subtract)\
                            .then_inc(sem["flo"], 1)
                    dve.drain()
                    nc.vector.tensor_copy(mods[:, bass.ds(lg * (2 * ADA_PER_GROUP), 2 * ADA_PER_GROUP)], ada_sum[:, :])
                    for q in range(2 * DOWN_TILES):
                        n = N_FFN + 2 * FG + q
                        if q < 2 * DOWN_TILES - 1:
                            split(l, g, n + 1)
                        if q % DOWN_TILES == DOWN_TILES - 1:
                            half = q // DOWN_TILES
                            used(l, g, n)
                            add_to_x(half, 4 - 4 * half)
                    dve.wait_ge(sem["hi_done"], tiles_before(l, g, N_FFN + GROUP_TILES)[0] + 1)
                    nc.vector.tensor_tensor(wlo[0][:, :], raw[0][:, :], whi[0][:, :].bitcast(F32), ALU.subtract)\
                        .then_inc(sem["lo_done"], 1)

            def diff2(out, a, hi, name, wait, value):
                dve.wait_ge(sem[wait], value)
                nc.vector.tensor_tensor(out, a, hi.bitcast(F32), ALU.subtract).then_inc(sem[name], 1)

            def split2(n):
                t = MIX2_T0 + n
                diff2(wlo[t % 2], raw[t % 2], whi[t % 2], "lo_done", "hi_done", t + 1)

            def used2(n):
                dve.wait_ge(sem["tile_used"], MIX2_T0 + n + 3)

            V = nc.vector
            dve.drain()
            dve.wait_ge(sem["p2_in"], 16)
            logit = p2[:, P2_LOGIT:P2_LOGIT + 2 * RET_HEADS]
            V.scalar_tensor_tensor(out=decay_lg[:, 0, :], in0=logit, scalar=-1.0, in1=logit, op0=ALU.mult, op1=ALU.max).then_inc(sem["sg_in"], 1)
            V.tensor_tensor(mods[:, :], mods[:, :], p2[:, P2_B:P2_B + 6 * DK], ALU.add)
            dve.drain()
            for sc, g0 in ((SCALE_M, P2_PRE), (SCALE_F, P2_FPRE)):
                V.scalar_tensor_tensor(out=mods[:, sc:sc + DK], in0=mods[:, sc:sc + DK], scalar=1.0, in1=p2[:, g0:g0 + DK],
                                       op0=ALU.add, op1=ALU.mult)
            for gt, g0 in ((GATE_M, P2_POST), (GATE_F, P2_FPOST)):
                V.tensor_tensor(mods[:, gt:gt + DK], mods[:, gt:gt + DK], p2[:, g0:g0 + DK], ALU.mult)
            dve.drain()
            for r, gt in enumerate((GATE_M, GATE_F)):
                for k in range(DK):
                    last = V.tensor_scalar(diag[:, r * DK + k, :], ident, mods[:, gt + k:gt + k + 1], None, ALU.mult)
            last.then_inc(sem["diag_done"], 1)
            dve.wait_ge(sem["nrt"], 5)
            V.reciprocal(stats[:, 8:12], stats[:, 4:8])
            dve.drain()
            dve.wait_ge(sem["fn_in"], 16)
            for i in range(TC):
                last = V.scalar_tensor_tensor(out=x[:, i, :], in0=x[:, i, :], scalar=stats[:, 8 + i:9 + i], in1=fnrow[:, :],
                                              op0=ALU.mult, op1=ALU.mult)
            last.then_inc(sem["xf_done"], 1)
            dve.wait_ge(sem["sg_exp"], 1)
            y, z, z2, ac = (decay_lg[:, r, :] for r in (1, 2, 3, 4))
            V.tensor_scalar(z, y, 2.0, None, ALU.add)
            dve.drain()
            V.reciprocal(z, z)
            dve.drain()
            V.tensor_tensor(z, z, y, ALU.mult)
            dve.drain()
            V.tensor_tensor(z2, z, z, ALU.mult)
            dve.drain()
            V.tensor_scalar(ac, z2, 1.0 / 17.0, None, ALU.mult)
            for k in (15, 13, 11, 9, 7, 5, 3):
                dve.drain()
                V.scalar_tensor_tensor(out=ac, in0=ac, scalar=1.0 / k, in1=z2, op0=ALU.add, op1=ALU.mult)
            dve.drain()
            V.scalar_tensor_tensor(out=ac, in0=ac, scalar=1.0, in1=z, op0=ALU.add, op1=ALU.mult)
            V.tensor_scalar(decay_lg[:, 5, :], logit, 0.0, None, ALU.min)
            dve.drain()
            V.scalar_tensor_tensor(out=decay_lg[:, 6, :], in0=ac, scalar=-2.0, in1=decay_lg[:, 5, :], op0=ALU.mult, op1=ALU.add)
            dve.drain()
            V.tensor_scalar(decay_lg[:, 7, :], decay_lg[:, 6, :], -1.0, None, ALU.mult)
            dve.wait_ge(sem["nrt"], 6)
            V.reciprocal(stats[:, 8:12], stats[:, 4:8])
            dve.drain()
            dve.wait_ge(sem["rows_done"], 2)
            for i in range(TC):
                last = V.tensor_scalar(xh4[:, i, :], x[:, i, :], stats[:, 8 + i:9 + i], None, ALU.mult)
            last.then_inc(sem["xn_done"], 1)
            for k in range(DK):
                dve.wait_ge(sem["tr_done"], 4 * DK + k + 1)
                dve.drain()
                V.tensor_scalar(sm[:, k % 2, :], bank[k % 4][:, :], mods[:, SCALE_M + k:SCALE_M + k + 1],
                                mods[:, SHIFT_M + k:SHIFT_M + k + 1], ALU.mult, ALU.add).then_inc(sem["tmb"], 1)
                if k:
                    diff2(hTl[:, k - 1, :], sm[:, (k - 1) % 2, :], hTh[:, k - 1, :], "lob", "hib", k)
            diff2(hTl[:, DK - 1, :], sm[:, (DK - 1) % 2, :], hTh[:, DK - 1, :], "lob", "hib", DK)

            def table(h):
                dve.drain()
                V.tensor_scalar(tab[:, h % 2, :], delta, 0.0, decay_lg[:, 6, h:h + 1], ALU.max, ALU.mult)
                dve.drain()
                for a, b in ((0, S), (S, REL)):
                    V.tensor_scalar(junk[:, 0:b - a], delta[:, a:b], 0.0, decay_lg[:, 7, RET_HEADS + h:RET_HEADS + h + 1],
                                    ALU.min, ALU.mult)
                    dve.drain()
                    last = V.tensor_tensor(tab[:, h % 2, a:b], tab[:, h % 2, a:b], junk[:, 0:b - a], ALU.add)
                    dve.drain()
                dve.sem_inc(sem["e_arg"], 1)

            dve.wait_ge(sem["rel_in"], 16)
            def retention_scores(u):
                h, j = u // TC, u % TC
                if j == 0:
                    dve.wait_ge(sem["e_tab"], h + 1)
                    if h >= 2:
                        dve.wait_ge(sem["y_done"], h - 1)
                dve.wait_ge(sem["rs_done"], u + 1)
                V.tensor_tensor(decayed[h % 2][:, j, :], bank[6 + u % 2][:, :], tab[:, h % 2, rel_cols(j)], ALU.mult)\
                    .then_inc(sem["dec_done"], 1)
                if j == TC - 1:
                    dve.drain()
                    dve.sem_inc(sem["tab_free"], 1)
                    if h + 2 < RET_HEADS:
                        table(h + 2)
                    if h + 2 == RET_HEADS:
                        V.scalar_tensor_tensor(out=delta, in0=delta, scalar=-1.0, in1=delta, op0=ALU.mult, op1=ALU.max)\
                            .then_inc(sem["abs_done"], 1)

            def group_norm_stats(h):
                dve.wait_ge(sem["y_done"], h + 1)
                dve.drain()
                for i in range(TC):
                    V.bn_stats(bst[:, i, :], bank[Y_BANK[h]][:, i * P:(i + 1) * P])
                dve.drain()
                for i in range(TC):
                    last = V.bn_aggr(mv[:, i, :], bst[:, i, :])
                last.then_inc(sem["gn_var"], 1)

            def group_norm(h):
                dve.wait_ge(sem["gn_rt"], h + 1)
                V.reciprocal(gr[:, TC:2 * TC], gr[:, 0:TC])
                dve.drain()
                for i in range(TC):
                    last = V.tensor_scalar(cat[:, i, h * RET_V:(h + 1) * RET_V], bank[Y_BANK[h]][:, i * P:(i + 1) * P],
                                           mv[:, i, 0:1], gr[:, TC + i:TC + i + 1], ALU.subtract, ALU.mult)
                last.then_inc(sem["yn"], 1)

            for n in range(Q2["wo"]):
                split2(n + 1)
                if n in (1, 2):
                    table(n - 1)
                elif n == Q2["aqk"] - 1:
                    used2(n)
                    for i in range(TC):
                        V.tensor_copy(rvt[:, i, :], bank[i][:, :]).then_inc(sem["rv_out"], 1)
                if n == 20:
                    group_norm_stats(1)
                if n >= Q2["aqk"]:
                    retention_scores(n - Q2["aqk"])
                if n == 13:
                    group_norm_stats(0)
                elif n == 14:
                    group_norm(0)
                elif n == 21:
                    group_norm(1)
                elif n == 22:
                    group_norm_stats(2)
            used2(Q2["wo"] - 1)
            for i in range(TC):
                V.tensor_copy(avt[:, i, :], bank[2 + i][:, :]).then_inc(sem["av_out"], 1)
            group_norm(2)
            for it in range(DIL_HEADS * TC + 2):
                if it < DIL_HEADS * TC:
                    h, i = it // TC, it % TC
                    if i == 0:
                        dve.wait_ge(sem["tab_ready"], h + 1)
                    dve.wait_ge(sem["s2_done"], it + 1)
                    if it >= 2:
                        dve.wait_ge(sem["p2_done"], it - 1)
                    V.tensor_tensor_reduce(out=sm[:, it % 2, :], in0=bank[it % 2][:, :], in1=tab[:, h % 2, rel_cols(i)],
                                           scale=1.0, scalar=-3e38, op0=ALU.add, op1=ALU.max, accum_out=ast2[:, 0, it:it + 1])
                    dve.drain()
                    V.tensor_scalar(ast2[:, 1, it:it + 1], ast2[:, 0, it:it + 1], -1.0, None, ALU.mult).then_inc(sem["nm2"], 1)
                    if i == TC - 1:
                        dve.sem_inc(sem["tab_free"], 1)
                if it == 4:
                    group_norm_stats(3)
                if it >= 2:
                    c = it - 2
                    h, i = c // TC, c % TC
                    dve.wait_ge(sem["av2"], c + 1)
                    V.reciprocal(ast2[:, 3, c:c + 1], ast2[:, 2, c:c + 1])
                    dve.drain()
                    o0 = RET_HEADS * RET_V + h * DIL_DIM
                    V.tensor_scalar(cat[:, i, o0:o0 + DIL_DIM], bank[4 + c % 2][:, 0:DIL_DIM], ast2[:, 3, c:c + 1], None, ALU.mult)\
                        .then_inc(sem["a2_out"], 1)
            group_norm(3)
            for c, k in enumerate(CAT_ORDER):
                diff2(hTl[:, k, :], bank[4 + c % 2][:, :], hTh[:, k, :], "ml", "mh", c + 1)
            for n in range(Q2["wo"] + 1, MIX2_TILES + WO2_TILES):
                split2(n)
            dve.wait_ge(sem["post_ss"], 1)
            V.tensor_tensor(st2[:, 0:4], st2[:, 0:4], st2[:, 4:8], ALU.add).then_inc(sem["post_r"], 1)
            dve.wait_ge(sem["post_rt"], 1)
            V.reciprocal(st2[:, 8:12], st2[:, 4:8])
            dve.drain()
            for p in range(2 * TC):
                i, half = p % TC, p // TC
                if p >= 2:
                    dve.wait_ge(sem["x2_upd"], p - 1)
                V.scalar_tensor_tensor(out=sm[:, p % 2, :], in0=bank[p][:, :], scalar=st2[:, 8 + i:9 + i],
                                       in1=rows[:, 0, half * BANK:(half + 1) * BANK], op0=ALU.mult, op1=ALU.mult)\
                    .then_inc(sem["t_ready"], 1)
            dve.wait_ge(sem["nrt"], 7)
            V.reciprocal(stats[:, 8:12], stats[:, 4:8])
            dve.drain()
            for i in range(TC):
                last = V.tensor_scalar(hn[i], x[:, i, :], stats[:, 8 + i:9 + i], None, ALU.mult)
            last.then_inc(sem["h_done"], 1)

            def over(ap, n):
                return ap.rearrange("p (i a) -> p i a", a=1).broadcast_to([P, TC, n])

            lgt = bank[4][:, 0:TC * EXPERTS].rearrange("p (i e) -> p i e", e=EXPERTS)
            ex = rt_s[:, 0, :, :]
            dve.wait_ge(sem["lg_done"], 1)
            V.tensor_reduce(stats[:, 12:16], lgt, AX.X, ALU.max)
            dve.drain()
            V.tensor_tensor(ex, lgt, over(stats[:, 12:16], EXPERTS), ALU.subtract).then_inc(sem["lg_sh"], 1)
            dve.wait_ge(sem["lg_exp"], 1)
            V.tensor_reduce(stats[:, 16:20], ex, AX.X, ALU.add)
            dve.drain()
            V.reciprocal(stats[:, 20:24], stats[:, 16:20])
            dve.drain()
            V.tensor_tensor(aff[:, :, :], ex, over(stats[:, 20:24], EXPERTS), ALU.mult).then_inc(sem["aff_done"], 1)
            dve.wait_ge(sem["affT"], 1)
            V.tensor_copy(top, bank[5][0:EXPERTS, :])
            for r in range(CAPACITY // 8):
                dve.drain()
                V.max(top8[:, 8 * r:8 * r + 8], top)
                dve.drain()
                if r < CAPACITY // 8 - 1:
                    V.match_replace(top, top8[:, 8 * r:8 * r + 8], top, -1.0)
            V.tensor_scalar(dthr, const[0:EXPERTS, C_ID:C_ID + EXPERTS], top8[:, CAPACITY - 1:CAPACITY], None, ALU.mult)\
                .then_inc(sem["thr_d"], 1)
            ge = rt_s[:, 1:3, :, :]
            dve.wait_ge(sem["thr_bc"], 1)
            thr = bank[6][:, 0:EXPERTS].rearrange("p (a e) -> p a e", a=1).broadcast_to([P, TC, EXPERTS])
            V.tensor_tensor(ge[:, 0], aff[:, :, :], thr, ALU.is_gt)
            V.tensor_tensor(ge[:, 1], aff[:, :, :], thr, ALU.is_equal).then_inc(sem["ge_done"], 1)
            dve.wait_ge(sem["pre_done"], 1)
            before = bank[7][:, 0:2 * TC * EXPERTS].rearrange("p (w i e) -> p w i e", w=2, i=TC)
            total = bank[7][:, 2 * TC * EXPERTS:2 * TC * EXPERTS + EXPERTS]
            need = stats[:, 24:24 + EXPERTS]
            V.tensor_scalar(need, total, -1.0, float(CAPACITY), ALU.mult, ALU.add)
            dve.drain()
            need4 = need.rearrange("p (a e) -> p a e", a=1).broadcast_to([P, TC, EXPERTS])
            V.tensor_tensor(rt_s[:, 3], before[:, 1], need4, ALU.is_lt)
            V.tensor_tensor(rt_s[:, 4], before[:, 1], need4, ALU.min)
            dve.drain()
            V.tensor_tensor(rt_s[:, 3], rt_s[:, 3], ge[:, 1], ALU.mult)
            V.tensor_tensor(rt_s[:, 4], before[:, 0], rt_s[:, 4], ALU.add)
            dve.drain()
            V.tensor_tensor(rt_s[:, 3], rt_s[:, 3], ge[:, 0], ALU.add)
            dve.drain()
            V.scalar_tensor_tensor(out=rt_s[:, 5], in0=rt_s[:, 4], scalar=1.0, in1=rt_s[:, 3], op0=ALU.add, op1=ALU.mult)
            dve.drain()
            by_e = lambda t: t[:, 0:EXPERTS * TC].rearrange("p (e i) -> p i e", i=TC)
            V.tensor_scalar(by_e(slots), rt_s[:, 5], 1.0, None, ALU.subtract)
            V.tensor_copy(by_e(affe), aff[:, :, :])
            V.memset(slots[:, EXPERTS * TC:], -1.0)
            V.memset(affe[:, EXPERTS * TC:], 0.0)
            V.memset(sgt[:, :], 0.0)
            V.memset(hot[:, :, :].bitcast(F32), 0.0)
            dve.drain()
            dve.sem_inc(sem["sg_ready"], 1)

            def look_up(at):
                cols = slice(at * TC, (at + 1) * TC) if type(at) is int else bass.ds(at * TC, TC)
                V.tensor_copy(cur[:, 0, :], slots[:, cols])
                V.tensor_copy(cur[:, 1, :], affe[:, cols])
                dve.drain()
                V.tensor_tensor(hot[:, :, 64:128], const[:, C_IOTA:C_IOTA + 64].rearrange("p (a n) -> p a n", a=1)
                                .broadcast_to([P, TC, 64]), over(cur[:, 0, :], 64), ALU.is_equal).then_inc(sem["g2_ready"], 1)

            h3 = lambda ap: ap.rearrange("p (k t) -> p k t", t=64)

            def h_f32(value):
                dve.drain()
                dve.wait_ge(sem["silu_m"], value)
                dve.wait_ge(sem["up_t"], value)
                V.tensor_tensor(hf[:, :], sgl[:, :], bank[7][:, :], ALU.mult).then_inc(sem["hf_m"], 1)

            def h_low(r, value):
                dve.wait_ge(sem["hhi"], value)
                V.tensor_tensor(hTe[:, 8 * r:8 * r + 8, 64:128], h3(hf[:, :]), hTe[:, 8 * r:8 * r + 8, 0:64].bitcast(F32),
                                ALU.subtract).then_inc(sem["hlo"], 1)

            def add_scattered(which, value):
                dve.wait_ge(sem["sc_done"], value)
                for i, b in enumerate(SCATTER_BANKS):
                    part = acc[:, i, which * BANK:(which + 1) * BANK]
                    last = V.tensor_tensor(part, bank[b][:, :], part, ALU.add)
                last.then_inc(sem["sc_add"], 1)

            def expert_lo(e):
                this, ahead = not is_round(e, OPENING), not is_round(e, LAST)
                for n in range(0 if this else NEXT0, E_TILES):
                    there, before, c = round_tile(e, n)
                    if there:
                        dve.wait_ge(sem["moe_hi"], before + 1)
                        V.tensor_tensor(moe_lo[c % SPLIT_RING], moe_raw[c % RAW_RING][:, :],
                                        moe_hi[c % SPLIT_RING][:, :].bitcast(F32), ALU.subtract).then_inc(sem["moe_lo"], 1)
                    if n == 1:
                        h_f32(2 * e + 1)
                    elif n == 6:
                        h_low(0, 2 * e + 1)
                    elif n == 5:
                        add_scattered(0, 2 * e + 1)
                    elif n == 8:
                        add_scattered(1, 2 * e + 2)
                    elif n == 14 and this:
                        h_f32(2 * e + 2)
                    elif n == 17 and this:
                        h_low(1, 2 * e + 2)
                    elif n == 20 and ahead:
                        dve.wait_ge(sem["gat_done"], e + 2)
                        dve.wait_ge(sem["gg_ready"], e + 2)
                        look_up(e + 2)

            look_up(0)
            dve.sem_inc(sem["moe_lo"], RAW_RING)
            rounds(dve, expert_lo)
            for which in range(2):
                add_scattered(which, EXPERTS * 2 + which + 1)
            dve.wait_ge(sem["fin_ss"], 1)
            V.reciprocal(stats[:, 8:12], stats[:, 4:8])
            dve.drain()
            for i in range(TC):
                V.scalar_tensor_tensor(out=acc[:, i, :], in0=acc[:, i, :], scalar=stats[:, 8 + i:9 + i], in1=rows[:, 1, :],
                                       op0=ALU.mult, op1=ALU.mult)
                dve.drain()
                V.tensor_tensor(x[:, i, :], x[:, i, :], acc[:, i, :], ALU.add).then_inc(sem["fin_out"], 1)

        @block.gpsimd
        def _(pool):
            pool.dma_start(cbc[:, :], A["c"].broadcast_to([P, D])).then_inc(sem["cbc_in"], 16)
            pool.dma_start(trig[64:96, 0, :].bitcast(I32), A["positions"].broadcast_to([ROPE, S])).then_inc(sem["pos_in"], 16)
            pool.wait_ge(sem["counts_in"], 16)
            with pool.Fori(0, LAYERS) as l:
                pool.wait_ge(sem["params_free"], l + 1)
                pool.dma_start(param[:, :], A["params"][bass.ds(l, 1)].rearrange("a p n -> p (a n)"))\
                    .then_inc(sem["params_in"], 16)
                pool.wait_ge(sem["v_out"], l * TC + TC)
                nc.gpsimd.tensor_tensor(vsq, vz, vz, ALU.mult).then_inc(sem["vsq_done"], 1)
                nc.gpsimd.memset(hp[:, :, 0:PAD], 0.0)
                nc.gpsimd.memset(hp[:, :, PAD + S:], 0.0)
                pool.drain()
                pool.wait_ge(sem["proj_out"], l * 10 + 2)
                nc.gpsimd.tensor_tensor(s2[:, :, 1:], hp[:, :, 0:W2 - 1], hp[:, :, 1:], ALU.add)
                pool.drain()
                nc.gpsimd.tensor_tensor(s4[:, :, 2:W2 - 1], s2[:, :, 1:W2 - 2], s2[:, :, 3:], ALU.add)
                pool.drain()
                nc.gpsimd.tensor_tensor(s8[:, 4:W2 - 3], s4[:, 1, 2:W2 - 5], s4[:, 1, 6:W2 - 1], ALU.add)
                pool.drain()
                lo, hi = slice(0, 64), slice(64, 128)
                mid = slice(PAD, PAD + S)
                pool.wait_ge(sem["const_in"], 16)
                nc.gpsimd.tensor_tensor(pooled[hi, 1, :], s8[hi, PAD - 4:PAD - 4 + S], s8[hi, PAD + 4:PAD + 4 + S], ALU.add)
                nc.gpsimd.tensor_tensor(pooled[lo, 0, :], s2[lo, 0, mid], cnt[lo, 0, :], ALU.mult)
                nc.gpsimd.tensor_tensor(pooled[hi, 0, :], s4[hi, 0, mid], cnt[hi, 0, :], ALU.mult)
                nc.gpsimd.tensor_tensor(pooled[lo, 1, :], s8[lo, mid], cnt[lo, 1, :], ALU.mult)
                pool.drain()
                nc.gpsimd.tensor_tensor(pooled[hi, 1, :], pooled[hi, 1, :], cnt[hi, 1, :], ALU.mult)
                pool.drain()
                nc.gpsimd.tensor_tensor(pooled, pooled, hp[:, :, mid], ALU.subtract).then_inc(sem["pool_ready"], 1)
                with pool.Fori(0, GROUPS) as g:
                    for j in range(ADA_PER_GROUP):
                        t = (l * GROUPS + g) * ADA_PER_GROUP + j
                        pool.wait_ge(sem["ada_used"], t + 1)
                        pool.dma_start(ada[:, :, :], A["ada"][bass.ds(t, 1)].rearrange("a p (r d) -> p (a r) d", r=2))\
                            .then_inc(sem["ada_in"], 16)

            pool.wait_ge(sem["x_upd"], LAYERS * 24 + 1)
            pool.dma_start(p2[:, :], A["params2"]).then_inc(sem["p2_in"], 16)
            pool.dma_start(fnrow[:, :], A["final_norm"].rearrange("(a d) -> a d", a=1).broadcast_to([P, D])).then_inc(sem["fn_in"], 16)
            pool.dma_start(rel[:, :], A["rel"]).then_inc(sem["rel_in"], 16)
            pool.wait_ge(sem["rg_out"], TC)
            def gate_retention(h):
                c = slice(h * RET_V, (h + 1) * RET_V)
                pool.wait_ge(sem["yn"], h + 1)
                nc.gpsimd.tensor_tensor(cat[:, :, c], cat[:, :, c], rgt[:, :, c], ALU.mult).then_inc(sem["ret_out"], 1)

            pool.wait_ge(sem["abs_done"], 1)
            for h in range(DIL_HEADS):
                pool.wait_ge(sem["tab_free"], RET_HEADS + h - 1)
                slope = 2.0 ** (-8.0 * (h + 1) / DIL_HEADS)
                pool.drain()
                nc.gpsimd.tensor_scalar(tab[:, h % 2, :], delta, -slope, 0.0, ALU.mult, ALU.add)
                pool.drain()
                nc.gpsimd.tensor_tensor(tab[:, h % 2, :], tab[:, h % 2, :], lnm, ALU.add).then_inc(sem["tab_ready"], 1)
                if h == 0:
                    for g in range(RET_HEADS - 1):
                        gate_retention(g)
            gate_retention(RET_HEADS - 1)
            pool.wait_ge(sem["a2_out"], DIL_HEADS * TC)
            pool.wait_ge(sem["ct_done"], DK)
            pool.sem_inc(sem["moe_free"], 1)
            for p in range(2 * TC):
                part = x[:, p % TC, (p // TC) * BANK:(p // TC + 1) * BANK]
                pool.wait_ge(sem["t_ready"], p + 1)
                nc.gpsimd.tensor_tensor(part, part, sm[:, p % 2, :], ALU.add).then_inc(sem["x2_upd"], 1)
            pool.wait_ge(sem["nrt"], 7)
            pool.dma_start(wr[:, :, :], A["w_router"].rearrange("(k p) e -> p k e", p=P)).then_inc(sem["wr_in"], 16)
            pool.wait_ge(sem["lg_done"], 1)
            for i in range(TC):
                pool.wait_ge(sem["h_out"], i + 1)
                nc.gpsimd.tensor_tensor(h_lo[i][:, :] if i < TC - 1 else h_lo[i], asb[:, i % 2, :], h_hi[i][:, :].bitcast(F32),
                                        ALU.subtract).then_inc(sem["h_split"], 1)
            pool.wait_ge(sem["back_done"], TC)
            nc.gpsimd.memset(acc[:, :, :], 0.0).then_inc(sem["acc_zero"], 1)

            def gates(value):
                pool.wait_ge(sem["g2_ready"], value)
                nc.gpsimd.tensor_tensor(gg2[:, :, :].rearrange("p i (w c) -> p i w c", w=2),
                                        hot[:, :, 64:128].bitcast(F32).rearrange("p i (a c) -> p i a c", a=1).broadcast_to([P, TC, 2, 64]),
                                        cur[:, 1, :].rearrange("p (i a b) -> p i a b", a=1, b=1).broadcast_to([P, TC, 2, 64]), ALU.mult)\
                    .then_inc(sem["gg_ready"], 1)

            gates(1)
            with pool.Fori(0, LAST) as e:
                pool.wait_ge(sem["sgT"], e + 1)
                gates(e + 2)

        @block.tensor
        def _(pe):
            def mm3(out, stat, mov, start, stop):
                nc.tensor.matmul(out, stat[0], mov[0], start=start, stop=False)
                nc.tensor.matmul(out, stat[0], mov[1], start=False, stop=False)
                return nc.tensor.matmul(out, stat[1], mov[0], start=False, stop=stop)

            def arrived(l, g, n):
                pe.wait_ge(sem["lo_done"], tiles_before(l, g, n)[0] + 3)

            def w(n, a, b):
                return whi[n % 2][:, a:b], wlo[n % 2][:, a:b]

            def h(k, a=0, b=S):
                return hTh[:, k, a:b], hTl[:, k, a:b]

            def norm_T(nn, ready):
                pe.wait_ge(sem["xn_done"], ready)
                for k in range(DK):
                    if k >= 4:
                        pe.wait_ge(sem["hn_lo"], nn * DK + k - 3)
                    for i in range(TC):
                        last = nc.tensor.transpose(bank[k % 4][:, i * P:(i + 1) * P], xn4[:, i, k * P:(k + 1) * P], ident)
                    last.then_inc(sem["tr_done"], 1)

            pe.wait_ge(sem["const_in"], 16)
            pe.sem_inc(sem["tile_used"], 2)
            with pe.Fori(0, LAYERS) as l:
                norm_T(l * 2, l * 2 + 1)
                pe.wait_ge(sem["hn_lo"], l * 16 + 8)
                for n in (0, 1):
                    arrived(l, 0, n)
                    for kk in range(4):
                        k = 4 * n + kk
                        for i in range(TC):
                            last = mm3(bank[i][:, 0:SG_WIDTH], h(k, i * P, (i + 1) * P),
                                       w(n, kk * SG_WIDTH, (kk + 1) * SG_WIDTH), k == 0, k == DK - 1)
                    last.then_inc(sem["tile_used"], 1)
                for n in range(N_POOL, N_UQ):
                    c = n - N_POOL
                    arrived(l, 0, n)
                    if c >= 4:
                        pe.wait_ge(sem["proj_out"], l * 10 + c - 3)
                    for k in range(DK):
                        last = mm3(bank[4 + c % 4][:, :], w(n, k * P, (k + 1) * P), h(k), k == 0, k == DK - 1)
                    last.then_inc(sem["tile_used"], 1)
                    if n == N_KR:
                        pe.wait_ge(sem["v_out"], l * TC + TC)
                        pe.wait_ge(sem["proj_out"], l * 10 + 7)
                        for b, c0, c1 in ((0, 0, QC), (1, QC, QC + KVC)):
                            for cc in range(c0, c1):
                                last = nc.tensor.matmul(bank[b][:, :], ones, csq[:, cc, :], start=cc == c0, stop=cc == c1 - 1)
                            last.then_inc(sem["ssq_done"], 1)
                pe.wait_ge(sem["pool_ready"], l + 1)
                for c in range(2):
                    nc.tensor.matmul(bank[2 + c][:, :], wp_bd[:, c, :], pooled[:, c, :], start=True, stop=True)\
                        .then_inc(sem["pmm_done"], 1)
                pe.wait_ge(sem["vn_ready"], l + 1)
                pe.wait_ge(sem["rt_done"], l * 3 + 3)
                for c in range(2):
                    for i in range(TC):
                        for gg in range(2):
                            hd = 2 * c + gg
                            last = nc.tensor.matmul(bank[c][gg * 64:(gg + 1) * 64, i * P:(i + 1) * P],
                                                    vn[:, i, hd * SG_DIM:(hd + 1) * SG_DIM], wsT[:, hd, :],
                                                    start=True, stop=True)
                    last.then_inc(sem["sg_done"], 1)

                def rot(hd):
                    vec = qT[0:QK, hd, :] if hd < HEADS else krw[0:QK, :]
                    pe.wait_ge(sem["q_raw"], l * 8 + min(hd, HEADS - 1) + 1)
                    if hd >= 2:
                        pe.wait_ge(sem["q_rope"], l * 9 + hd - 1)
                    nc.tensor.matmul(bank[6 + hd % 2][64:96, :], const[0:QK, C_ROT:C_ROT + ROPE], vec, start=True, stop=True)\
                        .then_inc(sem["rot_done"], 1)

                pe.wait_ge(sem["proj_out"], l * 10 + 10)
                pe.wait_ge(sem["c_lo"], l * 5 + QC)
                for hd in range(HEADS):
                    n = N_UQ + hd // 2
                    if hd % 2 == 0:
                        arrived(l, 0, n)
                    if hd >= 2:
                        pe.wait_ge(sem["q_raw"], l * 8 + hd - 1)
                    for k in range(QC):
                        a = ((hd % 2) * QC + k) * QK
                        last = mm3(bank[4 + hd % 2][0:QK, :], w(n, a, a + QK), (ch[:, k, :], cl[:, k, :]), k == 0, k == QC - 1)
                    last.then_inc(sem["tile_used" if hd % 2 else "qe_done"], 1)
                    if hd:
                        rot(hd - 1)
                rot(HEADS - 1)
                rot(HEADS)
                pe.wait_ge(sem["mix_lo"], l * 8 + 4)
                pe.wait_ge(sem["c_lo"], l * 5 + QC + KVC)
                arrived(l, 0, N_UK)
                for j in range(HEADS // 2):
                    for k in range(KVC):
                        a = k * BANK + j * P
                        last = mm3(bank[j][:, :], w(N_UK, a, a + P), (ch[:, QC + k, :], cl[:, QC + k, :]), k == 0, k == KVC - 1)
                    last.then_inc(sem["k_done" if j < 3 else "tile_used"], 1)
                arrived(l, 0, N_UV)
                pe.wait_ge(sem["q_raw"], l * 8 + 8)
                pe.wait_ge(sem["q_rope"], l * 9 + 9)
                for i in range(TC):
                    for k in range(KVC):
                        last = mm3(bank[4 + i][:, :], (ch[:, QC + k, i * P:(i + 1) * P], cl[:, QC + k, i * P:(i + 1) * P]),
                                   w(N_UV, k * BANK, (k + 1) * BANK), k == 0, k == KVC - 1)
                last.then_inc(sem["tile_used"], 1)
                pe.wait_ge(sem["k_out"], l * 4 + 4)
                pe.wait_ge(sem["v2_out"], l * 4 + 4)
                N_IT = HEADS * TC
                for it in range(-1, N_IT + 1):
                    if it + 1 < N_IT:
                        e = it + 1
                        hd, i = e // TC, e % TC
                        if e >= 2:
                            pe.wait_ge(sem["p_done"], l * 32 + e - 1)
                        nc.tensor.matmul(bank[e % 2][:, :], qT[0:QK, hd, i * P:(i + 1) * P], kT[0:QK, hd, :],
                                         start=True, stop=True).then_inc(sem["s_done"], 1)
                    if 0 <= it < N_IT:
                        pe.wait_ge(sem["p_done"], l * 32 + it + 1)
                        if it >= 2:
                            pe.wait_ge(sem["pts_done"], l * 32 + it - 1)
                        for kc in range(TC):
                            last = nc.tensor.transpose(bank[2 + it % 2][:, kc * P:(kc + 1) * P],
                                                       prob[it % 2][:, kc * P:(kc + 1) * P], ident)
                        last.then_inc(sem["tr2_done"], 1)
                    if it >= 1:
                        e = it - 1
                        hd = e // TC
                        pe.wait_ge(sem["pts_done"], l * 32 + e + 1)
                        if e >= 2:
                            pe.wait_ge(sem["a_out"], l * 32 + e - 1)
                        for kc in range(TC):
                            last = nc.tensor.matmul(bank[4 + e % 2][:, 0:VDIM], probT[e % 2][:, kc * P:(kc + 1) * P],
                                                    vt[:, kc, hd * VDIM:(hd + 1) * VDIM], start=kc == 0, stop=kc == TC - 1)
                        last.then_inc(sem["av_done"], 1)
                pe.wait_ge(sem["a_out"], l * 32 + 32)
                for k in range(4):
                    if k >= 2:
                        pe.wait_ge(sem["mix_lo"], l * 8 + 3 + k)
                    for i in range(TC):
                        last = nc.tensor.transpose(bank[6 + k % 2][:, i * P:(i + 1) * P], att[:, i, k * P:(k + 1) * P], ident)
                    last.then_inc(sem["at_done"], 1)
                pe.wait_ge(sem["mix_lo"], l * 8 + 8)
                for half in range(2):
                    for q in range(4):
                        n = N_WO + 4 * half + q
                        arrived(l, 0, n)
                        for kk in range(2):
                            k = 2 * q + kk
                            for i in range(TC):
                                last = mm3(bank[4 * half + i][:, :], h(k, i * P, (i + 1) * P),
                                           w(n, kk * BANK, (kk + 1) * BANK), k == 0, k == DK - 1)
                        last.then_inc(sem["tile_used"], 1)
                norm_T(l * 2 + 1, l * 2 + 2)
                with pe.Fori(0, GROUPS) as g:
                    pe.wait_ge(sem["hn_lo"], l * 16 + 16)
                    lg = l * GROUPS + g
                    pe.wait_ge(sem["x_upd"], l * 24 + g * 8 + 9)
                    for j in range(FG):
                        for up in range(2):
                            n = N_FFN + 2 * j + up
                            arrived(l, g, n)
                            if j >= 2:
                                pe.wait_ge(sem["fr_done"], lg * FG + j - 1)
                            for k in range(DK):
                                last = mm3(bank[2 * (j % 2) + up][:, :], w(n, k * P, (k + 1) * P), h(k), k == 0, k == DK - 1)
                            last.then_inc(sem["tile_used"], 1)
                    pe.wait_ge(sem["flo"], lg * FG + FG)
                    for half in range(2):
                        for q in range(DOWN_TILES):
                            n = N_FFN + 2 * FG + half * DOWN_TILES + q
                            arrived(l, g, n)
                            for ff in range(min(2, FG - 2 * q)):
                                f = 2 * q + ff
                                for i in range(TC):
                                    last = mm3(bank[4 - 4 * half + i][:, :], (fTh[:, f, i * P:(i + 1) * P], fTl[:, f, i * P:(i + 1) * P]),
                                               w(n, ff * BANK, (ff + 1) * BANK), f == 0, f == FG - 1)
                            last.then_inc(sem["tile_used"], 1)

            def arrived2(n):
                pe.wait_ge(sem["lo_done"], MIX2_T0 + n + 3)

            def w2(n, a, b):
                t = (MIX2_T0 + n) % 2
                return whi[t][:, a:b], wlo[t][:, a:b]

            pe.wait_ge(sem["diag_done"], 1)
            for r in range(2):
                for k in range(DK):
                    last = nc.tensor.matmul(bank[4 + 2 * r + k // 4][:, (k % 4) * P:(k % 4 + 1) * P], ones, diag[:, r * DK + k, :],
                                            start=True, stop=True)
                last.then_inc(sem["rows_done"], 1)
            pe.wait_ge(sem["xn_done"], 5)
            for k in range(DK):
                if k >= 4:
                    pe.wait_ge(sem["tmb"], k - 3)
                for i in range(TC):
                    last = nc.tensor.transpose(bank[k % 4][:, i * P:(i + 1) * P], xh4[:, i, k * P:(k + 1) * P], ident)
                last.then_inc(sem["tr_done"], 1)
            pe.wait_ge(sem["lob"], DK)
            pe.wait_ge(sem["rows_out"], 4)
            def feature_tile(n):
                f = by_feature(n)
                arrived2(n)
                if f >= 2:
                    pe.wait_ge(sem["pj2"], f - 1)
                for k in range(DK):
                    last = mm3(bank[4 + f % 2][:, :], w2(n, k * P, (k + 1) * P), h(k), k == 0, k == DK - 1)
                last.then_inc(sem["tile_used"], 1)

            def token_tile(n, q, b0):
                arrived2(n)
                for kk in range(2):
                    k = 2 * q + kk
                    for i in range(TC):
                        last = mm3(bank[b0 + i][:, :], h(k, i * P, (i + 1) * P), w2(n, kk * BANK, (kk + 1) * BANK),
                                   k == 0, k == DK - 1)
                last.then_inc(sem["tile_used"], 1)

            def retention_scores(u):
                hd, j = u // TC, u % TC
                r = slice(64 * (hd % 2), 64 * (hd % 2) + 64)
                if u == 0:
                    pe.wait_ge(sem["pj2"], 4)
                elif u >= 2:
                    pe.wait_ge(sem["dec_done"], u - 1)
                nc.tensor.matmul(bank[6 + u % 2][:, :], rqk[r, 2 + hd // 2, j * P:(j + 1) * P], rqk[r, hd // 2, :],
                                 start=True, stop=True).then_inc(sem["rs_done"], 1)

            def retention_sum(g):
                pe.wait_ge(sem["dec_done"], (g + 1) * TC)
                pe.wait_ge(sem["rv_out"], TC)
                if g == 2:
                    pe.wait_ge(sem["yn"], 1)
                for i in range(TC):
                    for j in range(TC):
                        last = nc.tensor.matmul(bank[Y_BANK[g]][:, i * P:(i + 1) * P], decayed[g % 2][:, j, i * P:(i + 1) * P],
                                                rvt[:, j, g * RET_V:(g + 1) * RET_V], start=j == 0, stop=j == TC - 1)
                last.then_inc(sem["y_done"], 1)

            for n in range(Q2["wo"]):
                if by_feature(n) is not None:
                    feature_tile(n)
                elif n < Q2["aqk"]:
                    token_tile(n, n - Q2["rv"], 0)
                elif n < Q2["av"]:
                    if n == Q2["rg"]:
                        pe.wait_ge(sem["pj2"], 12)
                    token_tile(n, n - Q2["rg"], 2)
                else:
                    if n == Q2["av"]:
                        pe.wait_ge(sem["rg_out"], TC)
                    token_tile(n, n - Q2["av"], 2)
                if n >= Q2["aqk"]:
                    retention_scores(n - Q2["aqk"])
                if n in (12, 19, 21):
                    retention_sum((12, 19, 21).index(n))
            retention_sum(3)
            pe.wait_ge(sem["av_out"], TC)
            pe.wait_ge(sem["yn"], 3)
            N_IT = DIL_HEADS * TC
            for it in range(-1, N_IT + 1):
                if it + 1 < N_IT:
                    c = it + 1
                    hd, i = c // TC, c % TC
                    r = slice(64 * (hd % 2), 64 * (hd % 2) + 64)
                    if c >= 2:
                        pe.wait_ge(sem["nm2"], c - 1)
                    nc.tensor.matmul(bank[c % 2][:, :], aqk[r, hd // 2, i * P:(i + 1) * P], aqk[r, 4 + hd // 2, :],
                                     start=True, stop=True).then_inc(sem["s2_done"], 1)
                if 0 <= it < N_IT:
                    pe.wait_ge(sem["p2_done"], it + 1)
                    if it >= 2:
                        pe.wait_ge(sem["pts2"], it - 1)
                    for kc in range(TC):
                        last = nc.tensor.transpose(bank[2 + it % 2][:, kc * P:(kc + 1) * P],
                                                   prob2[it % 2][:, kc * P:(kc + 1) * P], ident)
                    last.then_inc(sem["tr3"], 1)
                if it >= 1:
                    c = it - 1
                    hd = c // TC
                    pe.wait_ge(sem["pts2"], c + 1)
                    if c >= 2:
                        pe.wait_ge(sem["a2_out"], c - 1)
                    for kc in range(TC):
                        last = nc.tensor.matmul(bank[4 + c % 2][:, 0:DIL_DIM], probT2[c % 2][:, kc * P:(kc + 1) * P],
                                                avt[:, kc, hd * DIL_DIM:(hd + 1) * DIL_DIM], start=kc == 0, stop=kc == TC - 1)
                    last.then_inc(sem["av2"], 1)
            pe.wait_ge(sem["a2_out"], N_IT)
            for c, k in enumerate(CAT_ORDER):
                if c == 4:
                    pe.wait_ge(sem["ret_out"], RET_HEADS - 1)
                elif c == 7:
                    pe.wait_ge(sem["ret_out"], RET_HEADS)
                if c >= 2:
                    pe.wait_ge(sem["ml"], c - 1)
                for i in range(TC):
                    last = nc.tensor.transpose(bank[4 + c % 2][:, i * P:(i + 1) * P], cat[:, i, k * P:(k + 1) * P], ident)
                last.then_inc(sem["ct_done"], 1)
            pe.wait_ge(sem["ml"], DK)
            for q in range(8):
                token_tile(Q2["wo"] + q, q % 4, 4 * (q // 4))
            pe.wait_ge(sem["h_done"], 1)
            for k in range(DK):
                if k >= 4:
                    pe.wait_ge(sem["hT_out"], k - 3)
                for i in range(TC):
                    last = nc.tensor.transpose(bank[k % 4][:, i * P:(i + 1) * P], hn[i][:, k * P:(k + 1) * P], ident)
                last.then_inc(sem["hT_done"], 1)
            pe.wait_ge(sem["hT_out"], DK)
            pe.wait_ge(sem["wr_in"], 16)
            for i in range(TC):
                for k in range(DK):
                    last = nc.tensor.matmul(bank[4][:, i * EXPERTS:(i + 1) * EXPERTS], hTf[:, k, i * P:(i + 1) * P], wr[:, k, :],
                                            start=k == 0, stop=k == DK - 1)
            last.then_inc(sem["lg_done"], 1)

            def back(i):
                if i >= 2:
                    pe.wait_ge(sem["h_out"], i - 1)
                for k in range(DK):
                    last = nc.tensor.transpose(bank[2 * (i % 2) + k // 4][:, (k % 4) * P:(k % 4 + 1) * P],
                                               hTf[:, k, i * P:(i + 1) * P], ident)
                last.then_inc(sem["back_done"], 1)

            back(0)
            back(1)
            pe.wait_ge(sem["aff_done"], 1)
            for i in range(TC):
                last = nc.tensor.transpose(bank[5][0:EXPERTS, i * P:(i + 1) * P], aff[:, i, :], ident)
            last.then_inc(sem["affT"], 1)
            back(2)
            back(3)
            pe.wait_ge(sem["thr_d"], 1)
            nc.tensor.matmul(bank[6][:, 0:EXPERTS], const[0:EXPERTS, C_ONE:C_ONE + P], dthr, start=True, stop=True)\
                .then_inc(sem["thr_bc"], 1)
            pe.wait_ge(sem["ge_done"], 1)
            for wh in range(2):
                for i in range(TC):
                    for j in range(i + 1):
                        nc.tensor.matmul(bank[7][:, (wh * TC + i) * EXPERTS:(wh * TC + i + 1) * EXPERTS],
                                         ones if j < i else const[:, C_TRI:C_TRI + P], rt_s[:, 1 + wh, j, :], start=j == 0, stop=j == i)
            for j in range(TC):
                last = nc.tensor.matmul(bank[7][:, 2 * TC * EXPERTS:2 * TC * EXPERTS + EXPERTS], ones, rt_s[:, 1, j, :],
                                        start=j == 0, stop=j == TC - 1)
            last.then_inc(sem["pre_done"], 1)

            def gather(value):
                pe.wait_ge(sem["g2_ready"], value)
                for i in range(TC):
                    for w, part in enumerate((h_hi[i], h_lo[i])):
                        for b in range(2):
                            last = nc.tensor.matmul(bank[2 + b][:, :], hot[:, i, 64 - 64 * w:192 - 64 * w],
                                                    part[:, b * BANK:(b + 1) * BANK], start=i == 0 and w == 0, stop=i == TC - 1 and w == 1)
                last.then_inc(sem["gat_done"], 1)

            def turn_tokens(value):
                pe.wait_ge(sem["gat_out"], value)
                for k in range(DK):
                    last = nc.tensor.transpose(bank[k // 4][:, (k % 4) * P:(k % 4 + 1) * P], gathered[:, k * P:(k + 1) * P], ident)
                last.then_inc(sem["x_turned"], 1)

            def scatter(which):
                for i, b in enumerate(SCATTER_BANKS):
                    last = nc.tensor.matmul(bank[b][:, :], sgt[:, i * P:(i + 1) * P], ysb[:, which * BANK:(which + 1) * BANK],
                                            start=True, stop=True)
                last.then_inc(sem["sc_done"], 1)

            def add_halves_T(row, b, name):
                for j in range(8):
                    last = nc.tensor.matmul(bank[b][:, j * 64:(j + 1) * 64], asb[:, row, j * P:(j + 1) * P],
                                            const[:, C_I2:C_I2 + 64], start=True, stop=True)
                last.then_inc(sem[name], 1)

            def expert_products(e):
                this, ahead = not is_round(e, OPENING), not is_round(e, LAST)
                for n in range(0 if this else NEXT0, E_TILES):
                    there, before, c = round_tile(e, n)
                    if there:
                        name, half, _ = ROUND[n // 4]
                        pe.wait_ge(sem["moe_lo"], before + 1 + RAW_RING)
                        if n == 0:
                            pe.wait_ge(sem["gate_out"], 2 * e + 1)
                        elif n == 4:
                            pe.wait_ge(sem["up_out"], 2 * e + 1)
                            if ahead:
                                pe.wait_ge(sem["gat_out"], e + 2)
                        elif n == 8:
                            pe.wait_ge(sem["hlo"], 2 * e + 1)
                            pe.wait_ge(sem["sc_add"], 2 * e + 2)
                        elif n == 12:
                            if this:
                                pe.wait_ge(sem["gate_out"], 2 * e + 2)
                            pe.wait_ge(sem["x_done"], e + 2)
                        elif n == 16 and this:
                            pe.wait_ge(sem["up_out"], 2 * e + 2)
                        elif n == 16:
                            pe.wait_ge(sem["gat_out"], 1)
                        elif n == 20:
                            pe.wait_ge(sem["hlo"], 2 * e + 2)
                        b0 = {"w_gate": 0, "w_up": 2, "w_down": 4}[name]
                        slot = c % SPLIT_RING
                        for cc in range(2):
                            k = 2 * (n % 4) + cc + (DK * half if name == "w_down" else 0)
                            first, final = k == 0, k == (2 * DK if name == "w_down" else DK) - 1
                            stat = hTe[:, k, :] if name == "w_down" else xTe[:, k, :]
                            for is_hi, part in ((True, moe_hi[slot][:, :]), (False, moe_lo[slot])):
                                for b in range(2):
                                    a = cc * D + b * BANK
                                    last = nc.tensor.matmul(bank[b0 + b][:, :], stat, part[:, a:a + BANK],
                                                            start=first and is_hi, stop=final and not is_hi)
                        last.then_inc(sem["moe_used"], 1)
                    if n == 0 and ahead:
                        pe.wait_ge(sem["up_out"], 2 * e + 1)
                        gather(e + 2)
                    elif n == 3:
                        pe.wait_ge(sem["y_out"], e + 1)
                        pe.wait_ge(sem["sg_ready"], e + 1)
                        pe.wait_ge(sem["silu_m"], 2 * e + 1)
                        pe.wait_ge(sem["hf_m"], 2 * e + 1)
                        scatter(0)
                    elif n == 6:
                        pe.wait_ge(sem["sc_add"], 2 * e + 1)
                        scatter(1)
                    elif n == 8 and ahead:
                        pe.wait_ge(sem["gate_out"], 2 * e + 2)
                        turn_tokens(e + 2)
                    elif n == 10:
                        add_halves_T(0, 6, "gate_t")
                    elif n == 11:
                        pe.wait_ge(sem["up_out"], 2 * e + 2)
                        add_halves_T(1, 7, "up_t")
                    elif n == 15 and this:
                        pe.wait_ge(sem["hf_m"], 2 * e + 2)
                        pe.wait_ge(sem["gg_ready"], e + 1)
                        for i in range(TC):
                            last = nc.tensor.transpose(bank[7][:, i * P:(i + 1) * P], gg2[:, i, :], ident)
                        last.then_inc(sem["sgT"], 1)
                    elif n == 19 and ahead:
                        pe.wait_ge(sem["gate_out"], 2 * e + 3)
                        if this:
                            pe.wait_ge(sem["silu_m"], 2 * e + 2)
                        add_halves_T(0, 6, "gate_t")
                    elif n == 23 and ahead:
                        pe.wait_ge(sem["up_out"], 2 * e + 3)
                        pe.wait_ge(sem["sg_ready"], e + 2)
                        add_halves_T(1, 7, "up_t")

            pe.wait_ge(sem["h_split"], TC)
            gather(1)
            turn_tokens(1)
            pe.wait_ge(sem["acc_zero"], 1)
            pe.sem_inc(sem["moe_used"], SPLIT_RING)
            rounds(pe, expert_products)
            pe.wait_ge(sem["y_out"], EXPERTS + 1)
            pe.wait_ge(sem["sg_ready"], EXPERTS + 1)
            for which in range(2):
                pe.wait_ge(sem["sc_add"], EXPERTS * 2 + which)
                scatter(which)


def _chunks(w, cols):
    import numpy as np
    k = w.shape[0] // P
    return np.ascontiguousarray(w.reshape(k, P, cols).transpose(1, 0, 2).reshape(P, k * cols))


def _tiles(a):
    import numpy as np
    out = np.zeros((N_TILES, P, TILE), np.float32)
    o1, o2 = Q_LORA, Q_LORA + KV_LORA
    o3 = o2 + ROPE
    o4 = o3 + 256
    o5 = o4 + SG_WIDTH
    for l in range(LAYERS):
        w_in, w_o, w_uq, w_ukv = a["w_in"][l], a["w_o"][l], a["w_uq"][l], a["w_ukv"][l]
        t0 = l * LAYER_TILES

        def put(n, block):
            out[t0 + n, :, 0:block.shape[1]] = block

        for q in range(2):
            put(N_V + q, _chunks(w_in[q * 512:(q + 1) * 512, o5:], SG_WIDTH))
            put(N_POOL + q, _chunks(w_in[:, o3 + q * P:o3 + (q + 1) * P], P))
            put(N_U + q, _chunks(w_in[:, o4 + q * P:o4 + (q + 1) * P], P))
            put(N_KV + q, _chunks(w_in[:, o1 + q * P:o1 + (q + 1) * P], P))
        for q in range(QC):
            put(N_Q + q, _chunks(w_in[:, q * P:(q + 1) * P], P))
        put(N_KR, _chunks(w_in[:, o2 - 64:o2 + 64], P))
        for m in range(HEADS // 2):
            put(N_UQ + m, np.concatenate([_chunks(w_uq[:, hd * QK:(hd + 1) * QK], QK) for hd in (2 * m, 2 * m + 1)], axis=1))
        kv = w_ukv.reshape(KV_LORA, HEADS, NOPE + VDIM)
        put(N_UK, _chunks(kv[:, :, :NOPE].reshape(KV_LORA, -1), BANK))
        put(N_UV, _chunks(kv[:, :, NOPE:].reshape(KV_LORA, -1), BANK))
        for half in range(2):
            cols = slice(half * BANK, (half + 1) * BANK)
            for q in range(4):
                put(N_WO + 4 * half + q, _chunks(w_o[q * 256:(q + 1) * 256, cols], BANK))
        for g in range(GROUPS):
            g0 = N_FFN + g * GROUP_TILES
            for j in range(FG):
                f = g * FG + j
                put(g0 + 2 * j, _chunks(a["w_gate"][l][:, f * P:(f + 1) * P], P))
                put(g0 + 2 * j + 1, _chunks(a["w_up"][l][:, f * P:(f + 1) * P], P))
            for half in range(2):
                for q in range(DOWN_TILES):
                    r0 = (g * FG + 2 * q) * P
                    r1 = min(r0 + 2 * P, (g + 1) * FG * P)
                    put(g0 + 2 * FG + half * DOWN_TILES + q,
                        _chunks(a["w_down"][l][r0:r1, half * BANK:(half + 1) * BANK], BANK))
    w = a["w_in_2"][0]
    for n in range(12):
        c0 = n * P if n < 4 else 1536 + (n - 4) * P
        out[MIX2_T0 + (Q2["rqk"] + n if n < 4 else Q2["aqk"] + n - 4)] = _chunks(w[:, c0:c0 + P], P)
    for name, c0 in (("rv", 512), ("rg", 1024), ("av", 2560)):
        for q in range(4):
            out[MIX2_T0 + Q2[name] + q] = _chunks(w[q * 256:(q + 1) * 256, c0:c0 + BANK], BANK)
    for half in range(2):
        for q in range(4):
            out[MIX2_T0 + Q2["wo"] + 4 * half + q] = _chunks(a["w_out_2"][0][q * 256:(q + 1) * 256, half * BANK:(half + 1) * BANK], BANK)
    return out


def _params(a):
    import numpy as np
    out = np.zeros((LAYERS, P, N_PARAM), np.float32)
    for l in range(LAYERS):
        p = out[l]
        for off, v in ((G_MIX, a["mix_norm"][l]), (G_FFN, a["ffn_norm"][l]), (G_Q, a["q_norm"][l]), (G_KV, a["kv_norm"][l]),
                       (G_PS, a["pool_scale"][l])):
            p[:, off:off + v.size // P] = v.reshape(-1, P).T
        for c in range(2):
            p[:, PR_BS + c * P:PR_BS + (c + 1) * P] = np.repeat(a["b_s"][l][2 * c:2 * c + 2], 64, axis=0)
            for q in range(2):
                p[q * 64:(q + 1) * 64, PR_WP + c * P + q * 64:PR_WP + c * P + (q + 1) * 64] = a["w_pool"][l][2 * c + q]
        p[:, PR_SG:PR_WS] = a["sg_norm"][l][None, :]
        p[:, PR_WS:PR_WP] = a["w_s"][l].transpose(2, 0, 1).reshape(P, -1)
    return out


def _const():
    import numpy as np
    c = np.zeros((P, N_CONST), np.float32)
    c[:, C_ID:C_ID + P] = np.eye(P)
    c[:, C_ONE:C_ONE + P] = 1.0
    half = ROPE // 2
    for j in range(half):
        c[64 + half + j, C_ROT + j] = -1.0
        c[64 + j, C_ROT + half + j] = 1.0
    freq = (np.float32(10000.0) ** (-np.arange(0, ROPE, 2, dtype=np.float32) / np.float32(ROPE))).astype(np.float32)
    c[64:96, C_FREQ] = np.concatenate([freq, freq])
    c[:, C_TRI:C_TRI + P] = np.triu(np.ones((P, P)), 1)
    c[:, C_IOTA:C_IOTA + P] = (np.arange(P) % 64)[None, :]
    c[:, C_I2:C_I2 + 64] = (np.arange(P)[:, None] % 64) == np.arange(64)[None, :]
    c[:, C_EPS] = EPS
    c[:, C_GEPS] = GN_EPS
    return c


def _counts():
    import numpy as np
    c = np.zeros((P, 2, S), np.float32)
    t = np.arange(S)
    for g, wdw in enumerate(POOL_WINDOWS):
        left = wdw // 2
        n = np.clip(t + wdw - left, 0, S) - np.clip(t - left, 0, S)
        c[(g % 2) * 64:(g % 2) * 64 + 64, g // 2] = (1.0 / n.astype(np.float32))[None, :]
    return c


def _ada(w_ada):
    import numpy as np
    return np.ascontiguousarray(w_ada.T.reshape(ADA_TILES, 2, P, D).transpose(0, 2, 1, 3).reshape(ADA_TILES, P, 2 * D))


def _params2(a):
    import numpy as np
    out = np.zeros((P, N_P2), np.float32)
    for off, name in ((P2_PRE, "g_pre_mix_2"), (P2_POST, "g_post_mix_2"), (P2_FPRE, "g_pre_ffn_2"), (P2_FPOST, "g_post_ffn_2"),
                      (P2_B, "b_ada_2")):
        v = a[name][0]
        out[:, off:off + v.size // P] = v.reshape(-1, P).T
    out[:, P2_LOGIT:P2_LOGIT + RET_HEADS] = a["ret_decay_fwd_2"][0][None, :]
    out[:, P2_LOGIT + RET_HEADS:] = a["ret_decay_bwd_2"][0][None, :]
    return out


def _rel():
    import numpy as np
    d = np.arange(REL)[None, :] - REL0 - np.arange(P)[:, None]
    many = sum(((d % dil == 0) & (abs(d) <= win // 2)).astype(np.float64) for win, dil in DIL_CONFIGS)
    lnm = np.where(many > 0, np.log(np.maximum(many, 1.0)), MASKED)
    return np.concatenate([d, lnm], axis=1).astype(np.float32)


def arrays_of(inputs):
    import numpy as np
    a = {k: np.asarray(v) for k, v in inputs.items()}
    return {
        "x": a["x"], "positions": a["positions"], "c": a["c_2"], "const": _const(), "counts": _counts(), "tiles": _tiles(a), "params": _params(a),
        "ada": _ada(a["w_ada_2"][0]), "params2": _params2(a), "rel": _rel(), "final_norm": a["final_norm"],
        "w_router": a["w_router_2"][0], "w_gate": a["w_gate_e_2"][0], "w_up": a["w_up_e_2"][0], "w_down": a["w_down_e_2"][0],
    }


def kernel(**inputs):
    import concourse.bacc as _bacc
    from concourse.bass_utils import run_bass_kernel_spmd as _run

    nc = _bacc.Bacc("TRN2", target_bir_lowering=False, num_devices=1)
    arrays = arrays_of(inputs)
    A = {k: nc.dram_tensor(f"in_{k}", v.shape, mybir.dt.from_np(v.dtype), kind="ExternalInput").ap() for k, v in arrays.items()}
    A["out"] = nc.dram_tensor("out_x", (1, S, D), F32, kind="ExternalOutput").ap()
    build(nc, A)
    r = _run(nc, [{f"in_{k}": v for k, v in arrays.items()}], core_ids=[0])
    return r.results[0]["out_x"]
```

```python
from contextlib import ExitStack

import concourse.bass as bass
from concourse import mybir

F32 = mybir.dt.float32
F32R = mybir.dt.float32r
I32 = mybir.dt.int32
ALU = mybir.AluOpType
ACT = mybir.ActivationFunctionType
AX = mybir.AxisListType

P = 128
S = 512
TC = S // P
D = 1024
DK = D // P
BANK = 512
EPS = 1e-6
GN_EPS = 1e-5

LAYERS = 2
HEADS, NOPE, ROPE, VDIM = 8, 64, 32, 64
QK = NOPE + ROPE
Q_LORA, KV_LORA = 384, 256
QC, KVC = Q_LORA // P, KV_LORA // P
ATT_SCALE = float(QK) ** -0.5
POOL_WINDOWS = (2, 4, 8, 16)
PAD = max(POOL_WINDOWS)
SG_HEADS, SG_DIM = 4, 64
SG_WIDTH = SG_HEADS * SG_DIM
D_FF = 2816
FF_CHUNKS = D_FF // P
GROUPS = 2
FG = FF_CHUNKS // GROUPS

TILE = 1024
N_V, N_POOL, N_Q, N_KV, N_KR, N_U = 0, 2, 4, 7, 9, 10
N_UQ, N_UK, N_UV, N_WO = 12, 16, 17, 18
N_FFN = 26
DOWN_TILES = -(-FG // 2)
GROUP_TILES = 2 * FG + 2 * DOWN_TILES
LAYER_TILES = N_FFN + GROUPS * GROUP_TILES
MIX2_T0 = LAYERS * LAYER_TILES
MIX2_TILES = 24
WO2_TILES = 8
N_TILES = MIX2_T0 + MIX2_TILES + WO2_TILES
UQ_W = 2 * QC * QK

ADA_TILES = 6 * D // (2 * P)
ADA_PER_GROUP = ADA_TILES // (LAYERS * GROUPS)

G_MIX, G_FFN, G_Q, G_KV, G_PS = 0, DK, 2 * DK, 2 * DK + QC, 2 * DK + QC + KVC
N_GAIN = G_PS + 2
PR_BS = N_GAIN + (N_GAIN % 2)
PR_SG = PR_BS + 2 * P
PR_WS = PR_SG + SG_WIDTH
PR_WP = PR_WS + SG_HEADS * P
N_PARAM = PR_WP + 2 * P

C_ID, C_ONE, C_ROT, C_FREQ = 0, P, 2 * P, 2 * P + ROPE
C_TRI = C_FREQ + 1
C_IOTA = C_TRI + P
C_I2 = C_IOTA + P
C_EPS = C_I2 + 64
C_GEPS = C_EPS + 1
N_CONST = C_GEPS + 1

RET_HEADS, RET_QK, RET_V = 4, 64, 128
DIL_HEADS, DIL_DIM = 8, 64
DIL_CONFIGS = ((128, 1), (512, 4), (2048, 16))
MASKED = -1e30
REL = 2 * S - P
REL0 = S - P
EXPERTS, CAPACITY, D_EXP = 16, 2 * S // 16, 2048
Q2 = {"rqk": 0, "rv": 4, "aqk": 8, "rg": 16, "av": 20, "wo": 24}
CAT_ORDER = (4, 5, 6, 7, 0, 1, 2, 3)
Y_BANK = (0, 1, 0, 6)
P2_PRE, P2_POST, P2_FPRE, P2_FPOST = 0, DK, 2 * DK, 3 * DK
P2_B = 4 * DK
P2_LOGIT = P2_B + 6 * DK
N_P2 = P2_LOGIT + 2 * RET_HEADS
SHIFT_M, SCALE_M, GATE_M, SHIFT_F, SCALE_F, GATE_F = (j * DK for j in range(6))

MT = 2 * D
E_TILES = 24
RAW_RING, SPLIT_RING = 6, 3
HALF_F = D_EXP // 2

X_LOADED = 5
X_PER_LAYER = 2 * TC * (1 + GROUPS)

TWO_PI = 6.283185307179586
PI2_A = 6.28125
PI2_B = 0.0019350051879882812
PI2_C = TWO_PI - PI2_A - PI2_B
MAGIC = 12582912.0
PI_IN = 3.1415925


def build(nc, A):
    ctx = ExitStack()
    with ctx:
        def sb(name, shape, dt=F32, where=None):
            return (where or ctx).enter_context(nc.sbuf_tensor(name, shape, dt))

        names = (
            "const_in x_in counts_in cbc_in raw_in0 raw_in1 hi_done lo_done tile_used params_in params_free "
            "pos_in trig_arg ada_in ada_used silu_c x_upd nss nsum nrt xn_done tr_done hn_hi hn_lo "
            "v_out vsq_done vss_done proj_out ssq_done rt_done cn_done c_hi c_lo vn_ready pool_ready "
            "pmm_done sg_done sgr mix_hi mix_lo qe_done q_raw rot_done q_rope k_done k_out v2_out s_done "
            "nm_done p_done tr2_done pts_done av_done a_out at_done silu_done fr_done fhi flo out_done p2_in "
            "mods_out fn_in rel_in diag_done rows_done rows_out sg_in sg_exp xf_done y_ready tmb hib lob pj2 rv_out "
            "rg_out av_out e_arg e_tab tab_free abs_done tab_ready rs_done dec_done y_done gn_var gn_rt yn "
            "ret_out s2_done nm2 p2_done tr3 pts2 av2 a2_out ct_done mh ml post_ss post_rt post_r t_ready "
            "x2_upd x2_own h_done hT_done hT_out wr_in lg_done lg_out lg_turned lg_sh back_done h_out "
            "h_split lg_exp aff_done affT thr_d thr_bc ge_done pre_done moe_hi moe_lo moe_used y_out "
            "gate_out up_out gate_t up_t sc_done sc_add sgT sg_ready silu_m hf_m hhi hlo g2_ready gg_ready "
            "gat_done gat_out x_turned x_done acc_zero moe_free fin_ss fin_out "
        ).split()
        names += [f"moe_in{i}" for i in range(RAW_RING)]
        sem = {n: ctx.enter_context(nc.semaphore(n)) for n in names}
        bank = [ctx.enter_context(nc.psum_tensor(f"bank{i}", [P, BANK], F32)) for i in range(8)]

        const = sb("const", [P, N_CONST])
        ident, ones = const[:, C_ID:C_ID + P], const[:, C_ONE:C_ONE + P]
        x = sb("x", [P, TC, D])
        hTh, hTl = sb("hTh", [P, DK, S], F32R), sb("hTl", [P, DK, S], F32R)
        raw_t, whi_t, wlo_t = sb("raw_t", [P, MT]), sb("whi_t", [P, MT], F32R), sb("wlo_t", [P, MT], F32R)
        raw, whi, wlo = ([t[:, i * TILE:(i + 1) * TILE] for i in range(2)] for t in (raw_t, whi_t, wlo_t))
        junk = sb("junk", [P, D])
        stats = sb("stats", [P, 64])
        mods = sb("mods", [P, 6 * DK])
        p2 = sb("p2", [P, N_P2])

        b1 = ExitStack()
        param = sb("param", [P, N_PARAM], where=b1)
        trig = sb("trig", [P, 2, S], where=b1)
        ada = sb("ada", [P, 2, D], where=b1)
        angles = sb("angles", [P, 2, S], where=b1)
        cbc = sb("cbc", [P, D], where=b1)
        ada_sum = sb("ada_sum", [P, 2 * ADA_PER_GROUP], where=b1)
        cnt = sb("cnt", [P, 2, S], where=b1)
        vstat = sb("vstat", [P, 3, TC * SG_HEADS], where=b1)
        astat = sb("astat", [P, 4, HEADS * TC], where=b1)
        xn = sb("xn", [P, TC * D], where=b1)
        with ExitStack() as mix_scope:
            craw = sb("craw", [P, QC + KVC, S], where=mix_scope)
            ch = sb("ch", [P, QC + KVC, S], F32R, where=mix_scope)
            cl = sb("cl", [P, QC + KVC, S], F32R, where=mix_scope)
            rbc = sb("rbc", [P, 2, S], where=mix_scope)
            qk = sb("qk", [P, 2 * HEADS * S], where=mix_scope)
            vt = sb("vt", [P, TC, HEADS * VDIM], where=mix_scope)
            uT = sb("uT", [P, 2, S], where=mix_scope)
            krw = sb("krw", [P, S], where=mix_scope)
        with ExitStack() as ffn_scope:
            fTh = sb("fTh", [P, FG, S], F32R, where=ffn_scope)
            fTl = sb("fTl", [P, FG, S], F32R, where=ffn_scope)
            sgr = sb("sgr_t", [P, 2, S], where=ffn_scope)
            fr = sb("fr", [P, 2, S], where=ffn_scope)
        b1.close()
        rows = sb("rows", [P, 2, D])
        with ExitStack() as b2:
            rqk = sb("rqk", [P, 4, S], where=b2)
            aqk = sb("aqk", [P, 8, S], where=b2)
            avt = sb("avt", [P, TC, S], where=b2)
            rvt = sb("rvt", [P, TC, S], where=b2)
            rgt = sb("rgt", [P, TC, S], where=b2)
            xh2 = sb("xh2", [P, TC * D], where=b2)
            cat = sb("cat", [P, TC, D], where=b2)
            tab = sb("tab", [P, 2, REL], where=b2)
            rel = sb("rel", [P, 2 * REL], where=b2)
            sm = sb("sm", [P, 2, S], where=b2)
            prob2_t = sb("prob2", [P, 4, S], where=b2)
            decay_lg = sb("decay_lg", [P, 8, 2 * RET_HEADS], where=b2)
            gn = sb("gn", [P, TC * 6 + TC * 2 + 2 * TC], where=b2)
            ast2 = sb("ast2", [P, 4, DIL_HEADS * TC], where=b2)
            st2 = sb("st2", [P, 16], where=b2)
        with ExitStack() as b3:
            moe_raw = [sb(f"mraw{i}", [P, MT], where=b3) for i in range(RAW_RING - 1)] + [raw_t]
            h_hi = [sb(f"h_hi{i}", [P, D], F32R, where=b3) for i in range(TC)]
            h_lo = [sb(f"h_lo{i}", [P, D], F32R, where=b3) for i in range(TC - 1)]
            acc = sb("acc", [P, TC, D], where=b3)
            moe_hi = [whi_t] + [sb(f"mhi{i}", [P, MT], F32R, where=b3) for i in range(SPLIT_RING - 1)]
            asb = sb("asb", [P, 2, HALF_F], where=b3)
            sgl = sb("sgl", [P, S], where=b3)
            hf = sb("hf", [P, S], where=b3)
            hot = sb("hot", [P, TC, 3 * 64], F32R, where=b3)
            gg2 = sb("gg2", [P, TC, P], where=b3)
            sgt = sb("sgt", [P, S], where=b3)
            aff = sb("aff", [P, TC, EXPERTS], where=b3)
            affe = sb("affe", [P, (EXPERTS + 1) * TC], where=b3)
            slots = sb("slots", [P, (EXPERTS + 1) * TC], where=b3)
            cur = sb("cur", [P, 2, TC], where=b3)
        hT_flat = hTh[:, :, :].rearrange("p k t -> p (k t)")
        lo_flat = hTl[:, :, :].rearrange("p k t -> p (k t)")
        xTe = hT_flat[:, 0:DK * P].rearrange("p (k t) -> p k t", t=P)
        hTe = hT_flat[:, DK * P:3 * DK * P].rearrange("p (k t) -> p k t", t=P)
        moe_lo = [wlo_t[:, :], lo_flat[:, 0:MT], lo_flat[:, MT:2 * MT]]
        h_lo.append(hT_flat[:, 3 * DK * P:4 * DK * P])
        ysb, gathered = rows[:, 0, :], junk
        hn = [asb[:, 0, :], asb[:, 1, :], ysb, junk[:, :]]
        wr = hf[:, 0:DK * EXPERTS].rearrange("p (k e) -> p k e", e=EXPERTS)
        rt_s = sgl[:, :].rearrange("p (r i e) -> p r i e", i=TC, e=EXPERTS)
        offset = rt_s[:, 6:8]
        hTf = acc[:, :, :].rearrange("p i d -> p (i d)").rearrange("p (k t) -> p k t", t=S)
        top = ysb[0:EXPERTS, 0:S]
        top8 = ysb[0:EXPERTS, S:S + 64]
        dthr = ysb[0:EXPERTS, S + 64:S + 64 + EXPERTS]
        diag = ada[:, :, :].rearrange("p r (k n) -> p (r k) n", n=P)
        decayed = [xh2[:, r * TC * S:(r + 1) * TC * S].rearrange("p (j t) -> p j t", t=S) for r in range(2)]
        xh4 = xh2[:, :].rearrange("p (i d) -> p i d", i=TC)
        xb4 = cat
        prob2 = [prob2_t[:, r, :] for r in range(2)]
        probT2 = [prob2_t[:, 2 + r, :] for r in range(2)]
        delta, lnm = rel[:, 0:REL], rel[:, REL:2 * REL]
        bst = gn[:, 0:6 * TC].rearrange("p (i s) -> p i s", s=6)
        mv = gn[:, 6 * TC:8 * TC].rearrange("p (i s) -> p i s", s=2)
        gr = gn[:, 8 * TC:10 * TC]

        ROUND = (("w_gate", 1, 0), ("w_up", 1, 0), ("w_down", 0, 0), ("w_gate", 0, 1), ("w_up", 0, 1), ("w_down", 1, 0))
        NEXT0, NEXT1 = 12, 20
        HEAD_TILES = NEXT1 - NEXT0
        SCATTER_BANKS = (4, 5, 6, 7)
        EARLY = SPLIT_RING
        OPENING, LAST = -1, EXPERTS - 1

        def is_round(e, which):
            return type(e) is int and e == which

        def round_tile(e, n):
            if is_round(e, OPENING):
                return NEXT0 <= n < NEXT1, n - NEXT0, n - NEXT0
            if is_round(e, LAST):
                m = n if n < NEXT0 else n - HEAD_TILES
                return not NEXT0 <= n < NEXT1, HEAD_TILES + LAST * E_TILES + m, HEAD_TILES + m
            return True, HEAD_TILES + e * E_TILES + n, HEAD_TILES + n

        def rounds(eng, steps):
            steps(OPENING)
            with eng.Fori(0, LAST) as e:
                steps(e)
            steps(LAST)

        def by_feature(n):
            return n if n < Q2["rv"] else n - Q2["aqk"] + 4 if Q2["aqk"] <= n < Q2["rg"] else None

        def rel_cols(i):
            return slice(REL0 - i * P, REL0 - i * P + S)

        xn4 = xn[:, :].rearrange("p (i d) -> p i d", i=TC)
        csq = xn[:, 0:(QC + KVC) * S].rearrange("p (c t) -> p c t", t=S)
        prob = [xn[:, r * S:(r + 1) * S] for r in range(2)]
        probT = [xn[:, (2 + r) * S:(3 + r) * S] for r in range(2)]
        att = xn[:, 4 * S:8 * S].rearrange("p (i n) -> p i n", i=TC)
        qT = qk[:, 0:HEADS * S].rearrange("p (h t) -> p h t", t=S)
        kT = qk[:, HEADS * S:].rearrange("p (h t) -> p h t", t=S)
        W2 = S + 2 * PAD
        hp = qk[:, 0:2 * W2].rearrange("p (c t) -> p c t", c=2)
        s2 = qk[:, 2 * W2:4 * W2].rearrange("p (c t) -> p c t", c=2)
        s4 = qk[:, 4 * W2:6 * W2].rearrange("p (c t) -> p c t", c=2)
        s8 = qk[:, 6 * W2:7 * W2]
        o = 7 * W2
        pooled = qk[:, o:o + 2 * S].rearrange("p (c t) -> p c t", c=2)
        vz = qk[:, o + 2 * S:o + 4 * S].rearrange("p (i n) -> p i n", i=TC)
        vsq = qk[:, o + 4 * S:o + 6 * S].rearrange("p (i n) -> p i n", i=TC)
        assert o + 6 * S <= 2 * HEADS * S
        vn = junk[:, :].rearrange("p (i n) -> p i n", i=TC)
        wsT = param[:, PR_WS:PR_WP].rearrange("p (g n) -> p g n", g=SG_HEADS)
        wp_bd = param[:, PR_WP:N_PARAM].rearrange("p (c n) -> p c n", c=2)

        def gain(k):
            return param[:, k:k + 1]

        def tiles_before(l, g, n):
            return l * LAYER_TILES + g * GROUP_TILES + n, l * (LAYER_TILES // 2) + g * (GROUP_TILES // 2) + n // 2

        def tile_width(n):
            if N_UQ <= n < N_UK:
                return UQ_W
            if n >= N_FFN and (n - N_FFN) % GROUP_TILES >= 2 * FG:
                q = ((n - N_FFN) % GROUP_TILES - 2 * FG) % DOWN_TILES
                return min(2, FG - 2 * q) * BANK
            return TILE

        block = ctx.enter_context(nc.Block())

        @block.sync
        def _(sp):
            sp.dma_start(x[:, :, :], A["x"].rearrange("b (i p) d -> p (b i) d", p=P)).then_inc(sem["x_in"], 16)
            sp.dma_start(const[:, :], A["const"]).then_inc(sem["const_in"], 16)
            sp.dma_start(cnt[:, :, :], A["counts"]).then_inc(sem["counts_in"], 16)

            def load(l, g, n):
                before, pair = tiles_before(l, g, n)
                w = tile_width(n)
                sp.wait_ge(sem["lo_done"], before + 1)
                sp.dma_start(raw[n % 2][:, 0:w], A["tiles"][bass.ds(before, 1), :, 0:w].rearrange("a p n -> p (a n)"))\
                    .then_inc(sem[f"raw_in{n % 2}"], 16)

            with sp.Fori(0, LAYERS) as l:
                for n in range(N_FFN):
                    load(l, 0, n)
                with sp.Fori(0, GROUPS) as g:
                    for n in range(N_FFN, N_FFN + GROUP_TILES):
                        load(l, g, n)
            for t in range(MIX2_T0, N_TILES):
                sp.wait_ge(sem["lo_done"], t + 1)
                sp.dma_start(raw[t % 2], A["tiles"][t]).then_inc(sem[f"raw_in{t % 2}"], 16)
            sp.wait_ge(sem["moe_free"], 1)
            def expert_loads(e):
                for n in range(E_TILES):
                    there, before, c = round_tile(e, n)
                    if not there:
                        continue
                    sp.wait_ge(sem["moe_lo"], before + 1)
                    if is_round(e, OPENING) and c == RAW_RING - 1:
                        sp.wait_ge(sem["lo_done"], N_TILES + 2)
                    name, half, ahead = ROUND[n // 4]
                    q = n % 4 + (4 * half if name == "w_down" else 0)
                    rows_of = D_EXP if name == "w_down" else D
                    cols = slice(0, D) if name == "w_down" else slice(half * HALF_F, (half + 1) * HALF_F)
                    r0 = (e + ahead) * rows_of + q * 256
                    r = slice(r0, r0 + 256) if type(e) is int else bass.ds(r0, 256)
                    sp.dma_start(moe_raw[c % RAW_RING][:, :].rearrange("p (c f) -> p c f", c=2),
                                 A[name].rearrange("e k f -> (e k) f")[r, cols].rearrange("(c p) f -> p c f", p=P))\
                        .then_inc(sem[f"moe_in{c % RAW_RING}"], 16)

            rounds(sp, expert_loads)
            for i in range(TC):
                sp.wait_ge(sem["fin_out"], i + 1)
                sp.dma_start(A["out"][0, i * P:(i + 1) * P, :], x[:, i, :]).then_inc(sem["out_done"], 16)
            sp.wait_ge(sem["out_done"], 16 * TC)

        @block.scalar
        def _(act):
            def split(l, g, n):
                before, pair = tiles_before(l, g, n)
                s, w = n % 2, tile_width(n)
                act.wait_ge(sem[f"raw_in{s}"], (pair + 1) * 16)
                act.wait_ge(sem["tile_used"], before + 1)
                nc.scalar.activation(whi[s][:, 0:w], raw[s][:, 0:w], ACT.Copy).then_inc(sem["hi_done"], 1)

            def used(l, g, n):
                act.wait_ge(sem["tile_used"], tiles_before(l, g, n)[0] + 3)

            def squares(half, updates):
                for i in range(TC):
                    act.drain()
                    act.wait_ge(sem["x_upd"], updates + i + 1)
                    last = nc.scalar.activation(junk[:, 0:BANK], x[:, i, half * BANK:(half + 1) * BANK], ACT.Square,
                                                accum_out=stats[:, 24 * half + i:24 * half + i + 1])
                return last

            def norm_root(nn, updates):
                nc.scalar.activation(stats[:, 60:61], const[:, C_EPS:C_EPS + 1], ACT.Sqrt)
                squares(1, updates).then_inc(sem["nss"], 1)
                act.wait_ge(sem["nsum"], nn + 1)
                nc.scalar.activation(stats[:, 4:8], stats[:, 28:32], ACT.Sqrt, scale=1.0 / D,
                                     bias=const[:, C_EPS:C_EPS + 1]).then_inc(sem["nrt"], 1)

            def norm_hi(nn, g0):
                for k in range(DK):
                    act.wait_ge(sem["tr_done"], nn * DK + k + 1)
                    nc.scalar.activation(hTh[:, k, :], bank[4 + k % 4][:, :], ACT.Copy, scale=gain(g0 + k))\
                        .then_inc(sem["hn_hi"], 1)

            act.wait_ge(sem["const_in"], 16)
            squares(0, 1)
            act.wait_ge(sem["cbc_in"], 16)
            nc.scalar.activation(cbc[:, :], cbc[:, :], ACT.Silu).then_inc(sem["silu_c"], 1)
            split(0, 0, 0)
            with act.Fori(0, LAYERS) as l:
                norm_root(l * 2, l * X_PER_LAYER + X_LOADED - TC)
                act.wait_ge(sem["params_in"], l * 16 + 16)
                norm_hi(l * 2, G_MIX)
                split(l, 0, 1)
                used(l, 0, 0)
                split(l, 0, 2)
                used(l, 0, 1)
                for i in range(TC):
                    nc.scalar.activation(vz[:, i, :], bank[i][:, 0:SG_WIDTH], ACT.Gelu_apprx_tanh).then_inc(sem["v_out"], 1)
                for n in range(N_POOL, N_UQ):
                    c = n - N_POOL
                    b = bank[4 + c % 4]
                    split(l, 0, n + 1)
                    if n == N_Q + 1:
                        act.wait_ge(sem["trig_arg"], 1)
                        for r in range(2):
                            nc.scalar.activation(trig[64:96, r, :], angles[64:96, r, :], ACT.Sin)
                    if n == N_U:
                        act.wait_ge(sem["ssq_done"], l * 2 + 2)
                        nc.scalar.activation(rbc[:, 0, :], bank[0][:, :], ACT.Sqrt, scale=1.0 / Q_LORA,
                                             bias=const[:, C_EPS:C_EPS + 1]).then_inc(sem["rt_done"], 1)
                        nc.scalar.activation(rbc[:, 1, :], bank[1][:, :], ACT.Sqrt, scale=1.0 / KV_LORA,
                                             bias=const[:, C_EPS:C_EPS + 1]).then_inc(sem["rt_done"], 1)
                        act.wait_ge(sem["vss_done"], l + 1)
                        nc.scalar.activation(vstat[:, 1, :], vstat[:, 0, :], ACT.Sqrt, scale=1.0 / SG_DIM,
                                             bias=const[:, C_EPS:C_EPS + 1]).then_inc(sem["rt_done"], 1)
                    used(l, 0, n)
                    if n < N_Q:
                        nc.scalar.activation(hp[:, c, PAD:PAD + S], b[:, :], ACT.Copy).then_inc(sem["proj_out"], 1)
                    elif n < N_KR:
                        nc.scalar.activation(craw[:, n - N_Q, :], b[:, :], ACT.Copy)
                        nc.scalar.activation(csq[:, n - N_Q, :], b[:, :], ACT.Square).then_inc(sem["proj_out"], 1)
                    elif n < N_U:
                        nc.scalar.activation(krw[0:QK, :], b[0:QK, :], ACT.Copy).then_inc(sem["proj_out"], 1)
                    else:
                        nc.scalar.activation(uT[:, n - N_U, :], b[:, :], ACT.Gelu_apprx_tanh).then_inc(sem["proj_out"], 1)
                act.wait_ge(sem["cn_done"], l + 1)
                for c in range(QC + KVC):
                    nc.scalar.activation(ch[:, c, :], craw[:, c, :], ACT.Copy, scale=gain(G_Q + c)).then_inc(sem["c_hi"], 1)
                for c in range(2):
                    act.wait_ge(sem["pmm_done"], l * 2 + c + 1)
                    nc.scalar.activation(hTh[:, 4 + c, :], bank[2 + c][:, :], ACT.Copy, scale=gain(G_PS + c))\
                        .then_inc(sem["mix_hi"], 1)
                for c in range(2):
                    act.wait_ge(sem["sgr"], l * 2 + c + 1)
                    nc.scalar.activation(hTh[:, 6 + c, :], craw[:, c, :], ACT.Copy).then_inc(sem["mix_hi"], 1)
                for m in range(HEADS // 2):
                    split(l, 0, N_UQ + m + 1)
                    act.wait_ge(sem["qe_done"], l * 4 + m + 1)
                    nc.scalar.activation(qT[0:QK, 2 * m, :], bank[4][0:QK, :], ACT.Copy).then_inc(sem["q_raw"], 1)
                    used(l, 0, N_UQ + m)
                    nc.scalar.activation(qT[0:QK, 2 * m + 1, :], bank[5][0:QK, :], ACT.Copy).then_inc(sem["q_raw"], 1)
                split(l, 0, N_UV)
                for j in range(HEADS // 2):
                    if j < 3:
                        act.wait_ge(sem["k_done"], l * 3 + j + 1)
                    else:
                        used(l, 0, N_UK)
                    nc.scalar.activation(kT[0:NOPE, 2 * j, :], bank[j][0:64, :], ACT.Copy)
                    nc.scalar.activation(kT[0:NOPE, 2 * j + 1, :], bank[j][64:128, :], ACT.Copy).then_inc(sem["k_out"], 1)
                split(l, 0, N_WO)
                for it in range(HEADS * TC + 1):
                    if it < HEADS * TC:
                        act.wait_ge(sem["nm_done"], l * 32 + it + 1)
                        if it >= 2:
                            act.wait_ge(sem["tr2_done"], l * 32 + it - 1)
                        nc.scalar.activation(prob[it % 2], bank[it % 2][:, :], ACT.Exp, bias=astat[:, 1, it:it + 1],
                                             scale=ATT_SCALE, accum_out=astat[:, 2, it:it + 1]).then_inc(sem["p_done"], 1)
                    if it >= 1:
                        e = it - 1
                        act.wait_ge(sem["tr2_done"], l * 32 + e + 1)
                        if e >= 2:
                            act.wait_ge(sem["av_done"], l * 32 + e - 1)
                        nc.scalar.activation(probT[e % 2], bank[2 + e % 2][:, :], ACT.Copy).then_inc(sem["pts_done"], 1)
                for k in range(4):
                    if k == 2:
                        split(l, 0, N_WO + 1)
                    act.wait_ge(sem["at_done"], l * 4 + k + 1)
                    nc.scalar.activation(hTh[:, k, :], bank[6 + k % 2][:, :], ACT.Copy).then_inc(sem["mix_hi"], 1)
                for n in range(N_WO + 1, N_FFN):
                    split(l, 0, n + 1)
                    if n == N_WO + 5:
                        squares(0, l * X_PER_LAYER + X_LOADED)
                norm_root(l * 2 + 1, l * X_PER_LAYER + X_LOADED + TC)
                norm_hi(l * 2 + 1, G_FFN)
                with act.Fori(0, GROUPS) as g:
                    for j in range(FG):
                        n = N_FFN + 2 * j
                        split(l, g, n + 1)
                        used(l, g, n)
                        nc.scalar.activation(sgr[:, j % 2, :], bank[2 * (j % 2)][:, :], ACT.Silu).then_inc(sem["silu_done"], 1)
                        split(l, g, n + 2)
                        act.wait_ge(sem["fr_done"], (l * GROUPS + g) * FG + j + 1)
                        nc.scalar.activation(fTh[:, j, :], fr[:, j % 2, :], ACT.Copy).then_inc(sem["fhi"], 1)
                    for q in range(2 * DOWN_TILES):
                        n = N_FFN + 2 * FG + q
                        if q < 2 * DOWN_TILES - 1:
                            split(l, g, n + 1)
                        if q == DOWN_TILES + 1:
                            squares(0, l * X_PER_LAYER + g * (2 * TC) + X_LOADED + 2 * TC)
                    before, pair = tiles_before(l, g, N_FFN + GROUP_TILES)
                    act.wait_ge(sem["raw_in0"], (pair + 1) * 16)
                    act.wait_ge(sem["tile_used"], before + 1)
                    nc.scalar.activation(whi[0][:, :], raw[0][:, :], ACT.Copy).then_inc(sem["hi_done"], 1)

            def copy2(out, in_, name, **kw):
                nc.scalar.activation(out, in_, kw.pop("func", ACT.Copy), **kw).then_inc(sem[name], 1)

            def split2(n):
                t = MIX2_T0 + n
                act.wait_ge(sem[f"raw_in{t % 2}"], (t // 2 + 1) * 16)
                act.wait_ge(sem["tile_used"], t + 1)
                copy2(whi[t % 2], raw[t % 2], "hi_done")

            def used2(n):
                act.wait_ge(sem["tile_used"], MIX2_T0 + n + 3)

            nc.scalar.activation(stats[:, 60:61], const[:, C_EPS:C_EPS + 1], ACT.Sqrt)
            squares(1, LAYERS * X_PER_LAYER + X_LOADED - TC).then_inc(sem["nss"], 1)
            act.wait_ge(sem["nsum"], 5)
            nc.scalar.activation(stats[:, 4:8], stats[:, 28:32], ACT.Sqrt, scale=1.0 / D,
                                 bias=const[:, C_EPS:C_EPS + 1]).then_inc(sem["nrt"], 1)
            for i in range(TC):
                act.drain()
                act.wait_ge(sem["y_ready"], i + 1)
                last = nc.scalar.activation(junk[:, :], xh4[:, i, :], ACT.Square, accum_out=stats[:, 32 + i:33 + i])
            last.then_inc(sem["nss"], 1)
            act.wait_ge(sem["nsum"], 6)
            nc.scalar.activation(stats[:, 40:44], stats[:, 36:40], ACT.Sqrt, scale=1.0 / D,
                                 bias=const[:, C_EPS:C_EPS + 1]).then_inc(sem["nrt"], 1)
            act.wait_ge(sem["params_in"], 16 * (LAYERS + 1))
            for k in range(DK):
                act.wait_ge(sem["tmb"], k + 1)
                copy2(hTh[:, k, :], sm[:, k % 2, :], "hib")
                if k < 4:
                    act.wait_ge(sem["rows_done"], k // 2 + 1)
                    copy2(rows[:, k // 2, (k % 2) * BANK:(k % 2 + 1) * BANK], bank[4 + k][:, :], "rows_out")
            def expert_tile_hi(e, n):
                _, before, c = round_tile(e, n)
                s = c % RAW_RING
                in_before = c // RAW_RING + 1 + (0 if is_round(e, OPENING) else e * (E_TILES // RAW_RING))
                act.wait_ge(sem[f"moe_in{s}"], in_before * 16)
                act.wait_ge(sem["moe_used"], before + 1)
                copy2(moe_hi[c % SPLIT_RING][:, :], moe_raw[s][:, :], "moe_hi")

            act.wait_ge(sem["sg_in"], 1)
            copy2(decay_lg[:, 1, :], decay_lg[:, 0, :], "sg_exp", func=ACT.Exp, scale=-1.0)

            def table(h):
                act.wait_ge(sem["e_arg"], h + 1)
                copy2(tab[:, h % 2, :], tab[:, h % 2, :], "e_tab", func=ACT.Exp)

            def group_norm_root(h):
                act.wait_ge(sem["gn_var"], h + 1)
                copy2(gr[:, 0:TC], mv[:, :, 1], "gn_rt", func=ACT.Sqrt, bias=const[:, C_GEPS:C_GEPS + 1])

            for n in range(Q2["wo"]):
                split2(n + 1)
                f = by_feature(n)
                if f is not None:
                    used2(n)
                    dst = rqk[:, f, :] if f < 4 else aqk[:, f - 4, :]
                    scale = 1.0 if f < 2 or f >= 8 else RET_QK ** -0.5 if f < 4 else DIL_DIM ** -0.5
                    copy2(dst, bank[4 + f % 2][:, :], "pj2", scale=scale)
                if n == 4:
                    table(0)
                    table(1)
                elif n == 12:
                    table(2)
                elif n == 13:
                    group_norm_root(0)
                elif n == 16:
                    table(3)
                elif n == 20:
                    used2(Q2["av"] - 1)
                    for i in range(TC):
                        copy2(rgt[:, i, :], bank[2 + i][:, :], "rg_out", func=ACT.Silu)
                    group_norm_root(1)
                elif n == 22:
                    group_norm_root(2)
            for it in range(DIL_HEADS * TC + 1):
                if it < DIL_HEADS * TC:
                    act.wait_ge(sem["nm2"], it + 1)
                    if it >= 2:
                        act.wait_ge(sem["tr3"], it - 1)
                    copy2(prob2[it % 2], sm[:, it % 2, :], "p2_done", func=ACT.Exp, bias=ast2[:, 1, it:it + 1],
                          accum_out=ast2[:, 2, it:it + 1])
                if it >= 1:
                    act.wait_ge(sem["tr3"], it)
                    if it >= 3:
                        act.wait_ge(sem["av2"], it - 2)
                    copy2(probT2[(it - 1) % 2], bank[2 + (it - 1) % 2][:, :], "pts2")
            group_norm_root(3)
            for c, k in enumerate(CAT_ORDER):
                act.wait_ge(sem["ct_done"], c + 1)
                copy2(hTh[:, k, :], bank[4 + c % 2][:, :], "mh")
            for half in range(2):
                for q in range(4):
                    n = Q2["wo"] + 4 * half + q
                    if n + 1 < MIX2_TILES + WO2_TILES:
                        split2(n + 1)
                used2(Q2["wo"] + 4 * half + 3)
                for i in range(TC):
                    act.drain()
                    last = nc.scalar.activation(junk[:, 0:BANK], bank[4 * half + i][:, :], ACT.Square,
                                                accum_out=st2[:, 4 * half + i:4 * half + i + 1])
            last.then_inc(sem["post_ss"], 1)
            act.wait_ge(sem["post_r"], 1)
            copy2(st2[:, 4:8], st2[:, 0:4], "post_rt", func=ACT.Sqrt, scale=1.0 / D, bias=const[:, C_EPS:C_EPS + 1])
            for i in range(TC):
                act.drain()
                act.wait_ge(sem["x2_upd"], i + 1)
                act.wait_ge(sem["x2_own"], i + 1)
                nc.scalar.activation(junk[:, :], x[:, i, :], ACT.Square, accum_out=stats[:, i:i + 1])
            act.drain()
            nc.scalar.activation(stats[:, 4:8], stats[:, 0:4], ACT.Sqrt, scale=1.0 / D,
                                 bias=const[:, C_EPS:C_EPS + 1]).then_inc(sem["nrt"], 1)
            expert_tile_hi(OPENING, NEXT0)
            expert_tile_hi(OPENING, NEXT0 + 1)
            for k in range(DK):
                act.wait_ge(sem["hT_done"], k + 1)
                copy2(hTf[:, k, :], bank[k % 4][:, :], "hT_out", func=ACT.Identity, scale=mods[:, SCALE_F + k:SCALE_F + k + 1],
                      bias=mods[:, SHIFT_F + k:SHIFT_F + k + 1])
            act.wait_ge(sem["lg_done"], 1)
            copy2(top, bank[4][0:EXPERTS, :], "lg_out")
            expert_tile_hi(OPENING, NEXT0 + 2)
            act.wait_ge(sem["lg_sh"], 1)
            copy2(rt_s[:, 0, :, :], rt_s[:, 0, :, :], "lg_exp", func=ACT.Exp)

            for i in range(TC):
                act.wait_ge(sem["back_done"], i + 1)
                if i >= 2:
                    act.wait_ge(sem["h_split"], i - 1)
                for b in range(2):
                    c = slice(b * BANK, (b + 1) * BANK)
                    nc.scalar.activation(asb[:, i % 2, c], bank[2 * (i % 2) + b][:, :], ACT.Copy)
                    last = nc.scalar.activation(h_hi[i][:, c], bank[2 * (i % 2) + b][:, :], ACT.Copy)
                last.then_inc(sem["h_out"], 1)

            def stash_tokens(value):
                act.wait_ge(sem["gat_done"], value)
                for w in range(2):
                    last = nc.scalar.activation(gathered[:, w * BANK:(w + 1) * BANK], bank[2 + w][:, :], ACT.Copy)
                last.then_inc(sem["gat_out"], 1)
                act.drain()

            def new_tokens(value):
                act.wait_ge(sem["x_turned"], value)
                for b in range(2):
                    last = nc.scalar.activation(xTe[:, 4 * b:4 * b + 4, :], bank[b][:, :].rearrange("p (k t) -> p k t", t=P), ACT.Copy)
                last.then_inc(sem["x_done"], 1)

            def evac(dst, b0, name, used_tiles):
                act.wait_ge(sem["moe_used"], used_tiles + SPLIT_RING)
                for b in range(2):
                    last = nc.scalar.activation(dst[:, b * BANK:(b + 1) * BANK], bank[b0 + b][:, :], ACT.Copy)
                last.then_inc(sem[name], 1)

            def silu_gate(value):
                act.wait_ge(sem["gate_t"], value)
                copy2(sgl[:, :], bank[6][:, :], "silu_m", func=ACT.Silu)

            def h_high(r, value):
                act.wait_ge(sem["hf_m"], value)
                copy2(hTe[:, 8 * r:8 * r + 8, 0:64], hf[:, :].rearrange("p (k t) -> p k t", t=64), "hhi")

            def expert_hi(e):
                this, ahead = not is_round(e, OPENING), not is_round(e, LAST)
                for n in range(0 if this else NEXT0, E_TILES):
                    if round_tile(e, n)[0] and not (is_round(e, OPENING) and n < NEXT0 + EARLY):
                        expert_tile_hi(e, n)
                    if n == 2:
                        evac(ysb, 4, "y_out", HEAD_TILES + e * E_TILES)
                    elif n == 3:
                        if ahead:
                            stash_tokens(e + 2)
                    elif n == 4:
                        h_high(0, 2 * e + 1)
                    elif n == 6:
                        evac(asb[:, 0, :], 0, "gate_out", round_tile(e, 4)[1])
                    elif n == 10:
                        evac(asb[:, 1, :], 2, "up_out", round_tile(e, 8)[1])
                        if ahead:
                            new_tokens(e + 2)
                    elif n == 13 and this:
                        silu_gate(2 * e + 2)
                    elif n == 16 and this:
                        h_high(1, 2 * e + 2)
                    elif n == 18:
                        if this:
                            act.wait_ge(sem["sgT"], e + 1)
                            copy2(sgt[:, :], bank[7][:, :], "sg_ready")
                        if ahead:
                            evac(asb[:, 0, :], 0, "gate_out", round_tile(e, 16)[1])
                    elif n == 21 and ahead:
                        silu_gate(2 * e + 3)
                    elif n == 22 and ahead:
                        evac(asb[:, 1, :], 2, "up_out", round_tile(e, 19)[1] + 1)

            stash_tokens(1)
            new_tokens(1)
            rounds(act, expert_hi)
            evac(ysb, 4, "y_out", EXPERTS * E_TILES)
            nc.scalar.activation(stats[:, 60:61], const[:, C_EPS:C_EPS + 1], ACT.Sqrt)
            for which in range(2):
                act.wait_ge(sem["sc_add"], 2 * EXPERTS + 1 + which)
                for i in range(TC):
                    act.drain()
                    last = nc.scalar.activation(asb[:, 0, 0:BANK], acc[:, i, which * BANK:(which + 1) * BANK], ACT.Square,
                                                accum_out=stats[:, 12 * which + i:12 * which + i + 1])
            last.then_inc(sem["nss"], 1)
            act.wait_ge(sem["nsum"], 7)
            copy2(stats[:, 4:8], stats[:, 28:32], "fin_ss", func=ACT.Sqrt, scale=1.0 / D, bias=const[:, C_EPS:C_EPS + 1])

        @block.vector
        def _(dve):
            def split(l, g, n):
                before, _ = tiles_before(l, g, n)
                s, w = n % 2, tile_width(n)
                dve.wait_ge(sem["hi_done"], before + 1)
                nc.vector.tensor_tensor(wlo[s][:, 0:w], raw[s][:, 0:w], whi[s][:, 0:w].bitcast(F32), ALU.subtract)\
                    .then_inc(sem["lo_done"], 1)

            def used(l, g, n):
                dve.wait_ge(sem["tile_used"], tiles_before(l, g, n)[0] + 3)

            def norm_scale(nn):
                dve.wait_ge(sem["nss"], nn + 1)
                nc.vector.tensor_tensor(stats[:, 28:32], stats[:, 0:4], stats[:, 24:28], ALU.add).then_inc(sem["nsum"], 1)
                dve.wait_ge(sem["nrt"], nn + 1)
                nc.vector.reciprocal(stats[:, 8:12], stats[:, 4:8])
                dve.drain()
                for i in range(TC):
                    last = nc.vector.tensor_scalar(xn4[:, i, :], x[:, i, :], stats[:, 8 + i:9 + i], None, ALU.mult)
                last.then_inc(sem["xn_done"], 1)

            def norm_lo(nn, g0):
                for k in range(DK):
                    dve.wait_ge(sem["hn_hi"], nn * DK + k + 1)
                    nc.vector.scalar_tensor_tensor(out=hTl[:, k, :], in0=bank[4 + k % 4][:, :], scalar=gain(g0 + k),
                                                   in1=hTh[:, k, :].bitcast(F32), op0=ALU.mult, op1=ALU.subtract)\
                        .then_inc(sem["hn_lo"], 1)

            dve.sem_inc(sem["lo_done"], 2)
            dve.sem_inc(sem["moe_lo"], RAW_RING)
            dve.wait_ge(sem["x_in"], 16)
            dve.sem_inc(sem["x_upd"], X_LOADED)
            dve.sem_inc(sem["ada_used"], 1)
            split(0, 0, 0)
            with dve.Fori(0, LAYERS) as l:
                norm_scale(l * 2)
                norm_lo(l * 2, G_MIX)
                split(l, 0, 1)
                split(l, 0, 2)
                for n in range(N_POOL, N_UQ):
                    split(l, 0, n + 1)
                    if n == N_Q:
                        dve.wait_ge(sem["vsq_done"], l + 1)
                        nc.vector.tensor_reduce(vstat[:, 0, :], vsq.rearrange("p i (h e) -> p (i h) e", e=SG_DIM),
                                                AX.X, ALU.add).then_inc(sem["vss_done"], 1)
                    if n == N_U:
                        dve.wait_ge(sem["rt_done"], l * 3 + 3)
                        nc.vector.reciprocal(rbc[:, :, :], rbc[:, :, :])
                        nc.vector.reciprocal(vstat[:, 2, :], vstat[:, 1, :])
                        dve.drain()
                        nc.vector.tensor_tensor(craw[:, 0:QC, :], craw[:, 0:QC, :],
                                                rbc[:, 0:1, :].broadcast_to([P, QC, S]), ALU.mult)
                        nc.vector.tensor_tensor(craw[:, QC:, :], craw[:, QC:, :],
                                                rbc[:, 1:2, :].broadcast_to([P, KVC, S]), ALU.mult)\
                            .then_inc(sem["cn_done"], 1)
                        nc.vector.tensor_tensor(
                            vn.rearrange("p i (h e) -> p (i h) e", e=SG_DIM), vz.rearrange("p i (h e) -> p (i h) e", e=SG_DIM),
                            vstat[:, 2, :].rearrange("p (a b) -> p a b", b=1).broadcast_to([P, TC * SG_HEADS, SG_DIM]), ALU.mult)
                        dve.drain()
                        nc.vector.tensor_tensor(
                            vn, vn, param[:, PR_SG:PR_WS].rearrange("p (a n) -> p a n", a=1).broadcast_to([P, TC, SG_WIDTH]),
                            ALU.mult).then_inc(sem["vn_ready"], 1)
                for c in range(QC + KVC):
                    dve.wait_ge(sem["c_hi"], l * 5 + c + 1)
                    nc.vector.scalar_tensor_tensor(out=cl[:, c, :], in0=craw[:, c, :], scalar=gain(G_Q + c),
                                                   in1=ch[:, c, :].bitcast(F32), op0=ALU.mult, op1=ALU.subtract)\
                        .then_inc(sem["c_lo"], 1)
                for c in range(2):
                    dve.wait_ge(sem["mix_hi"], l * 8 + c + 1)
                    nc.vector.scalar_tensor_tensor(out=hTl[:, 4 + c, :], in0=bank[2 + c][:, :], scalar=gain(G_PS + c),
                                                   in1=hTh[:, 4 + c, :].bitcast(F32), op0=ALU.mult, op1=ALU.subtract)\
                        .then_inc(sem["mix_lo"], 1)
                dve.drain()
                dve.wait_ge(sem["proj_out"], l * 10 + 10)
                for c in range(2):
                    dve.wait_ge(sem["sg_done"], l * 2 + c + 1)
                    bias = param[:, PR_BS + c * P:PR_BS + (c + 1) * P].rearrange("p (a n) -> p a n", a=1)
                    v4 = lambda ap: ap.rearrange("p (i n) -> p i n", i=TC)
                    nc.vector.tensor_tensor(v4(craw[:, c, :]), v4(bank[c][:, :]), bias.broadcast_to([P, TC, P]), ALU.add)
                    dve.drain()
                    nc.vector.tensor_tensor(craw[:, c, :], craw[:, c, :], uT[:, c, :], ALU.mult).then_inc(sem["sgr"], 1)
                for c in range(2):
                    dve.wait_ge(sem["mix_hi"], l * 8 + c + 3)
                    nc.vector.tensor_tensor(hTl[:, 6 + c, :], craw[:, c, :], hTh[:, 6 + c, :].bitcast(F32), ALU.subtract)\
                        .then_inc(sem["mix_lo"], 1)

                def rope(h):
                    vec = qT[64:96, h, :] if h < HEADS else krw[64:96, :]
                    turned = craw[64:96, 2 + h % 2, :]
                    dve.wait_ge(sem["rot_done"], l * 9 + h + 1)
                    nc.vector.tensor_tensor(turned, bank[6 + h % 2][64:96, :], trig[64:96, 1, :], ALU.mult)
                    nc.vector.tensor_tensor(vec, vec, trig[64:96, 0, :], ALU.mult)
                    dve.drain()
                    last = nc.vector.tensor_tensor(vec, vec, turned, ALU.add)
                    if h == HEADS:
                        dve.drain()
                        last = nc.vector.tensor_copy(
                            kT[64:96, :, :], vec.rearrange("p (a t) -> p a t", a=1).broadcast_to([ROPE, HEADS, S]))
                    last.then_inc(sem["q_rope"], 1)
                    dve.drain()

                for m in range(HEADS // 2):
                    split(l, 0, N_UQ + m + 1)
                    if m:
                        rope(2 * m - 2)
                        rope(2 * m - 1)
                split(l, 0, N_UV)
                for h in range(HEADS - 2, HEADS + 1):
                    rope(h)
                split(l, 0, N_WO)
                used(l, 0, N_UV)
                for i in range(TC):
                    nc.vector.tensor_copy(vt[:, i, :], bank[4 + i][:, :]).then_inc(sem["v2_out"], 1)
                for it in range(HEADS * TC + 2):
                    if it < HEADS * TC:
                        dve.wait_ge(sem["s_done"], l * 32 + it + 1)
                        nc.vector.tensor_reduce(astat[:, 0, it:it + 1], bank[it % 2][:, :], AX.X, ALU.max)
                        dve.drain()
                        nc.vector.tensor_scalar(astat[:, 1, it:it + 1], astat[:, 0, it:it + 1], -ATT_SCALE, None, ALU.mult)\
                            .then_inc(sem["nm_done"], 1)
                    if it >= 2:
                        e = it - 2
                        h, i = e // TC, e % TC
                        dve.wait_ge(sem["av_done"], l * 32 + e + 1)
                        nc.vector.reciprocal(astat[:, 3, e:e + 1], astat[:, 2, e:e + 1])
                        dve.drain()
                        nc.vector.tensor_scalar(att[:, i, h * VDIM:(h + 1) * VDIM], bank[4 + e % 2][:, 0:VDIM],
                                                astat[:, 3, e:e + 1], None, ALU.mult).then_inc(sem["a_out"], 1)
                for k in range(4):
                    if k == 2:
                        split(l, 0, N_WO + 1)
                    dve.wait_ge(sem["mix_hi"], l * 8 + 5 + k)
                    nc.vector.tensor_tensor(hTl[:, k, :], bank[6 + k % 2][:, :], hTh[:, k, :].bitcast(F32), ALU.subtract)\
                        .then_inc(sem["mix_lo"], 1)

                def add_to_x(half, b0):
                    for i in range(TC):
                        cols = x[:, i, half * BANK:(half + 1) * BANK]
                        nc.vector.tensor_tensor(cols, bank[b0 + i][:, :], cols, ALU.add).then_inc(sem["x_upd"], 1)

                for half in range(2):
                    for n in range(N_WO + 4 * half, N_WO + 4 * half + 4):
                        if n > N_WO:
                            split(l, 0, n + 1)
                    used(l, 0, N_WO + 4 * half + 3)
                    add_to_x(half, 4 * half)
                dve.drain()
                norm_scale(l * 2 + 1)
                norm_lo(l * 2 + 1, G_FFN)
                dve.drain()
                dve.sem_inc(sem["params_free"], 1)
                with dve.Fori(0, GROUPS) as g:
                    lg = l * GROUPS + g
                    for j in range(FG):
                        n = N_FFN + 2 * j
                        split(l, g, n + 1)
                        if j < ADA_PER_GROUP:
                            dve.drain()
                            if j == 0:
                                dve.wait_ge(sem["silu_c"], 1)
                            dve.wait_ge(sem["ada_in"], (lg * ADA_PER_GROUP + j + 1) * 16)
                            for r in range(2):
                                if r:
                                    dve.drain()
                                last = nc.vector.tensor_tensor_reduce(
                                    out=junk[:, :], in0=ada[:, r, :], in1=cbc[:, :], scale=1.0, scalar=0.0, op0=ALU.mult,
                                    op1=ALU.add, accum_out=ada_sum[:, 2 * j + r:2 * j + r + 1])
                            last.then_inc(sem["ada_used"], 1)
                        split(l, g, n + 2)
                        used(l, g, n + 1)
                        dve.wait_ge(sem["silu_done"], lg * FG + j + 1)
                        nc.vector.tensor_tensor(fr[:, j % 2, :], sgr[:, j % 2, :], bank[2 * (j % 2) + 1][:, :], ALU.mult)\
                            .then_inc(sem["fr_done"], 1)
                        dve.wait_ge(sem["fhi"], lg * FG + j + 1)
                        nc.vector.tensor_tensor(fTl[:, j, :], fr[:, j % 2, :], fTh[:, j, :].bitcast(F32), ALU.subtract)\
                            .then_inc(sem["flo"], 1)
                    dve.drain()
                    nc.vector.tensor_copy(mods[:, bass.ds(lg * (2 * ADA_PER_GROUP), 2 * ADA_PER_GROUP)], ada_sum[:, :])\
                        .then_inc(sem["mods_out"], 1)
                    for q in range(2 * DOWN_TILES):
                        n = N_FFN + 2 * FG + q
                        if q < 2 * DOWN_TILES - 1:
                            split(l, g, n + 1)
                        if q % DOWN_TILES == DOWN_TILES - 1:
                            half = q // DOWN_TILES
                            used(l, g, n)
                            add_to_x(half, 4 - 4 * half)
                    dve.wait_ge(sem["hi_done"], tiles_before(l, g, N_FFN + GROUP_TILES)[0] + 1)
                    nc.vector.tensor_tensor(wlo[0][:, :], raw[0][:, :], whi[0][:, :].bitcast(F32), ALU.subtract)\
                        .then_inc(sem["lo_done"], 1)

            def diff2(out, a, hi, name, wait, value):
                dve.wait_ge(sem[wait], value)
                nc.vector.tensor_tensor(out, a, hi.bitcast(F32), ALU.subtract).then_inc(sem[name], 1)

            def split2(n):
                t = MIX2_T0 + n
                diff2(wlo[t % 2], raw[t % 2], whi[t % 2], "lo_done", "hi_done", t + 1)

            def used2(n):
                dve.wait_ge(sem["tile_used"], MIX2_T0 + n + 3)

            V = nc.vector
            dve.drain()
            dve.wait_ge(sem["fn_in"], 16)
            for i in range(TC):
                if i == 1:
                    dve.wait_ge(sem["nss"], 5)
                    V.tensor_tensor(stats[:, 28:32], stats[:, 0:4], stats[:, 24:28], ALU.add).then_inc(sem["nsum"], 1)
                V.tensor_tensor(xh4[:, i, :], x[:, i, :], cbc[:, :], ALU.mult).then_inc(sem["y_ready"], 1)
            dve.wait_ge(sem["nrt"], 5)
            V.reciprocal(stats[:, 8:12], stats[:, 4:8])
            dve.drain()
            dve.wait_ge(sem["nss"], 6)
            V.tensor_tensor(stats[:, 36:40], stats[:, 32:36], stats[:, 8:12], ALU.mult)
            dve.drain()
            V.tensor_tensor(stats[:, 36:40], stats[:, 36:40], stats[:, 8:12], ALU.mult).then_inc(sem["nsum"], 1)
            dve.wait_ge(sem["nrt"], 6)
            V.reciprocal(stats[:, 40:44], stats[:, 40:44])
            dve.drain()
            V.tensor_tensor(stats[:, 40:44], stats[:, 40:44], stats[:, 8:12], ALU.mult)
            dve.drain()
            for i in range(TC):
                last = V.tensor_scalar(xb4[:, i, :], xh4[:, i, :], stats[:, 40 + i:41 + i], None, ALU.mult)
            last.then_inc(sem["xn_done"], 1)
            dve.wait_ge(sem["diag_done"], 1)
            for k in range(DK):
                dve.wait_ge(sem["tr_done"], 4 * DK + k + 1)
                dve.drain()
                V.tensor_scalar(sm[:, k % 2, :], bank[k % 4][:, :], mods[:, SCALE_M + k:SCALE_M + k + 1],
                                mods[:, SHIFT_M + k:SHIFT_M + k + 1], ALU.mult, ALU.add).then_inc(sem["tmb"], 1)
                if k:
                    diff2(hTl[:, k - 1, :], sm[:, (k - 1) % 2, :], hTh[:, k - 1, :], "lob", "hib", k)
            diff2(hTl[:, DK - 1, :], sm[:, (DK - 1) % 2, :], hTh[:, DK - 1, :], "lob", "hib", DK)

            logit = p2[:, P2_LOGIT:P2_LOGIT + 2 * RET_HEADS]
            V.scalar_tensor_tensor(out=decay_lg[:, 0, :], in0=logit, scalar=-1.0, in1=logit, op0=ALU.mult, op1=ALU.max)\
                .then_inc(sem["sg_in"], 1)
            dve.wait_ge(sem["sg_exp"], 1)
            y, z, z2, ac = (decay_lg[:, r, :] for r in (1, 2, 3, 4))
            V.tensor_scalar(z, y, 2.0, None, ALU.add)
            dve.drain()
            V.reciprocal(z, z)
            dve.drain()
            V.tensor_tensor(z, z, y, ALU.mult)
            dve.drain()
            V.tensor_tensor(z2, z, z, ALU.mult)
            dve.drain()
            V.tensor_scalar(ac, z2, 1.0 / 17.0, None, ALU.mult)
            for k in (15, 13, 11, 9, 7, 5, 3):
                dve.drain()
                V.scalar_tensor_tensor(out=ac, in0=ac, scalar=1.0 / k, in1=z2, op0=ALU.add, op1=ALU.mult)
            dve.drain()
            V.scalar_tensor_tensor(out=ac, in0=ac, scalar=1.0, in1=z, op0=ALU.add, op1=ALU.mult)
            V.tensor_scalar(decay_lg[:, 5, :], logit, 0.0, None, ALU.min)
            dve.drain()
            V.scalar_tensor_tensor(out=decay_lg[:, 6, :], in0=ac, scalar=-2.0, in1=decay_lg[:, 5, :], op0=ALU.mult, op1=ALU.add)
            dve.drain()
            V.tensor_scalar(decay_lg[:, 7, :], decay_lg[:, 6, :], -1.0, None, ALU.mult)

            def table(h):
                dve.drain()
                V.tensor_scalar(tab[:, h % 2, :], delta, 0.0, decay_lg[:, 6, h:h + 1], ALU.max, ALU.mult)
                dve.drain()
                for a, b in ((0, S), (S, REL)):
                    V.tensor_scalar(junk[:, 0:b - a], delta[:, a:b], 0.0, decay_lg[:, 7, RET_HEADS + h:RET_HEADS + h + 1],
                                    ALU.min, ALU.mult)
                    dve.drain()
                    last = V.tensor_tensor(tab[:, h % 2, a:b], tab[:, h % 2, a:b], junk[:, 0:b - a], ALU.add)
                    dve.drain()
                dve.sem_inc(sem["e_arg"], 1)

            dve.wait_ge(sem["rel_in"], 16)
            def retention_scores(u):
                h, j = u // TC, u % TC
                if j == 0:
                    if h == 0:
                        dve.wait_ge(sem["xf_done"], 1)
                    dve.wait_ge(sem["e_tab"], h + 1)
                    if h >= 2:
                        dve.wait_ge(sem["y_done"], h - 1)
                dve.wait_ge(sem["rs_done"], u + 1)
                V.tensor_tensor(decayed[h % 2][:, j, :], bank[6 + u % 2][:, :], tab[:, h % 2, rel_cols(j)], ALU.mult)\
                    .then_inc(sem["dec_done"], 1)
                if j == TC - 1:
                    dve.drain()
                    dve.sem_inc(sem["tab_free"], 1)
                    if h + 2 < RET_HEADS:
                        table(h + 2)
                    if h + 2 == RET_HEADS:
                        V.scalar_tensor_tensor(out=delta, in0=delta, scalar=-1.0, in1=delta, op0=ALU.mult, op1=ALU.max)\
                            .then_inc(sem["abs_done"], 1)

            def group_norm_stats(h):
                dve.wait_ge(sem["y_done"], h + 1)
                dve.drain()
                for i in range(TC):
                    V.bn_stats(bst[:, i, :], bank[Y_BANK[h]][:, i * P:(i + 1) * P])
                dve.drain()
                for i in range(TC):
                    last = V.bn_aggr(mv[:, i, :], bst[:, i, :])
                last.then_inc(sem["gn_var"], 1)

            def group_norm(h):
                dve.wait_ge(sem["gn_rt"], h + 1)
                V.reciprocal(gr[:, TC:2 * TC], gr[:, 0:TC])
                dve.drain()
                for i in range(TC):
                    last = V.tensor_scalar(cat[:, i, h * RET_V:(h + 1) * RET_V], bank[Y_BANK[h]][:, i * P:(i + 1) * P],
                                           mv[:, i, 0:1], gr[:, TC + i:TC + i + 1], ALU.subtract, ALU.mult)
                last.then_inc(sem["yn"], 1)

            for n in range(Q2["wo"]):
                split2(n + 1)
                if n in (1, 2):
                    table(n - 1)
                elif n == Q2["aqk"] - 1:
                    used2(n)
                    for i in range(TC):
                        V.tensor_copy(rvt[:, i, :], bank[i][:, :]).then_inc(sem["rv_out"], 1)
                if n == 20:
                    group_norm_stats(1)
                if n >= Q2["aqk"]:
                    retention_scores(n - Q2["aqk"])
                if n == 13:
                    group_norm_stats(0)
                elif n == 14:
                    group_norm(0)
                elif n == 21:
                    group_norm(1)
                elif n == 22:
                    group_norm_stats(2)
            used2(Q2["wo"] - 1)
            for i in range(TC):
                V.tensor_copy(avt[:, i, :], bank[2 + i][:, :]).then_inc(sem["av_out"], 1)
            group_norm(2)
            for it in range(DIL_HEADS * TC + 2):
                if it < DIL_HEADS * TC:
                    h, i = it // TC, it % TC
                    if i == 0:
                        dve.wait_ge(sem["tab_ready"], h + 1)
                    dve.wait_ge(sem["s2_done"], it + 1)
                    if it >= 2:
                        dve.wait_ge(sem["p2_done"], it - 1)
                    V.tensor_tensor_reduce(out=sm[:, it % 2, :], in0=bank[it % 2][:, :], in1=tab[:, h % 2, rel_cols(i)],
                                           scale=1.0, scalar=-3e38, op0=ALU.add, op1=ALU.max, accum_out=ast2[:, 0, it:it + 1])
                    dve.drain()
                    V.tensor_scalar(ast2[:, 1, it:it + 1], ast2[:, 0, it:it + 1], -1.0, None, ALU.mult).then_inc(sem["nm2"], 1)
                    if i == TC - 1:
                        dve.sem_inc(sem["tab_free"], 1)
                if it == 4:
                    group_norm_stats(3)
                if it >= 2:
                    c = it - 2
                    h, i = c // TC, c % TC
                    dve.wait_ge(sem["av2"], c + 1)
                    V.reciprocal(ast2[:, 3, c:c + 1], ast2[:, 2, c:c + 1])
                    dve.drain()
                    o0 = RET_HEADS * RET_V + h * DIL_DIM
                    V.tensor_scalar(cat[:, i, o0:o0 + DIL_DIM], bank[4 + c % 2][:, 0:DIL_DIM], ast2[:, 3, c:c + 1], None, ALU.mult)\
                        .then_inc(sem["a2_out"], 1)
            group_norm(3)
            for c, k in enumerate(CAT_ORDER):
                diff2(hTl[:, k, :], bank[4 + c % 2][:, :], hTh[:, k, :], "ml", "mh", c + 1)
            for n in range(Q2["wo"] + 1, MIX2_TILES + WO2_TILES):
                split2(n)
            dve.wait_ge(sem["post_ss"], 1)
            V.tensor_tensor(st2[:, 0:4], st2[:, 0:4], st2[:, 4:8], ALU.add).then_inc(sem["post_r"], 1)
            dve.wait_ge(sem["post_rt"], 1)
            V.reciprocal(st2[:, 8:12], st2[:, 4:8])
            dve.drain()
            for p in range(2 * TC):
                i, half = p // 2, p % 2
                if half == 0 and i:
                    dve.wait_ge(sem["x2_upd"], i)
                if half and i:
                    dve.drain()
                V.scalar_tensor_tensor(out=sm[:, p % 2, :], in0=bank[4 * half + i][:, :], scalar=st2[:, 8 + i:9 + i],
                                       in1=rows[:, 0, half * BANK:(half + 1) * BANK], op0=ALU.mult, op1=ALU.mult)\
                    .then_inc(sem["t_ready"], 1)
                if half:
                    dve.drain()
                    part = x[:, i, BANK:2 * BANK]
                    V.tensor_tensor(part, part, sm[:, 1, :], ALU.add).then_inc(sem["x2_own"], 1)
            dve.wait_ge(sem["nrt"], 7)
            V.reciprocal(stats[:, 8:12], stats[:, 4:8])
            dve.drain()
            for i in range(TC):
                last = V.tensor_scalar(hn[i], x[:, i, :], stats[:, 8 + i:9 + i], None, ALU.mult)
            last.then_inc(sem["h_done"], 1)

            def expert_tile_lo(e, n):
                _, before, c = round_tile(e, n)
                dve.wait_ge(sem["moe_hi"], before + 1)
                V.tensor_tensor(moe_lo[c % SPLIT_RING], moe_raw[c % RAW_RING][:, :],
                                moe_hi[c % SPLIT_RING][:, :].bitcast(F32), ALU.subtract).then_inc(sem["moe_lo"], 1)

            expert_tile_lo(OPENING, NEXT0)
            expert_tile_lo(OPENING, NEXT0 + 1)
            V.memset(slots[:, EXPERTS * TC:], -1.0)
            V.memset(affe[:, EXPERTS * TC:], 0.0)
            V.memset(sgt[:, :], 0.0)
            V.memset(hot[:, :, :].bitcast(F32), 0.0)
            V.memset(offset[:, :, 0, :], 0.0)

            def over(ap, n):
                return ap.rearrange("p (i a) -> p i a", a=1).broadcast_to([P, TC, n])

            lgt = bank[5][:, 0:TC * EXPERTS].rearrange("p (i e) -> p i e", e=EXPERTS)
            ex = rt_s[:, 0, :, :]
            dve.wait_ge(sem["lg_turned"], 1)
            V.tensor_reduce(stats[:, 12:16], lgt, AX.X, ALU.max)
            dve.drain()
            V.tensor_tensor(ex, lgt, over(stats[:, 12:16], EXPERTS), ALU.subtract).then_inc(sem["lg_sh"], 1)
            dve.wait_ge(sem["lg_exp"], 1)
            V.tensor_reduce(stats[:, 16:20], ex, AX.X, ALU.add)
            dve.drain()
            V.reciprocal(stats[:, 20:24], stats[:, 16:20])
            dve.drain()
            V.tensor_tensor(aff[:, :, :], ex, over(stats[:, 20:24], EXPERTS), ALU.mult).then_inc(sem["aff_done"], 1)
            dve.wait_ge(sem["affT"], 1)
            V.tensor_copy(top, bank[7][0:EXPERTS, :])
            for r in range(CAPACITY // 8):
                dve.drain()
                V.max(top8[:, 8 * r:8 * r + 8], top)
                dve.drain()
                if r < CAPACITY // 8 - 1:
                    V.match_replace(top, top8[:, 8 * r:8 * r + 8], top, -1.0)
            V.tensor_scalar(dthr, const[0:EXPERTS, C_ID:C_ID + EXPERTS], top8[:, CAPACITY - 1:CAPACITY], None, ALU.mult)\
                .then_inc(sem["thr_d"], 1)
            ge = rt_s[:, 1:3, :, :]
            dve.wait_ge(sem["thr_bc"], 1)
            thr = bank[6][:, 0:EXPERTS].rearrange("p (a e) -> p a e", a=1).broadcast_to([P, TC, EXPERTS])
            V.tensor_tensor(ge[:, 0], aff[:, :, :], thr, ALU.is_gt)
            V.tensor_tensor(ge[:, 1], aff[:, :, :], thr, ALU.is_equal).then_inc(sem["ge_done"], 1)
            dve.wait_ge(sem["pre_done"], 1)
            sums = bank[4][:, 0:2 * P].rearrange("p (r w i e) -> p r w i e", r=2, w=2, i=TC)
            need = stats[:, 24:24 + EXPERTS]
            for i in range(1, TC):
                V.tensor_tensor(offset[:, :, i, :], sums[:, 1, :, i - 1, :], offset[:, :, i - 1, :], ALU.add)
                dve.drain()
            V.tensor_tensor(need, sums[:, 1, 0, TC - 1, :], offset[:, 0, TC - 1, :], ALU.add)
            dve.drain()
            V.tensor_tensor(offset[:, :, :, :], sums[:, 0], offset[:, :, :, :], ALU.add)
            before = offset
            V.tensor_scalar(need, need, -1.0, float(CAPACITY), ALU.mult, ALU.add)
            dve.drain()
            need4 = need.rearrange("p (a e) -> p a e", a=1).broadcast_to([P, TC, EXPERTS])
            V.tensor_tensor(rt_s[:, 3], before[:, 1], need4, ALU.is_lt)
            V.tensor_tensor(rt_s[:, 4], before[:, 1], need4, ALU.min)
            dve.drain()
            V.tensor_tensor(rt_s[:, 3], rt_s[:, 3], ge[:, 1], ALU.mult)
            V.tensor_tensor(rt_s[:, 4], before[:, 0], rt_s[:, 4], ALU.add)
            dve.drain()
            V.tensor_tensor(rt_s[:, 3], rt_s[:, 3], ge[:, 0], ALU.add)
            dve.drain()
            V.scalar_tensor_tensor(out=rt_s[:, 5], in0=rt_s[:, 4], scalar=1.0, in1=rt_s[:, 3], op0=ALU.add, op1=ALU.mult)
            dve.drain()
            by_e = lambda t: t[:, 0:EXPERTS * TC].rearrange("p (e i) -> p i e", i=TC)
            V.tensor_scalar(by_e(slots), rt_s[:, 5], 1.0, None, ALU.subtract)
            V.tensor_copy(by_e(affe), aff[:, :, :])
            dve.drain()
            dve.sem_inc(sem["sg_ready"], 1)

            def look_up(at):
                cols = slice(at * TC, (at + 1) * TC) if type(at) is int else bass.ds(at * TC, TC)
                V.tensor_copy(cur[:, 0, :], slots[:, cols])
                V.tensor_copy(cur[:, 1, :], affe[:, cols])
                dve.drain()
                V.tensor_tensor(hot[:, :, 64:128], const[:, C_IOTA:C_IOTA + 64].rearrange("p (a n) -> p a n", a=1)
                                .broadcast_to([P, TC, 64]), over(cur[:, 0, :], 64), ALU.is_equal).then_inc(sem["g2_ready"], 1)

            h3 = lambda ap: ap.rearrange("p (k t) -> p k t", t=64)

            def h_f32(value):
                dve.drain()
                dve.wait_ge(sem["silu_m"], value)
                dve.wait_ge(sem["up_t"], value)
                V.tensor_tensor(hf[:, :], sgl[:, :], bank[7][:, :], ALU.mult).then_inc(sem["hf_m"], 1)

            def h_low(r, value):
                dve.wait_ge(sem["hhi"], value)
                V.tensor_tensor(hTe[:, 8 * r:8 * r + 8, 64:128], h3(hf[:, :]), hTe[:, 8 * r:8 * r + 8, 0:64].bitcast(F32),
                                ALU.subtract).then_inc(sem["hlo"], 1)

            def add_scattered(which, value):
                dve.wait_ge(sem["sc_done"], value)
                for i, b in enumerate(SCATTER_BANKS):
                    part = acc[:, i, which * BANK:(which + 1) * BANK]
                    last = V.tensor_tensor(part, bank[b][:, :], part, ALU.add)
                last.then_inc(sem["sc_add"], 1)

            def expert_lo(e):
                this, ahead = not is_round(e, OPENING), not is_round(e, LAST)
                for n in range(0 if this else NEXT0, E_TILES):
                    if round_tile(e, n)[0] and not (is_round(e, OPENING) and n < NEXT0 + EARLY):
                        expert_tile_lo(e, n)
                    if n == 1:
                        h_f32(2 * e + 1)
                    elif n == 6:
                        h_low(0, 2 * e + 1)
                    elif n == 5:
                        add_scattered(0, 2 * e + 1)
                    elif n == 8:
                        add_scattered(1, 2 * e + 2)
                    elif n == 14 and this:
                        h_f32(2 * e + 2)
                    elif n == 17 and this:
                        h_low(1, 2 * e + 2)
                    elif n == 20 and ahead:
                        dve.wait_ge(sem["gat_done"], e + 2)
                        dve.wait_ge(sem["gg_ready"], e + 2)
                        look_up(e + 2)

            look_up(0)
            expert_tile_lo(OPENING, NEXT0 + 2)
            rounds(dve, expert_lo)
            scaled = [moe_raw[i // 2][:, (i % 2) * D:(i % 2 + 1) * D] for i in range(TC)]
            for which in range(2):
                add_scattered(which, EXPERTS * 2 + which + 1)
                dve.drain()
                c = slice(which * BANK, (which + 1) * BANK)
                for i in range(TC):
                    V.tensor_tensor(scaled[i][:, c], acc[:, i, c], rows[:, 1, c], ALU.mult)
            dve.wait_ge(sem["nss"], 7)
            V.tensor_tensor(stats[:, 28:32], stats[:, 0:4], stats[:, 12:16], ALU.add).then_inc(sem["nsum"], 1)
            dve.wait_ge(sem["fin_ss"], 1)
            V.reciprocal(stats[:, 8:12], stats[:, 4:8])
            dve.drain()
            for i in range(TC):
                V.scalar_tensor_tensor(out=x[:, i, :], in0=scaled[i], scalar=stats[:, 8 + i:9 + i], in1=x[:, i, :],
                                       op0=ALU.mult, op1=ALU.add).then_inc(sem["fin_out"], 1)

        @block.gpsimd
        def _(pool):
            R = slice(64, 96)
            pool.dma_start(angles[R, 0, :].bitcast(I32), A["positions"].broadcast_to([ROPE, S])).then_inc(sem["pos_in"], 16)
            pool.dma_start(cbc[:, :], A["c"].broadcast_to([P, D])).then_inc(sem["cbc_in"], 16)
            pool.dma_start(param[:, :], A["params"][0]).then_inc(sem["params_in"], 16)
            pool.dma_start(p2[:, :], A["params2"]).then_inc(sem["p2_in"], 16)
            pool.wait_ge(sem["pos_in"], 16)
            pool.wait_ge(sem["const_in"], 16)
            ang, turns, t2, product = rbc[R, 0, :], rbc[R, 1, :], krw[R, :], angles[R, 1, :]
            nc.gpsimd.tensor_copy(ang, angles[R, 0, :].bitcast(I32))
            pool.drain()
            nc.gpsimd.tensor_scalar(ang, ang, const[R, C_FREQ:C_FREQ + 1], None, ALU.mult)
            for r, quarter in ((0, 0.25), (1, 0.0)):
                pool.drain()
                nc.gpsimd.tensor_scalar(turns, ang, 1.0 / TWO_PI, quarter, ALU.mult, ALU.add)
                for part in (MAGIC, -MAGIC):
                    pool.drain()
                    nc.gpsimd.tensor_scalar(turns, turns, part, None, ALU.add)
                pool.drain()
                for part, rest in ((PI2_A, ang), (PI2_B, t2), (PI2_C, t2)):
                    nc.gpsimd.tensor_scalar(product, turns, -part, None, ALU.mult)
                    pool.drain()
                    nc.gpsimd.tensor_tensor(t2, product, rest, ALU.add)
                    pool.drain()
                nc.gpsimd.tensor_scalar(t2, t2, quarter * TWO_PI, PI_IN, ALU.add, ALU.min)
                pool.drain()
                last = nc.gpsimd.tensor_scalar(angles[R, r, :], t2, -PI_IN, None, ALU.max)
            last.then_inc(sem["trig_arg"], 1)
            pool.drain()
            pool.wait_ge(sem["counts_in"], 16)
            with pool.Fori(0, LAYERS) as l:
                pool.wait_ge(sem["v_out"], l * TC + TC)
                nc.gpsimd.tensor_tensor(vsq, vz, vz, ALU.mult).then_inc(sem["vsq_done"], 1)
                nc.gpsimd.memset(hp[:, :, 0:PAD], 0.0)
                nc.gpsimd.memset(hp[:, :, PAD + S:], 0.0)
                pool.drain()
                pool.wait_ge(sem["proj_out"], l * 10 + 2)
                nc.gpsimd.tensor_tensor(s2[:, :, 1:], hp[:, :, 0:W2 - 1], hp[:, :, 1:], ALU.add)
                pool.drain()
                nc.gpsimd.tensor_tensor(s4[:, :, 2:W2 - 1], s2[:, :, 1:W2 - 2], s2[:, :, 3:], ALU.add)
                pool.drain()
                nc.gpsimd.tensor_tensor(s8[:, 4:W2 - 3], s4[:, 1, 2:W2 - 5], s4[:, 1, 6:W2 - 1], ALU.add)
                pool.drain()
                lo, hi = slice(0, 64), slice(64, 128)
                mid = slice(PAD, PAD + S)
                pool.wait_ge(sem["const_in"], 16)
                nc.gpsimd.tensor_tensor(pooled[hi, 1, :], s8[hi, PAD - 4:PAD - 4 + S], s8[hi, PAD + 4:PAD + 4 + S], ALU.add)
                nc.gpsimd.tensor_tensor(pooled[lo, 0, :], s2[lo, 0, mid], cnt[lo, 0, :], ALU.mult)
                nc.gpsimd.tensor_tensor(pooled[hi, 0, :], s4[hi, 0, mid], cnt[hi, 0, :], ALU.mult)
                nc.gpsimd.tensor_tensor(pooled[lo, 1, :], s8[lo, mid], cnt[lo, 1, :], ALU.mult)
                pool.drain()
                nc.gpsimd.tensor_tensor(pooled[hi, 1, :], pooled[hi, 1, :], cnt[hi, 1, :], ALU.mult)
                pool.drain()
                nc.gpsimd.tensor_tensor(pooled, pooled, hp[:, :, mid], ALU.subtract).then_inc(sem["pool_ready"], 1)
                pool.wait_ge(sem["params_free"], l + 1)
                pool.dma_start(param[:, :], A["params"][1:][bass.ds(l, 1)].rearrange("a p n -> p (a n)"))\
                    .then_inc(sem["params_in"], 16)
                with pool.Fori(0, GROUPS) as g:
                    for j in range(ADA_PER_GROUP):
                        t = (l * GROUPS + g) * ADA_PER_GROUP + j
                        pool.wait_ge(sem["ada_used"], t + 1)
                        pool.dma_start(ada[:, :, :], A["ada"][bass.ds(t, 1)].rearrange("a p (r d) -> p (a r) d", r=2))\
                            .then_inc(sem["ada_in"], 16)

            pool.wait_ge(sem["ada_used"], ADA_TILES + 1)
            pool.dma_start(cbc[:, :], A["final_norm"].rearrange("(a d) -> a d", a=1).broadcast_to([P, D])).then_inc(sem["fn_in"], 16)
            G = nc.gpsimd
            pool.wait_ge(sem["p2_in"], 16)
            pool.wait_ge(sem["mods_out"], LAYERS * GROUPS)
            G.tensor_tensor(mods[:, :], mods[:, :], p2[:, P2_B:P2_B + 6 * DK], ALU.add)
            for sc, g0 in ((SCALE_M, P2_PRE), (SCALE_F, P2_FPRE)):
                v = mods[:, sc:sc + DK]
                pool.drain()
                G.tensor_scalar(v, v, 1.0, None, ALU.add)
                pool.drain()
                G.tensor_tensor(v, v, p2[:, g0:g0 + DK], ALU.mult)
            for gt, g0 in ((GATE_M, P2_POST), (GATE_F, P2_FPOST)):
                pool.drain()
                G.tensor_tensor(mods[:, gt:gt + DK], mods[:, gt:gt + DK], p2[:, g0:g0 + DK], ALU.mult)
            pool.drain()
            for r, gt in enumerate((GATE_M, GATE_F)):
                for k in range(DK):
                    last = G.tensor_scalar(diag[:, r * DK + k, :], ident, mods[:, gt + k:gt + k + 1], None, ALU.mult)
            last.then_inc(sem["diag_done"], 1)
            pool.drain()
            pool.wait_ge(sem["x_upd"], LAYERS * X_PER_LAYER + X_LOADED)
            pool.dma_start(rel[:, :], A["rel"]).then_inc(sem["rel_in"], 16)
            pool.wait_ge(sem["xn_done"], 5)
            for i in range(TC):
                last = nc.gpsimd.tensor_scalar(x[:, i, :], xh4[:, i, :], stats[:, 8 + i:9 + i], None, ALU.mult)
            last.then_inc(sem["xf_done"], 1)
            pool.wait_ge(sem["rg_out"], TC)
            def gate_retention(h):
                c = slice(h * RET_V, (h + 1) * RET_V)
                pool.wait_ge(sem["yn"], h + 1)
                nc.gpsimd.tensor_tensor(cat[:, :, c], cat[:, :, c], rgt[:, :, c], ALU.mult).then_inc(sem["ret_out"], 1)

            pool.wait_ge(sem["abs_done"], 1)
            for h in range(DIL_HEADS):
                pool.wait_ge(sem["tab_free"], RET_HEADS + h - 1)
                slope = 2.0 ** (-8.0 * (h + 1) / DIL_HEADS)
                pool.drain()
                nc.gpsimd.tensor_scalar(tab[:, h % 2, :], delta, -slope, 0.0, ALU.mult, ALU.add)
                pool.drain()
                nc.gpsimd.tensor_tensor(tab[:, h % 2, :], tab[:, h % 2, :], lnm, ALU.add).then_inc(sem["tab_ready"], 1)
                if h == 0:
                    for g in range(RET_HEADS - 1):
                        gate_retention(g)
            gate_retention(RET_HEADS - 1)
            pool.wait_ge(sem["a2_out"], DIL_HEADS * TC)
            pool.wait_ge(sem["ct_done"], DK)
            pool.sem_inc(sem["moe_free"], 1)
            for i in range(TC):
                part = x[:, i, 0:BANK]
                pool.wait_ge(sem["t_ready"], 2 * i + 1)
                nc.gpsimd.tensor_tensor(part, part, sm[:, 0, :], ALU.add).then_inc(sem["x2_upd"], 1)
            pool.dma_start(wr[:, :, :], A["w_router"].rearrange("(k p) e -> p k e", p=P)).then_inc(sem["wr_in"], 16)
            pool.wait_ge(sem["lg_done"], 1)
            for i in range(TC):
                pool.wait_ge(sem["h_out"], i + 1)
                nc.gpsimd.tensor_tensor(h_lo[i][:, :] if i < TC - 1 else h_lo[i], asb[:, i % 2, :], h_hi[i][:, :].bitcast(F32),
                                        ALU.subtract).then_inc(sem["h_split"], 1)
            pool.wait_ge(sem["back_done"], TC)
            nc.gpsimd.memset(acc[:, :, :], 0.0).then_inc(sem["acc_zero"], 1)

            def gates(value):
                pool.wait_ge(sem["g2_ready"], value)
                nc.gpsimd.tensor_tensor(gg2[:, :, :].rearrange("p i (w c) -> p i w c", w=2),
                                        hot[:, :, 64:128].bitcast(F32).rearrange("p i (a c) -> p i a c", a=1).broadcast_to([P, TC, 2, 64]),
                                        cur[:, 1, :].rearrange("p (i a b) -> p i a b", a=1, b=1).broadcast_to([P, TC, 2, 64]), ALU.mult)\
                    .then_inc(sem["gg_ready"], 1)

            gates(1)
            with pool.Fori(0, LAST) as e:
                pool.wait_ge(sem["sgT"], e + 1)
                gates(e + 2)

        @block.tensor
        def _(pe):
            def mm3(out, stat, mov, start, stop):
                nc.tensor.matmul(out, stat[0], mov[0], start=start, stop=False)
                nc.tensor.matmul(out, stat[0], mov[1], start=False, stop=False)
                return nc.tensor.matmul(out, stat[1], mov[0], start=False, stop=stop)

            def arrived(l, g, n):
                pe.wait_ge(sem["lo_done"], tiles_before(l, g, n)[0] + 3)

            def w(n, a, b):
                return whi[n % 2][:, a:b], wlo[n % 2][:, a:b]

            def h(k, a=0, b=S):
                return hTh[:, k, a:b], hTl[:, k, a:b]

            def norm_T(nn, ready):
                pe.wait_ge(sem["xn_done"], ready)
                for k in range(DK):
                    if k >= 4:
                        pe.wait_ge(sem["hn_lo"], nn * DK + k - 3)
                    for i in range(TC):
                        last = nc.tensor.transpose(bank[4 + k % 4][:, i * P:(i + 1) * P], xn4[:, i, k * P:(k + 1) * P], ident)
                    last.then_inc(sem["tr_done"], 1)

            pe.wait_ge(sem["const_in"], 16)
            pe.sem_inc(sem["tile_used"], 2)
            with pe.Fori(0, LAYERS) as l:
                norm_T(l * 2, l * 2 + 1)
                for n in (0, 1):
                    arrived(l, 0, n)
                    for kk in range(4):
                        k = 4 * n + kk
                        pe.wait_ge(sem["hn_lo"], l * 16 + k + 1)
                        for i in range(TC):
                            last = mm3(bank[i][:, 0:SG_WIDTH], h(k, i * P, (i + 1) * P),
                                       w(n, kk * SG_WIDTH, (kk + 1) * SG_WIDTH), k == 0, k == DK - 1)
                    last.then_inc(sem["tile_used"], 1)
                for n in range(N_POOL, N_UQ):
                    c = n - N_POOL
                    arrived(l, 0, n)
                    if c >= 4:
                        pe.wait_ge(sem["proj_out"], l * 10 + c - 3)
                    for k in range(DK):
                        last = mm3(bank[4 + c % 4][:, :], w(n, k * P, (k + 1) * P), h(k), k == 0, k == DK - 1)
                    last.then_inc(sem["tile_used"], 1)
                    if n == N_KR:
                        pe.wait_ge(sem["v_out"], l * TC + TC)
                        pe.wait_ge(sem["proj_out"], l * 10 + 7)
                        for b, c0, c1 in ((0, 0, QC), (1, QC, QC + KVC)):
                            for cc in range(c0, c1):
                                last = nc.tensor.matmul(bank[b][:, :], ones, csq[:, cc, :], start=cc == c0, stop=cc == c1 - 1)
                            last.then_inc(sem["ssq_done"], 1)
                pe.wait_ge(sem["pool_ready"], l + 1)
                for c in range(2):
                    nc.tensor.matmul(bank[2 + c][:, :], wp_bd[:, c, :], pooled[:, c, :], start=True, stop=True)\
                        .then_inc(sem["pmm_done"], 1)
                pe.wait_ge(sem["vn_ready"], l + 1)
                pe.wait_ge(sem["rt_done"], l * 3 + 3)
                for c in range(2):
                    for i in range(TC):
                        for gg in range(2):
                            hd = 2 * c + gg
                            last = nc.tensor.matmul(bank[c][gg * 64:(gg + 1) * 64, i * P:(i + 1) * P],
                                                    vn[:, i, hd * SG_DIM:(hd + 1) * SG_DIM], wsT[:, hd, :],
                                                    start=True, stop=True)
                    last.then_inc(sem["sg_done"], 1)

                def rot(hd):
                    vec = qT[0:QK, hd, :] if hd < HEADS else krw[0:QK, :]
                    pe.wait_ge(sem["q_raw"], l * 8 + min(hd, HEADS - 1) + 1)
                    if hd >= 2:
                        pe.wait_ge(sem["q_rope"], l * 9 + hd - 1)
                    nc.tensor.matmul(bank[6 + hd % 2][64:96, :], const[0:QK, C_ROT:C_ROT + ROPE], vec, start=True, stop=True)\
                        .then_inc(sem["rot_done"], 1)

                pe.wait_ge(sem["proj_out"], l * 10 + 10)
                pe.wait_ge(sem["c_lo"], l * 5 + QC)
                for hd in range(HEADS):
                    n = N_UQ + hd // 2
                    if hd % 2 == 0:
                        arrived(l, 0, n)
                    if hd >= 2:
                        pe.wait_ge(sem["q_raw"], l * 8 + hd - 1)
                    for k in range(QC):
                        a = ((hd % 2) * QC + k) * QK
                        last = mm3(bank[4 + hd % 2][0:QK, :], w(n, a, a + QK), (ch[:, k, :], cl[:, k, :]), k == 0, k == QC - 1)
                    last.then_inc(sem["tile_used" if hd % 2 else "qe_done"], 1)
                    if hd:
                        rot(hd - 1)
                rot(HEADS - 1)
                rot(HEADS)
                pe.wait_ge(sem["mix_lo"], l * 8 + 4)
                pe.wait_ge(sem["c_lo"], l * 5 + QC + KVC)
                arrived(l, 0, N_UK)
                for j in range(HEADS // 2):
                    for k in range(KVC):
                        a = k * BANK + j * P
                        last = mm3(bank[j][:, :], w(N_UK, a, a + P), (ch[:, QC + k, :], cl[:, QC + k, :]), k == 0, k == KVC - 1)
                    last.then_inc(sem["k_done" if j < 3 else "tile_used"], 1)
                arrived(l, 0, N_UV)
                pe.wait_ge(sem["q_raw"], l * 8 + 8)
                pe.wait_ge(sem["q_rope"], l * 9 + 9)
                for i in range(TC):
                    for k in range(KVC):
                        last = mm3(bank[4 + i][:, :], (ch[:, QC + k, i * P:(i + 1) * P], cl[:, QC + k, i * P:(i + 1) * P]),
                                   w(N_UV, k * BANK, (k + 1) * BANK), k == 0, k == KVC - 1)
                last.then_inc(sem["tile_used"], 1)
                pe.wait_ge(sem["k_out"], l * 4 + 4)
                pe.wait_ge(sem["v2_out"], l * 4 + 4)
                N_IT = HEADS * TC
                for it in range(-1, N_IT + 1):
                    if it + 1 < N_IT:
                        e = it + 1
                        hd, i = e // TC, e % TC
                        if e >= 2:
                            pe.wait_ge(sem["p_done"], l * 32 + e - 1)
                        nc.tensor.matmul(bank[e % 2][:, :], qT[0:QK, hd, i * P:(i + 1) * P], kT[0:QK, hd, :],
                                         start=True, stop=True).then_inc(sem["s_done"], 1)
                    if 0 <= it < N_IT:
                        pe.wait_ge(sem["p_done"], l * 32 + it + 1)
                        if it >= 2:
                            pe.wait_ge(sem["pts_done"], l * 32 + it - 1)
                        for kc in range(TC):
                            last = nc.tensor.transpose(bank[2 + it % 2][:, kc * P:(kc + 1) * P],
                                                       prob[it % 2][:, kc * P:(kc + 1) * P], ident)
                        last.then_inc(sem["tr2_done"], 1)
                    if it >= 1:
                        e = it - 1
                        hd = e // TC
                        pe.wait_ge(sem["pts_done"], l * 32 + e + 1)
                        if e >= 2:
                            pe.wait_ge(sem["a_out"], l * 32 + e - 1)
                        for kc in range(TC):
                            last = nc.tensor.matmul(bank[4 + e % 2][:, 0:VDIM], probT[e % 2][:, kc * P:(kc + 1) * P],
                                                    vt[:, kc, hd * VDIM:(hd + 1) * VDIM], start=kc == 0, stop=kc == TC - 1)
                        last.then_inc(sem["av_done"], 1)
                pe.wait_ge(sem["a_out"], l * 32 + 32)

                def turn_attention(k):
                    if k >= 2:
                        pe.wait_ge(sem["mix_lo"], l * 8 + 3 + k)
                    for i in range(TC):
                        last = nc.tensor.transpose(bank[6 + k % 2][:, i * P:(i + 1) * P], att[:, i, k * P:(k + 1) * P], ident)
                    last.then_inc(sem["at_done"], 1)

                turn_attention(0)
                turn_attention(1)
                for half in range(2):
                    for q in range(4):
                        n = N_WO + 4 * half + q
                        arrived(l, 0, n)
                        if half == 0 and q >= 2:
                            pe.wait_ge(sem["mix_lo"], l * 8 + 2 + 2 * q)
                        for kk in range(2):
                            k = CAT_ORDER[2 * q + kk]
                            for i in range(TC):
                                last = mm3(bank[4 * half + i][:, :], h(k, i * P, (i + 1) * P),
                                           w(n, kk * BANK, (kk + 1) * BANK), q == 0 and kk == 0, q == 3 and kk == 1)
                        last.then_inc(sem["tile_used"], 1)
                        if n == N_WO:
                            turn_attention(2)
                            turn_attention(3)
                norm_T(l * 2 + 1, l * 2 + 2)
                with pe.Fori(0, GROUPS) as g:
                    lg = l * GROUPS + g
                    for j in range(FG):
                        for up in range(2):
                            n = N_FFN + 2 * j + up
                            arrived(l, g, n)
                            if j >= 2:
                                pe.wait_ge(sem["fr_done"], lg * FG + j - 1)
                            else:
                                pe.wait_ge(sem["x_upd"], l * X_PER_LAYER + g * (2 * TC) + X_LOADED + TC + 2 + 2 * j)
                            for k in range(DK):
                                if j == 0 and up == 0:
                                    pe.wait_ge(sem["hn_lo"], l * 16 + 9 + k)
                                last = mm3(bank[2 * (j % 2) + up][:, :], w(n, k * P, (k + 1) * P), h(k), k == 0, k == DK - 1)
                            last.then_inc(sem["tile_used"], 1)
                    for half in range(2):
                        for q in range(DOWN_TILES):
                            n = N_FFN + 2 * FG + half * DOWN_TILES + q
                            arrived(l, g, n)
                            if half == 0:
                                pe.wait_ge(sem["flo"], lg * FG + min(2 * q + 2, FG))
                            for ff in range(min(2, FG - 2 * q)):
                                f = 2 * q + ff
                                for i in range(TC):
                                    last = mm3(bank[4 - 4 * half + i][:, :], (fTh[:, f, i * P:(i + 1) * P], fTl[:, f, i * P:(i + 1) * P]),
                                               w(n, ff * BANK, (ff + 1) * BANK), f == 0, f == FG - 1)
                            last.then_inc(sem["tile_used"], 1)

            def arrived2(n):
                pe.wait_ge(sem["lo_done"], MIX2_T0 + n + 3)

            def w2(n, a, b):
                t = (MIX2_T0 + n) % 2
                return whi[t][:, a:b], wlo[t][:, a:b]

            pe.wait_ge(sem["diag_done"], 1)
            pe.wait_ge(sem["x_upd"], LAYERS * X_PER_LAYER + X_LOADED - TC)
            for r in range(2):
                for k in range(DK):
                    last = nc.tensor.matmul(bank[4 + 2 * r + k // 4][:, (k % 4) * P:(k % 4 + 1) * P], ones, diag[:, r * DK + k, :],
                                            start=True, stop=True)
                last.then_inc(sem["rows_done"], 1)
            pe.wait_ge(sem["xn_done"], 5)
            for k in range(DK):
                if k >= 4:
                    pe.wait_ge(sem["tmb"], k - 3)
                for i in range(TC):
                    last = nc.tensor.transpose(bank[k % 4][:, i * P:(i + 1) * P], xb4[:, i, k * P:(k + 1) * P], ident)
                last.then_inc(sem["tr_done"], 1)
            pe.wait_ge(sem["rows_out"], 4)
            def feature_tile(n):
                f = by_feature(n)
                arrived2(n)
                if f >= 2:
                    pe.wait_ge(sem["pj2"], f - 1)
                for k in range(DK):
                    if f == 0:
                        pe.wait_ge(sem["lob"], k + 1)
                    last = mm3(bank[4 + f % 2][:, :], w2(n, k * P, (k + 1) * P), h(k), k == 0, k == DK - 1)
                last.then_inc(sem["tile_used"], 1)

            def token_tile(n, q, b0, order=range(DK), ready=None):
                arrived2(n)
                for kk in range(2):
                    k = order[2 * q + kk]
                    if ready:
                        pe.wait_ge(sem[ready], 2 * q + kk + 1)
                    for i in range(TC):
                        last = mm3(bank[b0 + i][:, :], h(k, i * P, (i + 1) * P), w2(n, kk * BANK, (kk + 1) * BANK),
                                   q == 0 and kk == 0, q == 3 and kk == 1)
                last.then_inc(sem["tile_used"], 1)

            def retention_scores(u):
                hd, j = u // TC, u % TC
                r = slice(64 * (hd % 2), 64 * (hd % 2) + 64)
                if u == 0:
                    pe.wait_ge(sem["pj2"], 4)
                elif u >= 2:
                    pe.wait_ge(sem["dec_done"], u - 1)
                nc.tensor.matmul(bank[6 + u % 2][:, :], rqk[r, 2 + hd // 2, j * P:(j + 1) * P], rqk[r, hd // 2, :],
                                 start=True, stop=True).then_inc(sem["rs_done"], 1)

            def retention_sum(g, chunks=range(TC)):
                pe.wait_ge(sem["dec_done"], (g + 1) * TC)
                pe.wait_ge(sem["rv_out"], TC)
                if g == 2:
                    pe.wait_ge(sem["yn"], 1)
                for i in chunks:
                    for j in range(TC):
                        last = nc.tensor.matmul(bank[Y_BANK[g]][:, i * P:(i + 1) * P], decayed[g % 2][:, j, i * P:(i + 1) * P],
                                                rvt[:, j, g * RET_V:(g + 1) * RET_V], start=j == 0, stop=j == TC - 1)
                if TC - 1 in chunks:
                    last.then_inc(sem["y_done"], 1)

            for n in range(Q2["wo"]):
                if by_feature(n) is not None:
                    feature_tile(n)
                elif n < Q2["aqk"]:
                    token_tile(n, n - Q2["rv"], 0)
                elif n < Q2["av"]:
                    if n == Q2["rg"]:
                        pe.wait_ge(sem["pj2"], 12)
                    token_tile(n, n - Q2["rg"], 2)
                else:
                    if n == Q2["av"]:
                        pe.wait_ge(sem["rg_out"], TC)
                    token_tile(n, n - Q2["av"], 2)
                if n >= Q2["aqk"]:
                    retention_scores(n - Q2["aqk"])
                if n in (12, 19, 21):
                    retention_sum((12, 19, 21).index(n))
            N_IT = DIL_HEADS * TC

            def dilated_scores(c):
                hd, i = c // TC, c % TC
                r = slice(64 * (hd % 2), 64 * (hd % 2) + 64)
                if c >= 2:
                    pe.wait_ge(sem["nm2"], c - 1)
                nc.tensor.matmul(bank[c % 2][:, :], aqk[r, hd // 2, i * P:(i + 1) * P], aqk[r, 4 + hd // 2, :],
                                 start=True, stop=True).then_inc(sem["s2_done"], 1)

            retention_sum(3, range(TC // 2))
            pe.wait_ge(sem["av_out"], TC)
            pe.wait_ge(sem["yn"], 3)
            dilated_scores(0)
            dilated_scores(1)
            retention_sum(3, range(TC // 2, TC))
            for it in range(N_IT + 1):
                if 1 <= it < N_IT - 1:
                    dilated_scores(it + 1)
                if 0 <= it < N_IT:
                    pe.wait_ge(sem["p2_done"], it + 1)
                    if it >= 2:
                        pe.wait_ge(sem["pts2"], it - 1)
                    for kc in range(TC):
                        last = nc.tensor.transpose(bank[2 + it % 2][:, kc * P:(kc + 1) * P],
                                                   prob2[it % 2][:, kc * P:(kc + 1) * P], ident)
                    last.then_inc(sem["tr3"], 1)
                if it >= 1:
                    c = it - 1
                    hd = c // TC
                    pe.wait_ge(sem["pts2"], c + 1)
                    if c >= 2:
                        pe.wait_ge(sem["a2_out"], c - 1)
                    for kc in range(TC):
                        last = nc.tensor.matmul(bank[4 + c % 2][:, 0:DIL_DIM], probT2[c % 2][:, kc * P:(kc + 1) * P],
                                                avt[:, kc, hd * DIL_DIM:(hd + 1) * DIL_DIM], start=kc == 0, stop=kc == TC - 1)
                    last.then_inc(sem["av2"], 1)
            pe.wait_ge(sem["a2_out"], N_IT)
            for c, k in enumerate(CAT_ORDER):
                if c == 4:
                    pe.wait_ge(sem["ret_out"], RET_HEADS - 1)
                elif c == 7:
                    pe.wait_ge(sem["ret_out"], RET_HEADS)
                if c >= 2:
                    pe.wait_ge(sem["ml"], c - 1)
                for i in range(TC):
                    last = nc.tensor.transpose(bank[4 + c % 2][:, i * P:(i + 1) * P], cat[:, i, k * P:(k + 1) * P], ident)
                last.then_inc(sem["ct_done"], 1)
            for q in range(8):
                token_tile(Q2["wo"] + q, q % 4, 4 * (q // 4), CAT_ORDER, None if q >= 4 else "ml")
            pe.wait_ge(sem["h_done"], 1)
            pe.sem_inc(sem["moe_used"], SPLIT_RING)
            pe.wait_ge(sem["wr_in"], 16)
            for k in range(DK + 1):
                if k < DK:
                    if k >= 4:
                        pe.wait_ge(sem["hT_out"], k - 3)
                    for i in range(TC):
                        last = nc.tensor.transpose(bank[k % 4][:, i * P:(i + 1) * P], hn[i][:, k * P:(k + 1) * P], ident)
                    last.then_inc(sem["hT_done"], 1)
                if k:
                    pe.wait_ge(sem["hT_out"], k)
                    last = nc.tensor.matmul(bank[4][0:EXPERTS, :], wr[:, k - 1, :], hTf[:, k - 1, :], start=k == 1, stop=k == DK)
            last.then_inc(sem["lg_done"], 1)
            pe.wait_ge(sem["lg_out"], 1)
            for i in range(TC):
                last = nc.tensor.transpose(bank[5][:, i * EXPERTS:(i + 1) * EXPERTS], top[:, i * P:(i + 1) * P],
                                           const[0:EXPERTS, C_ID:C_ID + EXPERTS])
            last.then_inc(sem["lg_turned"], 1)

            def back(i):
                if i >= 2:
                    pe.wait_ge(sem["h_out"], i - 1)
                for k in range(DK):
                    last = nc.tensor.transpose(bank[2 * (i % 2) + k // 4][:, (k % 4) * P:(k % 4 + 1) * P],
                                               hTf[:, k, i * P:(i + 1) * P], ident)
                last.then_inc(sem["back_done"], 1)

            back(0)
            back(1)
            pe.wait_ge(sem["aff_done"], 1)
            for i in range(TC):
                last = nc.tensor.transpose(bank[7][0:EXPERTS, i * P:(i + 1) * P], aff[:, i, :], ident)
            last.then_inc(sem["affT"], 1)
            back(2)
            back(3)
            pe.wait_ge(sem["thr_d"], 1)
            nc.tensor.matmul(bank[6][:, 0:EXPERTS], const[0:EXPERTS, C_ONE:C_ONE + P], dthr, start=True, stop=True)\
                .then_inc(sem["thr_bc"], 1)
            pe.wait_ge(sem["ge_done"], 1)
            ge = rt_s[:, 1:3, :, :].rearrange("p w i e -> p (w i e)")
            nc.tensor.matmul(bank[4][:, 0:P], const[:, C_TRI:C_TRI + P], ge, start=True, stop=True)
            last = nc.tensor.matmul(bank[4][:, P:2 * P], ones, ge, start=True, stop=True)
            last.then_inc(sem["pre_done"], 1)

            def gather(value):
                pe.wait_ge(sem["g2_ready"], value)
                for i in range(TC):
                    for w, part in enumerate((h_hi[i], h_lo[i])):
                        for b in range(2):
                            last = nc.tensor.matmul(bank[2 + b][:, :], hot[:, i, 64 - 64 * w:192 - 64 * w],
                                                    part[:, b * BANK:(b + 1) * BANK], start=i == 0 and w == 0, stop=i == TC - 1 and w == 1)
                last.then_inc(sem["gat_done"], 1)

            def turn_tokens(value):
                pe.wait_ge(sem["gat_out"], value)
                for k in range(DK):
                    last = nc.tensor.transpose(bank[k // 4][:, (k % 4) * P:(k % 4 + 1) * P], gathered[:, k * P:(k + 1) * P], ident)
                last.then_inc(sem["x_turned"], 1)

            def scatter(which):
                for i, b in enumerate(SCATTER_BANKS):
                    last = nc.tensor.matmul(bank[b][:, :], sgt[:, i * P:(i + 1) * P], ysb[:, which * BANK:(which + 1) * BANK],
                                            start=True, stop=True)
                last.then_inc(sem["sc_done"], 1)

            def add_halves_T(row, b, name):
                for j in range(8):
                    last = nc.tensor.matmul(bank[b][:, j * 64:(j + 1) * 64], asb[:, row, j * P:(j + 1) * P],
                                            const[:, C_I2:C_I2 + 64], start=True, stop=True)
                last.then_inc(sem[name], 1)

            def expert_products(e):
                this, ahead = not is_round(e, OPENING), not is_round(e, LAST)
                for n in range(0 if this else NEXT0, E_TILES):
                    there, before, c = round_tile(e, n)
                    if there:
                        name, half, _ = ROUND[n // 4]
                        pe.wait_ge(sem["moe_lo"], before + 1 + RAW_RING)
                        if n == 0:
                            pe.wait_ge(sem["gate_out"], 2 * e + 1)
                        elif n == 4:
                            pe.wait_ge(sem["up_out"], 2 * e + 1)
                            if ahead:
                                pe.wait_ge(sem["gat_out"], e + 2)
                        elif n == 8:
                            pe.wait_ge(sem["hlo"], 2 * e + 1)
                            pe.wait_ge(sem["sc_add"], 2 * e + 2)
                        elif n == 12:
                            if this:
                                pe.wait_ge(sem["gate_out"], 2 * e + 2)
                            pe.wait_ge(sem["x_done"], e + 2)
                        elif n == 16 and this:
                            pe.wait_ge(sem["up_out"], 2 * e + 2)
                        elif n == 16:
                            pe.wait_ge(sem["gat_out"], 1)
                        elif n == 20:
                            pe.wait_ge(sem["hlo"], 2 * e + 2)
                        b0 = {"w_gate": 0, "w_up": 2, "w_down": 4}[name]
                        slot = c % SPLIT_RING
                        for cc in range(2):
                            k = 2 * (n % 4) + cc + (DK * half if name == "w_down" else 0)
                            first, final = k == 0, k == (2 * DK if name == "w_down" else DK) - 1
                            stat = hTe[:, k, :] if name == "w_down" else xTe[:, k, :]
                            for is_hi, part in ((True, moe_hi[slot][:, :]), (False, moe_lo[slot])):
                                for b in range(2):
                                    a = cc * D + b * BANK
                                    last = nc.tensor.matmul(bank[b0 + b][:, :], stat, part[:, a:a + BANK],
                                                            start=first and is_hi, stop=final and not is_hi)
                        last.then_inc(sem["moe_used"], 1)
                    if n == 0 and ahead:
                        pe.wait_ge(sem["up_out"], 2 * e + 1)
                        gather(e + 2)
                    elif n == 3:
                        pe.wait_ge(sem["y_out"], e + 1)
                        pe.wait_ge(sem["sg_ready"], e + 1)
                        pe.wait_ge(sem["silu_m"], 2 * e + 1)
                        pe.wait_ge(sem["hf_m"], 2 * e + 1)
                        scatter(0)
                    elif n == 6:
                        pe.wait_ge(sem["sc_add"], 2 * e + 1)
                        scatter(1)
                    elif n == 8 and ahead:
                        pe.wait_ge(sem["gate_out"], 2 * e + 2)
                        turn_tokens(e + 2)
                    elif n == 10:
                        add_halves_T(0, 6, "gate_t")
                    elif n == 11:
                        pe.wait_ge(sem["up_out"], 2 * e + 2)
                        add_halves_T(1, 7, "up_t")
                    elif n == 15 and this:
                        pe.wait_ge(sem["hf_m"], 2 * e + 2)
                        pe.wait_ge(sem["gg_ready"], e + 1)
                        for i in range(TC):
                            last = nc.tensor.transpose(bank[7][:, i * P:(i + 1) * P], gg2[:, i, :], ident)
                        last.then_inc(sem["sgT"], 1)
                    elif n == 19 and ahead:
                        pe.wait_ge(sem["gate_out"], 2 * e + 3)
                        if this:
                            pe.wait_ge(sem["silu_m"], 2 * e + 2)
                        add_halves_T(0, 6, "gate_t")
                    elif n == 23 and ahead:
                        pe.wait_ge(sem["up_out"], 2 * e + 3)
                        pe.wait_ge(sem["sg_ready"], e + 2)
                        add_halves_T(1, 7, "up_t")

            pe.wait_ge(sem["h_split"], TC)
            gather(1)
            turn_tokens(1)
            pe.wait_ge(sem["acc_zero"], 1)
            rounds(pe, expert_products)
            pe.wait_ge(sem["y_out"], EXPERTS + 1)
            pe.wait_ge(sem["sg_ready"], EXPERTS + 1)
            for which in range(2):
                pe.wait_ge(sem["sc_add"], EXPERTS * 2 + which)
                scatter(which)


def _chunks(w, cols):
    import numpy as np
    k = w.shape[0] // P
    return np.ascontiguousarray(w.reshape(k, P, cols).transpose(1, 0, 2).reshape(P, k * cols))


def _tiles(a):
    import numpy as np
    out = np.zeros((N_TILES, P, TILE), np.float32)
    o1, o2 = Q_LORA, Q_LORA + KV_LORA
    o3 = o2 + ROPE
    o4 = o3 + 256
    o5 = o4 + SG_WIDTH
    for l in range(LAYERS):
        w_in, w_o, w_uq, w_ukv = a["w_in"][l], a["w_o"][l], a["w_uq"][l], a["w_ukv"][l]
        t0 = l * LAYER_TILES

        def put(n, block):
            out[t0 + n, :, 0:block.shape[1]] = block

        for q in range(2):
            put(N_V + q, _chunks(w_in[q * 512:(q + 1) * 512, o5:], SG_WIDTH))
            put(N_POOL + q, _chunks(w_in[:, o3 + q * P:o3 + (q + 1) * P], P))
            put(N_U + q, _chunks(w_in[:, o4 + q * P:o4 + (q + 1) * P], P))
            put(N_KV + q, _chunks(w_in[:, o1 + q * P:o1 + (q + 1) * P], P))
        for q in range(QC):
            put(N_Q + q, _chunks(w_in[:, q * P:(q + 1) * P], P))
        put(N_KR, _chunks(w_in[:, o2 - 64:o2 + 64], P))
        for m in range(HEADS // 2):
            put(N_UQ + m, np.concatenate([_chunks(w_uq[:, hd * QK:(hd + 1) * QK], QK) for hd in (2 * m, 2 * m + 1)], axis=1))
        kv = w_ukv.reshape(KV_LORA, HEADS, NOPE + VDIM)
        put(N_UK, _chunks(kv[:, :, :NOPE].reshape(KV_LORA, -1), BANK))
        put(N_UV, _chunks(kv[:, :, NOPE:].reshape(KV_LORA, -1), BANK))
        for half in range(2):
            cols = slice(half * BANK, (half + 1) * BANK)
            for q in range(4):
                k = CAT_ORDER[2 * q]
                put(N_WO + 4 * half + q, _chunks(w_o[k * P:(k + 2) * P, cols], BANK))
        for g in range(GROUPS):
            g0 = N_FFN + g * GROUP_TILES
            for j in range(FG):
                f = g * FG + j
                put(g0 + 2 * j, _chunks(a["w_gate"][l][:, f * P:(f + 1) * P], P))
                put(g0 + 2 * j + 1, _chunks(a["w_up"][l][:, f * P:(f + 1) * P], P))
            for half in range(2):
                for q in range(DOWN_TILES):
                    r0 = (g * FG + 2 * q) * P
                    r1 = min(r0 + 2 * P, (g + 1) * FG * P)
                    put(g0 + 2 * FG + half * DOWN_TILES + q,
                        _chunks(a["w_down"][l][r0:r1, half * BANK:(half + 1) * BANK], BANK))
    w = a["w_in_2"][0]
    for n in range(12):
        c0 = n * P if n < 4 else 1536 + (n - 4) * P
        out[MIX2_T0 + (Q2["rqk"] + n if n < 4 else Q2["aqk"] + n - 4)] = _chunks(w[:, c0:c0 + P], P)
    for name, c0 in (("rv", 512), ("rg", 1024), ("av", 2560)):
        for q in range(4):
            out[MIX2_T0 + Q2[name] + q] = _chunks(w[q * 256:(q + 1) * 256, c0:c0 + BANK], BANK)
    for half in range(2):
        for q in range(4):
            k = CAT_ORDER[2 * q]
            out[MIX2_T0 + Q2["wo"] + 4 * half + q] = _chunks(a["w_out_2"][0][k * P:(k + 2) * P, half * BANK:(half + 1) * BANK], BANK)
    return out


def _params(a):
    import numpy as np
    out = np.zeros((LAYERS + 1, P, N_PARAM), np.float32)
    for l in range(LAYERS):
        p = out[l]
        for off, v in ((G_MIX, a["mix_norm"][l]), (G_FFN, a["ffn_norm"][l]), (G_Q, a["q_norm"][l]), (G_KV, a["kv_norm"][l]),
                       (G_PS, a["pool_scale"][l])):
            p[:, off:off + v.size // P] = v.reshape(-1, P).T
        for c in range(2):
            p[:, PR_BS + c * P:PR_BS + (c + 1) * P] = np.repeat(a["b_s"][l][2 * c:2 * c + 2], 64, axis=0)
            for q in range(2):
                p[q * 64:(q + 1) * 64, PR_WP + c * P + q * 64:PR_WP + c * P + (q + 1) * 64] = a["w_pool"][l][2 * c + q]
        p[:, PR_SG:PR_WS] = a["sg_norm"][l][None, :]
        p[:, PR_WS:PR_WP] = a["w_s"][l].transpose(2, 0, 1).reshape(P, -1)
    return out


def _const():
    import numpy as np
    c = np.zeros((P, N_CONST), np.float32)
    c[:, C_ID:C_ID + P] = np.eye(P)
    c[:, C_ONE:C_ONE + P] = 1.0
    half = ROPE // 2
    for j in range(half):
        c[64 + half + j, C_ROT + j] = -1.0
        c[64 + j, C_ROT + half + j] = 1.0
    freq = (np.float32(10000.0) ** (-np.arange(0, ROPE, 2, dtype=np.float32) / np.float32(ROPE))).astype(np.float32)
    c[64:96, C_FREQ] = np.concatenate([freq, freq])
    c[:, C_TRI:C_TRI + P] = np.triu(np.ones((P, P)), 1)
    c[:, C_IOTA:C_IOTA + P] = (np.arange(P) % 64)[None, :]
    c[:, C_I2:C_I2 + 64] = (np.arange(P)[:, None] % 64) == np.arange(64)[None, :]
    c[:, C_EPS] = EPS
    c[:, C_GEPS] = GN_EPS
    return c


def _counts():
    import numpy as np
    c = np.zeros((P, 2, S), np.float32)
    t = np.arange(S)
    for g, wdw in enumerate(POOL_WINDOWS):
        left = wdw // 2
        n = np.clip(t + wdw - left, 0, S) - np.clip(t - left, 0, S)
        c[(g % 2) * 64:(g % 2) * 64 + 64, g // 2] = (1.0 / n.astype(np.float32))[None, :]
    return c


def _ada(w_ada):
    import numpy as np
    return np.ascontiguousarray(w_ada.T.reshape(ADA_TILES, 2, P, D).transpose(0, 2, 1, 3).reshape(ADA_TILES, P, 2 * D))


def _params2(a):
    import numpy as np
    out = np.zeros((P, N_P2), np.float32)
    for off, name in ((P2_PRE, "g_pre_mix_2"), (P2_POST, "g_post_mix_2"), (P2_FPRE, "g_pre_ffn_2"), (P2_FPOST, "g_post_ffn_2"),
                      (P2_B, "b_ada_2")):
        v = a[name][0]
        out[:, off:off + v.size // P] = v.reshape(-1, P).T
    out[:, P2_LOGIT:P2_LOGIT + RET_HEADS] = a["ret_decay_fwd_2"][0][None, :]
    out[:, P2_LOGIT + RET_HEADS:] = a["ret_decay_bwd_2"][0][None, :]
    return out


def _rel():
    import numpy as np
    d = np.arange(REL)[None, :] - REL0 - np.arange(P)[:, None]
    many = sum(((d % dil == 0) & (abs(d) <= win // 2)).astype(np.float64) for win, dil in DIL_CONFIGS)
    lnm = np.where(many > 0, np.log(np.maximum(many, 1.0)), MASKED)
    return np.concatenate([d, lnm], axis=1).astype(np.float32)


def arrays_of(inputs):
    import numpy as np
    a = {k: np.asarray(v) for k, v in inputs.items()}
    return {
        "x": a["x"], "positions": a["positions"], "c": a["c_2"], "const": _const(), "counts": _counts(), "tiles": _tiles(a), "params": _params(a),
        "ada": _ada(a["w_ada_2"][0]), "params2": _params2(a), "rel": _rel(), "final_norm": a["final_norm"],
        "w_router": a["w_router_2"][0], "w_gate": a["w_gate_e_2"][0], "w_up": a["w_up_e_2"][0], "w_down": a["w_down_e_2"][0],
    }


def kernel(**inputs):
    import concourse.bacc as _bacc
    from concourse.bass_utils import run_bass_kernel_spmd as _run

    nc = _bacc.Bacc("TRN2", target_bir_lowering=False, num_devices=1)
    arrays = arrays_of(inputs)
    A = {k: nc.dram_tensor(f"in_{k}", v.shape, mybir.dt.from_np(v.dtype), kind="ExternalInput").ap() for k, v in arrays.items()}
    A["out"] = nc.dram_tensor("out_x", (1, S, D), F32, kind="ExternalOutput").ap()
    build(nc, A)
    r = _run(nc, [{f"in_{k}": v for k, v in arrays.items()}], core_ids=[0])
    return r.results[0]["out_x"]
```
